# Optimizing a Trainium2 kernel written in Bass

```python
import math
import jax
import jax.numpy as jnp
from jax import lax
import numpy as np

D_MODEL = 1024
BATCH = 1
SEQ = 1024
DEPTH = 1
DEC_BATCH = 1
DEC_SEQ = 64
PAST_LEN = 2048

CHUNK = 64
EPS = 1e-6
F32 = jnp.float32

MIX_WIDTH = D_MODEL
MIX_A = MIX_WIDTH // 4
MIX_B = MIX_WIDTH // 4
MIX_C = MIX_WIDTH // 4
MIX_D = MIX_WIDTH - MIX_A - MIX_B - MIX_C

SSD_HEAD_DIM = 64
SSD_HEADS = MIX_A // SSD_HEAD_DIM
SSD_GROUPS = 2
SSD_STATE = 64
SSD_CONV = 4
SSD_CONV_CH = MIX_A + 2 * SSD_GROUPS * SSD_STATE
SSD_IN = MIX_A + SSD_CONV_CH + SSD_HEADS

CCM_WIDTH = 31
CCM_IN = 2 * MIX_B

ATT_HEAD_DIM = 64
ATT_HEADS = MIX_C // ATT_HEAD_DIM
ATT_PREV_CHUNKS = 8
ATT_WINDOW = ATT_PREV_CHUNKS * CHUNK
ATT_BAND = ATT_WINDOW + CHUNK
ATT_IN = 3 * MIX_C
ATT_SCALE = ATT_HEAD_DIM ** -0.5
REL_MAX = 128

S5_GROUP_CH = 16
S5_GROUPS = MIX_D // S5_GROUP_CH
S5_STATE = 64

IN_WIDTH = SSD_IN + CCM_IN + ATT_IN + MIX_D

MOE_GROUPS = 4
MOE_EXPERTS_PER_GROUP = 8
MOE_EXPERTS = MOE_GROUPS * MOE_EXPERTS_PER_GROUP
MOE_TOP_K = 2
MOE_D_FF = D_MODEL // 2
MOE_BLOCK = 128

kernel_name = 'hybrid_streaming_encoder_step'

def _rmsnorm(x, g):
    xf = x.astype(F32)
    y = xf * lax.rsqrt(jnp.mean(xf * xf, axis=-1, keepdims=True) + EPS)
    return (y * g.astype(F32)).astype(x.dtype)

def _layernorm(x, g, b):
    xf = x.astype(F32)
    mu = jnp.mean(xf, axis=-1, keepdims=True)
    var = jnp.mean(jnp.square(xf - mu), axis=-1, keepdims=True)
    return ((xf - mu) * lax.rsqrt(var + EPS) * g.astype(F32) + b.astype(F32)).astype(x.dtype)

def _causal_dwconv(hist, x, w, b):
    xp = jnp.concatenate([hist.astype(x.dtype), x], axis=1)
    y = lax.conv_general_dilated(xp, w.astype(x.dtype)[:, None, :], (1,), 'VALID',
                                 dimension_numbers=('NWC', 'WIO', 'NWC'),
                                 feature_group_count=x.shape[-1])
    return y + b.astype(x.dtype), xp[:, xp.shape[1] - (w.shape[0] - 1):]

def _segsum(a):
    t = a.shape[-1]
    ar = jnp.broadcast_to(a[..., None], a.shape + (t,))
    ar = jnp.where(jnp.tril(jnp.ones((t, t), bool), -1), ar, 0.0)
    s = jnp.cumsum(ar, axis=-2)
    return jnp.where(jnp.tril(jnp.ones((t, t), bool)), s, -jnp.inf)

def _ssd_scan(x, a, bm, cm, h0):
    b, l, h, p = x.shape
    n = bm.shape[-1]
    cl = min(CHUNK, l)
    nc = l // cl
    x = x.reshape(b, nc, cl, h, p)
    bm = bm.reshape(b, nc, cl, h, n)
    cm = cm.reshape(b, nc, cl, h, n)
    a = a.reshape(b, nc, cl, h).transpose(0, 3, 1, 2)
    a_cs = jnp.cumsum(a, axis=-1)
    decay_in = jnp.exp(_segsum(a))
    cb = jnp.einsum('bclhn,bcshn->bhcls', cm, bm)
    y_diag = jnp.einsum('bhcls,bcshp->bclhp', cb * decay_in, x)
    decay_states = jnp.exp(a_cs[..., -1:] - a_cs)
    states = jnp.einsum('bclhn,bhcl,bclhp->bchpn', bm, decay_states, x)
    states = jnp.concatenate([h0[:, None], states], axis=1)
    decay_chunk = jnp.exp(_segsum(jnp.pad(a_cs[..., -1], ((0, 0), (0, 0), (1, 0)))))
    new_states = jnp.einsum('bhzc,bchpn->bzhpn', decay_chunk, states)
    y_off = jnp.einsum('bclhn,bchpn,bhcl->bclhp', cm, new_states[:, :-1], jnp.exp(a_cs))
    return (y_diag + y_off).reshape(b, l, h, p), new_states[:, -1]

def _ssd_mixer(u, conv_hist, h0, p):
    b, l, _ = u.shape
    z, xbc, dt = jnp.split(u, [MIX_A, MIX_A + SSD_CONV_CH], axis=-1)
    xbc, conv_state = _causal_dwconv(conv_hist, xbc, p['ssd_conv_w'], p['ssd_conv_b'])
    xbc = jax.nn.silu(xbc.astype(F32))
    xs, bm, cm = jnp.split(xbc, [MIX_A, MIX_A + SSD_GROUPS * SSD_STATE], axis=-1)
    xs = xs.reshape(b, l, SSD_HEADS, SSD_HEAD_DIM)
    rep = SSD_HEADS // SSD_GROUPS
    bm = jnp.repeat(bm.reshape(b, l, SSD_GROUPS, SSD_STATE), rep, axis=2)
    cm = jnp.repeat(cm.reshape(b, l, SSD_GROUPS, SSD_STATE), rep, axis=2)
    dt = jax.nn.softplus(dt.astype(F32) + p['ssd_dt_bias'].astype(F32))
    a = -jnp.exp(p['ssd_a_log'].astype(F32))
    y, h_last = _ssd_scan(xs * dt[..., None], dt * a, bm, cm, h0.astype(F32))
    y = y + p['ssd_d'].astype(F32)[:, None] * xs
    y = y.reshape(b, l, MIX_A) * jax.nn.silu(z.astype(F32))
    yg = y.reshape(b, l, SSD_GROUPS, MIX_A // SSD_GROUPS)
    yg = yg * lax.rsqrt(jnp.mean(yg * yg, axis=-1, keepdims=True) + EPS)
    y = yg.reshape(b, l, MIX_A) * p['ssd_norm_w'].astype(F32)
    return y.astype(u.dtype), conv_state, h_last

def _conv_module(u, hist, p):
    a, g = jnp.split(u, 2, axis=-1)
    v = a * jax.nn.sigmoid(g)
    v, new_hist = _causal_dwconv(hist, v, p['ccm_dw_w'], p['ccm_dw_b'])
    v = jax.nn.silu(_layernorm(v, p['ccm_ln_g'], p['ccm_ln_b']))
    return v @ p['ccm_pw_w'] + p['ccm_pw_b'], new_hist

def _rel_bias(table, n_q, n_k, offset):
    d = offset + jnp.arange(n_q)[:, None] - jnp.arange(n_k)[None, :]
    idx = jnp.clip(d, -REL_MAX, REL_MAX) + REL_MAX
    return table.astype(F32)[:, idx]

def _split_qkv(u):
    b, l, _ = u.shape
    q, k, v = jnp.split(u, 3, axis=-1)
    shp = (b, l, ATT_HEADS, ATT_HEAD_DIM)
    return q.reshape(shp), k.reshape(shp), v.reshape(shp)

def _band_attention_prompt(u, table):
    q, k, v = _split_qkv(u)
    b, l = q.shape[:2]
    nc = l // CHUNK
    pad = jnp.zeros((b, ATT_WINDOW, ATT_HEADS, ATT_HEAD_DIM), k.dtype)

    def band(t):
        tp = jnp.concatenate([pad, t], axis=1).reshape(b, nc + ATT_PREV_CHUNKS, CHUNK, ATT_HEADS, ATT_HEAD_DIM)
        return jnp.concatenate([tp[:, j:j + nc] for j in range(ATT_PREV_CHUNKS + 1)], axis=2)

    kb, vb = band(k), band(v)
    qc = q.reshape(b, nc, CHUNK, ATT_HEADS, ATT_HEAD_DIM)
    s = jnp.einsum('bcqhd,bckhd->bchqk', qc, kb, preferred_element_type=F32) * ATT_SCALE
    s = s + _rel_bias(table, CHUNK, ATT_BAND, ATT_WINDOW)
    key_chunk = jnp.arange(nc)[:, None] - ATT_PREV_CHUNKS + jnp.arange(ATT_BAND)[None, :] // CHUNK
    s = jnp.where((key_chunk >= 0)[None, :, None, None, :], s, -jnp.inf)
    pr = jax.nn.softmax(s, axis=-1).astype(v.dtype)
    o = jnp.einsum('bchqk,bckhd->bcqhd', pr, vb).reshape(b, l, MIX_C)
    keep = min(ATT_WINDOW, l)
    return o, k[:, l - keep:], v[:, l - keep:]

def _band_attention_sample(u, k_cache, v_cache, table):
    q, k, v = _split_qkv(u)
    b, l = q.shape[:2]
    kk = jnp.concatenate([k_cache.astype(k.dtype), k], axis=1)
    vv = jnp.concatenate([v_cache.astype(v.dtype), v], axis=1)
    s = jnp.einsum('bqhd,bkhd->bhqk', q, kk, preferred_element_type=F32) * ATT_SCALE
    s = s + _rel_bias(table, l, kk.shape[1], k_cache.shape[1])
    pr = jax.nn.softmax(s, axis=-1).astype(v.dtype)
    o = jnp.einsum('bhqk,bkhd->bqhd', pr, vv).reshape(b, l, MIX_C)
    return o, k, v

def _complex_affine_combine(e1, e2):
    a1r, a1i, b1r, b1i = e1
    a2r, a2i, b2r, b2i = e2
    return (a2r * a1r - a2i * a1i, a2r * a1i + a2i * a1r,
            a2r * b1r - a2i * b1i + b2r, a2r * b1i + a2i * b1r + b2i)

def _s5_mixer(u, h0_re, h0_im, p):
    b, l, _ = u.shape
    uf = u.astype(F32).reshape(b, l, S5_GROUPS, S5_GROUP_CH)
    lr = p['s5_lam_re'].astype(F32)
    li = p['s5_lam_im'].astype(F32)
    dt = jnp.exp(p['s5_log_dt'].astype(F32))[:, None]
    mag = jnp.exp(lr * dt)
    ar, ai = mag * jnp.cos(li * dt), mag * jnp.sin(li * dt)
    den = lr * lr + li * li
    cr = ((ar - 1.0) * lr + ai * li) / den
    ci = (ai * lr - (ar - 1.0) * li) / den
    br, bi = p['s5_b_re'].astype(F32), p['s5_b_im'].astype(F32)
    bbr = cr[..., None] * br - ci[..., None] * bi
    bbi = cr[..., None] * bi + ci[..., None] * br
    xr = jnp.einsum('blgc,gnc->blgn', uf, bbr)
    xi = jnp.einsum('blgc,gnc->blgn', uf, bbi)
    h0r, h0i = h0_re.astype(F32), h0_im.astype(F32)
    xr = xr.at[:, 0].add(ar * h0r - ai * h0i)
    xi = xi.at[:, 0].add(ar * h0i + ai * h0r)
    a_r = jnp.broadcast_to(ar, xr.shape)
    a_i = jnp.broadcast_to(ai, xi.shape)
    _, _, hr, hi = lax.associative_scan(_complex_affine_combine, (a_r, a_i, xr, xi), axis=1)
    y = (jnp.einsum('blgn,gcn->blgc', hr, p['s5_c_re'].astype(F32))
         - jnp.einsum('blgn,gcn->blgc', hi, p['s5_c_im'].astype(F32))
         + p['s5_d'].astype(F32) * uf)
    g = jax.nn.gelu(y.reshape(b, l, MIX_D))
    ga, gb = jnp.split(g @ p['s5_glu_w'].astype(F32) + p['s5_glu_b'].astype(F32), 2, axis=-1)
    return (ga * jax.nn.sigmoid(gb)).astype(u.dtype), hr[:, -1], hi[:, -1]

def _hier_moe(h, p):
    t, d = h.shape
    lg = jnp.einsum('td,dg->tg', h, p['moe_w_group'], preferred_element_type=F32)
    grp = jnp.argmax(lg, axis=-1)
    tok = jnp.arange(t)
    p_grp = jax.nn.softmax(lg, axis=-1)[tok, grp]
    le = jnp.einsum('td,gde->tge', h, p['moe_w_expert'], preferred_element_type=F32)[tok, grp]
    top_l, top_i = lax.top_k(le, MOE_TOP_K)
    gate = jax.nn.softmax(top_l, axis=-1) * p_grp[:, None]
    e_flat = (grp[:, None] * MOE_EXPERTS_PER_GROUP + top_i).reshape(-1).astype(jnp.int32)
    n_assign = t * MOE_TOP_K
    order = jnp.argsort(e_flat)
    e_sorted = e_flat[order]
    counts = jnp.zeros((MOE_EXPERTS,), jnp.int32).at[e_flat].add(1)
    padded = (counts + MOE_BLOCK - 1) // MOE_BLOCK * MOE_BLOCK
    pad_end = jnp.cumsum(padded)
    pad_start = pad_end - padded
    start = jnp.cumsum(counts) - counts
    dest = pad_start[e_sorted] + jnp.arange(n_assign, dtype=jnp.int32) - start[e_sorted]
    n_blocks = -(-n_assign // MOE_BLOCK) + MOE_EXPERTS
    n_rows = n_blocks * MOE_BLOCK
    row_tok = jnp.full((n_rows,), t, jnp.int32).at[dest].set((order // MOE_TOP_K).astype(jnp.int32))
    row_w = jnp.zeros((n_rows,), F32).at[dest].set(gate.reshape(-1)[order])
    blk_expert = jnp.minimum(jnp.searchsorted(pad_end, jnp.arange(n_blocks, dtype=jnp.int32) * MOE_BLOCK,
                                              side='right'), MOE_EXPERTS - 1)
    hp = jnp.concatenate([h, jnp.zeros((1, d), h.dtype)], axis=0)

    def expert_block(args):
        rows, e = args
        xb = hp[rows]
        a = xb @ p['moe_w_gate'][e]
        v = xb @ p['moe_w_up'][e]
        return (jax.nn.silu(a) * v) @ p['moe_w_down'][e]

    out = lax.map(expert_block, (row_tok.reshape(n_blocks, MOE_BLOCK), blk_expert))
    out = out.reshape(n_rows, d)
    y = jnp.zeros((t + 1, d), out.dtype).at[row_tok].add(out * row_w[:, None].astype(out.dtype))
    return y[:t].astype(h.dtype)

def _layer(x, p, st, is_prompt):
    b, l, _ = x.shape
    xn = _rmsnorm(x, p['g_mix'])
    proj = xn @ p['w_in']
    u_a, u_b, u_c, u_d = jnp.split(proj, [SSD_IN, SSD_IN + CCM_IN, SSD_IN + CCM_IN + ATT_IN], axis=-1)
    if is_prompt:
        y_c, k_new, v_new = _band_attention_prompt(u_c, p['att_rel_bias'])
    else:
        y_c, k_new, v_new = _band_attention_sample(u_c, st['att_k'], st['att_v'], p['att_rel_bias'])
    y_a, ssd_conv, ssd = _ssd_mixer(u_a, st['ssd_conv'], st['ssd'], p)
    y_b, ccm_conv = _conv_module(u_b, st['ccm_conv'], p)
    y_d, s5_re, s5_im = _s5_mixer(u_d, st['s5_re'], st['s5_im'], p)
    mixed = jnp.concatenate([y_a.astype(x.dtype), y_b.astype(x.dtype), y_c.astype(x.dtype),
                             y_d.astype(x.dtype)], axis=-1) @ p['w_out']
    h = x + mixed.astype(x.dtype)
    hn = _rmsnorm(h, p['g_ffn']).reshape(b * l, D_MODEL)
    h = h + _hier_moe(hn, p).reshape(b, l, D_MODEL)
    new = {'ssd': ssd, 'ssd_conv': ssd_conv, 'ccm_conv': ccm_conv, 'att_k': k_new, 'att_v': v_new,
           's5_re': s5_re, 's5_im': s5_im}
    return h, new

def setup_inputs(seed: int = 0) -> dict:
    key = jax.random.key(seed)
    ks = iter(jax.random.split(key, 64))

    def nrm(shape, scale):
        return jax.random.normal(next(ks), shape, F32) * scale

    def uni(shape, lo, hi):
        return jax.random.uniform(next(ks), shape, F32, lo, hi)

    c_win = min(ATT_WINDOW, PAST_LEN)
    dt0 = jnp.exp(uni((DEPTH, SSD_HEADS), math.log(1e-3), math.log(1e-1)))
    return {
        'x_prompt': nrm((BATCH, SEQ, D_MODEL), 1.0),
        'x_sample': nrm((DEC_BATCH, DEC_SEQ, D_MODEL), 1.0),
        'state_ssd': nrm((DEPTH, DEC_BATCH, SSD_HEADS, SSD_HEAD_DIM, SSD_STATE), 0.5),
        'state_ssd_conv': nrm((DEPTH, DEC_BATCH, SSD_CONV - 1, SSD_CONV_CH), 1.0),
        'state_ccm_conv': nrm((DEPTH, DEC_BATCH, CCM_WIDTH - 1, MIX_B), 0.5),
        'cache_att_k': nrm((DEPTH, DEC_BATCH, c_win, ATT_HEADS, ATT_HEAD_DIM), 1.0),
        'cache_att_v': nrm((DEPTH, DEC_BATCH, c_win, ATT_HEADS, ATT_HEAD_DIM), 1.0),
        'state_s5_re': nrm((DEPTH, DEC_BATCH, S5_GROUPS, S5_STATE), 0.5),
        'state_s5_im': nrm((DEPTH, DEC_BATCH, S5_GROUPS, S5_STATE), 0.5),
        'g_mix': 1.0 + nrm((DEPTH, D_MODEL), 0.02),
        'w_in': nrm((DEPTH, D_MODEL, IN_WIDTH), D_MODEL ** -0.5),
        'ssd_conv_w': nrm((DEPTH, SSD_CONV, SSD_CONV_CH), SSD_CONV ** -0.5),
        'ssd_conv_b': nrm((DEPTH, SSD_CONV_CH), 0.02),
        'ssd_dt_bias': dt0 + jnp.log(-jnp.expm1(-dt0)),
        'ssd_a_log': jnp.log(uni((DEPTH, SSD_HEADS), 1.0, 16.0)),
        'ssd_d': 1.0 + nrm((DEPTH, SSD_HEADS), 0.1),
        'ssd_norm_w': 1.0 + nrm((DEPTH, MIX_A), 0.02),
        'ccm_dw_w': nrm((DEPTH, CCM_WIDTH, MIX_B), CCM_WIDTH ** -0.5),
        'ccm_dw_b': nrm((DEPTH, MIX_B), 0.02),
        'ccm_ln_g': 1.0 + nrm((DEPTH, MIX_B), 0.02),
        'ccm_ln_b': nrm((DEPTH, MIX_B), 0.02),
        'ccm_pw_w': nrm((DEPTH, MIX_B, MIX_B), MIX_B ** -0.5),
        'ccm_pw_b': nrm((DEPTH, MIX_B), 0.02),
        'att_rel_bias': nrm((DEPTH, ATT_HEADS, 2 * REL_MAX + 1), 0.1),
        's5_lam_re': -0.5 + nrm((DEPTH, S5_GROUPS, S5_STATE), 0.01),
        's5_lam_im': math.pi * jnp.arange(S5_STATE, dtype=F32) + nrm((DEPTH, S5_GROUPS, S5_STATE), 0.01),
        's5_log_dt': uni((DEPTH, S5_GROUPS), math.log(1e-3), math.log(1e-1)),
        's5_b_re': nrm((DEPTH, S5_GROUPS, S5_STATE, S5_GROUP_CH), (2 * S5_GROUP_CH) ** -0.5),
        's5_b_im': nrm((DEPTH, S5_GROUPS, S5_STATE, S5_GROUP_CH), (2 * S5_GROUP_CH) ** -0.5),
        's5_c_re': nrm((DEPTH, S5_GROUPS, S5_GROUP_CH, S5_STATE), (2 * S5_STATE) ** -0.5),
        's5_c_im': nrm((DEPTH, S5_GROUPS, S5_GROUP_CH, S5_STATE), (2 * S5_STATE) ** -0.5),
        's5_d': nrm((DEPTH, S5_GROUPS, S5_GROUP_CH), 0.5),
        's5_glu_w': nrm((DEPTH, MIX_D, 2 * MIX_D), MIX_D ** -0.5),
        's5_glu_b': nrm((DEPTH, 2 * MIX_D), 0.02),
        'w_out': nrm((DEPTH, MIX_WIDTH, D_MODEL), MIX_WIDTH ** -0.5),
        'g_ffn': 1.0 + nrm((DEPTH, D_MODEL), 0.02),
        'moe_w_group': nrm((DEPTH, D_MODEL, MOE_GROUPS), D_MODEL ** -0.5),
        'moe_w_expert': nrm((DEPTH, MOE_GROUPS, D_MODEL, MOE_EXPERTS_PER_GROUP), D_MODEL ** -0.5),
        'moe_w_gate': nrm((DEPTH, MOE_EXPERTS, D_MODEL, MOE_D_FF), D_MODEL ** -0.5),
        'moe_w_up': nrm((DEPTH, MOE_EXPERTS, D_MODEL, MOE_D_FF), D_MODEL ** -0.5),
        'moe_w_down': nrm((DEPTH, MOE_EXPERTS, MOE_D_FF, D_MODEL), MOE_D_FF ** -0.5),
        'g_final': 1.0 + nrm((D_MODEL,), 0.02),
    }

def reference(x_prompt, x_sample, state_ssd, state_ssd_conv, state_ccm_conv, cache_att_k, cache_att_v,
              state_s5_re, state_s5_im, g_mix, w_in, ssd_conv_w, ssd_conv_b, ssd_dt_bias, ssd_a_log, ssd_d,
              ssd_norm_w, ccm_dw_w, ccm_dw_b, ccm_ln_g, ccm_ln_b, ccm_pw_w, ccm_pw_b, att_rel_bias,
              s5_lam_re, s5_lam_im, s5_log_dt, s5_b_re, s5_b_im, s5_c_re, s5_c_im, s5_d, s5_glu_w, s5_glu_b,
              w_out, g_ffn, moe_w_group, moe_w_expert, moe_w_gate, moe_w_up, moe_w_down, g_final):
    names = ('ssd', 'ssd_conv', 'ccm_conv', 'att_k', 'att_v', 's5_re', 's5_im')
    new_p = {n: [] for n in names}
    new_s = {n: [] for n in names}
    bp = x_prompt.shape[0]
    yp, ys = x_prompt, x_sample
    for i in range(DEPTH):
        p = {'g_mix': g_mix[i], 'w_in': w_in[i], 'ssd_conv_w': ssd_conv_w[i], 'ssd_conv_b': ssd_conv_b[i],
             'ssd_dt_bias': ssd_dt_bias[i], 'ssd_a_log': ssd_a_log[i], 'ssd_d': ssd_d[i],
             'ssd_norm_w': ssd_norm_w[i], 'ccm_dw_w': ccm_dw_w[i], 'ccm_dw_b': ccm_dw_b[i],
             'ccm_ln_g': ccm_ln_g[i], 'ccm_ln_b': ccm_ln_b[i], 'ccm_pw_w': ccm_pw_w[i], 'ccm_pw_b': ccm_pw_b[i],
             'att_rel_bias': att_rel_bias[i], 's5_lam_re': s5_lam_re[i], 's5_lam_im': s5_lam_im[i],
             's5_log_dt': s5_log_dt[i], 's5_b_re': s5_b_re[i], 's5_b_im': s5_b_im[i], 's5_c_re': s5_c_re[i],
             's5_c_im': s5_c_im[i], 's5_d': s5_d[i], 's5_glu_w': s5_glu_w[i], 's5_glu_b': s5_glu_b[i],
             'w_out': w_out[i], 'g_ffn': g_ffn[i], 'moe_w_group': moe_w_group[i],
             'moe_w_expert': moe_w_expert[i], 'moe_w_gate': moe_w_gate[i], 'moe_w_up': moe_w_up[i],
             'moe_w_down': moe_w_down[i]}
        st_p = {'ssd': jnp.zeros((bp, SSD_HEADS, SSD_HEAD_DIM, SSD_STATE), F32),
                'ssd_conv': jnp.zeros((bp, SSD_CONV - 1, SSD_CONV_CH), x_prompt.dtype),
                'ccm_conv': jnp.zeros((bp, CCM_WIDTH - 1, MIX_B), x_prompt.dtype),
                's5_re': jnp.zeros((bp, S5_GROUPS, S5_STATE), F32),
                's5_im': jnp.zeros((bp, S5_GROUPS, S5_STATE), F32)}
        yp, sp = _layer(yp, p, st_p, True)
        st_s = {'ssd': state_ssd[i], 'ssd_conv': state_ssd_conv[i], 'ccm_conv': state_ccm_conv[i],
                'att_k': cache_att_k[i], 'att_v': cache_att_v[i], 's5_re': state_s5_re[i],
                's5_im': state_s5_im[i]}
        ys, ss = _layer(ys, p, st_s, False)
        for n in names:
            new_p[n].append(sp[n])
            new_s[n].append(ss[n])
    y_prompt = _rmsnorm(yp, g_final)
    y_sample = _rmsnorm(ys, g_final)
    sp = {n: jnp.stack(new_p[n]) for n in names}
    ss = {n: jnp.stack(new_s[n]) for n in names}
    return (y_prompt, y_sample, sp['ssd'], ss['ssd'], sp['ssd_conv'], ss['ssd_conv'], sp['ccm_conv'],
            ss['ccm_conv'], sp['att_k'], ss['att_k'], sp['att_v'], ss['att_v'], sp['s5_re'], ss['s5_re'],
            sp['s5_im'], ss['s5_im'])


_drawn_inputs = setup_inputs


def setup_inputs(seed=0):
    import zlib

    import numpy as np

    out = dict(_drawn_inputs(seed))
    spreads = {}
    factors = {'ssd_d': 200.0,
     'ssd_norm_w': 8.506,
     'ccm_ln_g': 11.986,
     'ccm_ln_b': 11.824,
     'ccm_pw_b': 7.827,
     'att_rel_bias': 18.659,
     's5_lam_re': 16.374,
     's5_glu_b': 16.463,
     'g_final': 24.062,
     'cache_att_k': 2.705,
     's5_c_re': 2.803,
     'g_ffn': 3.543,
     's5_c_im': 8.0}
    for name, (base, spread) in spreads.items():
        noise = np.random.default_rng([zlib.crc32(name.encode()), seed]).standard_normal(out[name].shape)
        drawn = base * np.exp(spread * noise) if base else spread * noise
        out[name] = jnp.asarray(drawn.astype(out[name].dtype))
    for name, factor in factors.items():
        out[name] = (out[name] * factor).astype(out[name].dtype)
    return out
```

```python
import math
from contextlib import ExitStack

import concourse.bass as bass
from concourse import mybir

F32 = mybir.dt.float32
I32 = mybir.dt.int32
ALU = mybir.AluOpType
ACT = mybir.ActivationFunctionType
AX = mybir.AxisListType
ds = bass.ds

P = 128
D = 1024
KT = D // P
TP, TS = 1024, 64
T = TP + TS
NT = TP // P + 1
NTOK = [P] * (NT - 1) + [TS]
HEADS, HD = 4, 64
EPS = 1e-6
ATT_SCALE = HD ** -0.5
WIN = 512
BANDW = WIN + P
CW, DW = 4, 31
XBW = (CW - 1) + TP + (CW - 1) + TS
VBW = (DW - 1) + TP + (DW - 1) + TS
VD = 260
ST = 8
NEG = -1e30
G, EPG = 4, 8
E = G * EPG
FF = 512
THR = -(-T // P)
BLOCKS = 48
SLOTS = (BLOCKS + 1) * P

FIELDS = [("g_mix", 8), ("conv_w", 16), ("conv_b", 4), ("dw_w", 62), ("dw_b", 2), ("ln_g", 2), ("ln_b", 2),
          ("pw_b", 2), ("ssd_d", 2), ("norm_w", 2), ("glu_b", 4), ("lam_re", 8), ("lam_im", 8), ("log_dt", 8),
          ("h0_re", 8), ("h0_im", 8), ("s5_d", 2), ("dt_bias", 4), ("a_log", 4), ("eps", 1), ("one", 1),
          ("thr", THR), ("iota", BLOCKS), ("order4", G), ("order8", EPG)]
COL, NCOL = {}, 0
for _n, _w in FIELDS:
    COL[_n] = (NCOL, _w)
    NCOL += _w


P5 = {"lrdt": 1, "angles": 9, "bb": 39, "tables": 83}
P5A = {"bbT": 5}
RT = {"d4": 2, "dm": 22, "pre": 37, "dest": 52, "routed": 59, "slotf": 60}


class Steps:

    def __init__(self, sem, *names):
        self.sem, self.names, self.n = sem, names, 0

    def of(self, name):
        assert self.names[self.n % len(self.names)] == name, (self.names, name)
        self.n += 1
        return self.sem, 1

    def at(self, rnd, name):
        return self.sem, rnd * len(self.names) + self.names.index(name) + 1


def encoder_step(nc, a, o):
    with ExitStack() as ctx:
        def sb(name, cols, dt=F32):
            return ctx.enter_context(nc.sbuf_tensor(name, [P, cols], dt))

        def sem(name):
            return ctx.enter_context(nc.semaphore(name))

        def steps(name, *names):
            return Steps(sem(name), *names)

        def bc(x, axis, n):
            x = x.unsqueeze(axis)
            return x.broadcast_to([n if d == axis else s for d, s in enumerate(x.shape)])

        hn_dram = nc.dram_tensor("hn_rows", [T, D], F32, kind="Internal").ap()
        slot_dram = nc.dram_tensor("slot_token", [SLOTS, 1], I32, kind="Internal").ap()
        out_dram = nc.dram_tensor("expert_rows", [2 * T, D], F32, kind="Internal").ap()

        arena1 = sb("arena1", 24576)
        arena2 = sb("arena2", NT * D)
        arena3 = sb("arena3", KT * T)
        arena4 = sb("arena4", 6400)
        cst = sb("params", NCOL)
        mats = sb("mats", 4 * P)
        small = sb("small", 1150)
        tables = sb("phase_tables", 2 * ST * P)
        ints = sb("ints", 4 * NT + 3 * BLOCKS + 8 + P, I32)

        def col(name, i=0, n=1):
            return cst[:, COL[name][0] + i:COL[name][0] + i + n]

        ident, ones, upper, negmask = (mats[:, i * P:(i + 1) * P] for i in range(4))

        class Arena:
            def __init__(self, t, at=0):
                self.t, self.at = t, at

            def take(self, n):
                self.at += n
                return self.t[:, self.at - n:self.at]

        a1 = Arena(arena1)
        xn = a1.take(KT * T).rearrange("p (k t) -> p k t", k=KT)
        wring = a1.take(4 * D).rearrange("p (r n) -> p r n", r=4)
        wvd = a1.take(KT * VD).rearrange("p (k n) -> p k n", k=KT)
        xb = a1.take(4 * XBW).rearrange("p (j t) -> p j t", j=4)
        sg = a1.take(2 * T).rearrange("p (j t) -> p j t", j=2)
        vc = a1.take(2 * T).rearrange("p (j t) -> p j t", j=2)
        s5 = Arena(arena1)

        def s5take():
            return s5.take(D).rearrange("p (s t) -> p s t", s=ST)
        s5u, s5g, s5t, s5h = ([s5take(), s5take()] for _ in range(4))
        s5v = [vc[:, 0, 0:D].rearrange("p (s t) -> p s t", s=ST),
               vc[:, 1, 0:D].rearrange("p (s t) -> p s t", s=ST)]
        s5m = Arena(arena1, KT * T)
        bb = [s5m.take(ST * 32).rearrange("p (s c) -> p s c", s=ST) for _ in range(2)]
        cc = [s5m.take(ST * 32).rearrange("p (s c) -> p s c", s=ST) for _ in range(2)]
        bbT = [s5m.take(2 * P).rearrange("p (j n) -> p j n", j=2) for _ in range(2)]
        s5raw = s5m.take(4 * ST * 16)
        s5w = s5raw.rearrange("p (m s c) -> p m s c", m=4, s=ST)
        glu_w = s5m.take(2 * 512).rearrange("p (k n) -> p k n", k=2)
        gel = sg
        w_out = Arena(arena1, KT * T).take(KT * D).rearrange("p (k n) -> p k n", k=KT)
        moe_w = arena1[:, :].rearrange("p (r n) -> p r n", r=2)
        wg = [moe_w[:, r, 0:4096].rearrange("p (k n) -> p k n", k=KT) for r in range(2)]
        wu = [moe_w[:, r, 4096:8192].rearrange("p (k n) -> p k n", k=KT) for r in range(2)]
        wd = [moe_w[:, r, 8192:12288].rearrange("p (k n) -> p k n", k=4) for r in range(2)]

        a2 = Arena(arena2)
        kt = a2.take(2 * 1600).rearrange("p (j t) -> p j t", j=2)
        vt = a2.take(13 * 256).rearrange("p (j n) -> p j n", j=13)
        vb = a2.take(2 * VBW).rearrange("p (j t) -> p j t", j=2)
        hres = arena2[:, :].rearrange("p (i n) -> p i n", i=NT)

        mix = arena3[:, :].rearrange("p (k t) -> p k t", k=KT)
        Z, CA, Q, UD = 0, 2, 4, 6
        a3 = Arena(arena3)
        xg = [a3.take(D) for _ in range(2)]
        xgT = [a3.take(D).rearrange("p (k n) -> p k n", k=KT) for _ in range(2)]
        actg = [a3.take(FF) for _ in range(2)]
        hmid = [a3.take(FF) for _ in range(2)]
        orow = [a3.take(D) for _ in range(2)]

        a4 = Arena(arena4)
        bias = a4.take(HEADS * BANDW).rearrange("p (h k) -> p h k", h=HEADS)
        sc, pr, pts = ([a4.take(BANDW) for _ in range(2)] for _ in range(3))
        sq = [arena4[:, i * T:(i + 1) * T] for i in range(2)]
        w4 = Arena(arena4, HEADS * BANDW)
        ua, ebc, dm, ce = (w4.take(512).rearrange("p (h t) -> p h t", h=4) for _ in range(4))
        xdt = w4.take(256)
        xdd = w4.take(256)
        btok = w4.take(P)
        pww = w4.take(2 * 256).rearrange("p (k n) -> p k n", k=2)
        v4 = Arena(arena4)
        xtok = [v4.take(D) for _ in range(2)]
        hn = [v4.take(D) for _ in range(2)]
        gffn = v4.take(D)
        hnT = v4.take(D).rearrange("p (k n) -> p k n", k=KT)
        f4 = Arena(arena4)
        og = [[f4.take(D) for _ in range(2)] for _ in range(2)]
        gfin = f4.take(D)
        f3 = Arena(arena3)
        yrow = [f3.take(D) for _ in range(2)]
        sqrow = [f3.take(D) for _ in range(2)]

        sm = Arena(small)
        dtr, dta, dtt, aa, nacs, dec, etot = (
            sm.take(NT * 4).rearrange("p (i h) -> p i h", h=4) for _ in range(7))
        aexp = sm.take(4)
        state = [sm.take(P) for _ in range(2)]
        tail = sm.take(24).rearrange("p (j s w) -> p j s w", j=4, s=2)
        nmx, rsum, rinv = (sm.take(NT * HEADS) for _ in range(3))
        s5p = sm.take(16 * ST).rearrange("p (n s) -> p n s", s=ST)
        s5end = sm.take(2 * 2 * ST).rearrange("p (r c s) -> p r c s", r=2, c=2)
        cmul = sm.take(4 * ST).rearrange("p (n s) -> p n s", s=ST)
        ssum, hrs = sm.take(NT), sm.take(NT)
        diag = [sm.take(P) for _ in range(2)]
        DT, MAG, TH, COS, SIN, AR, AI, CR, CI, T0, T1, T2 = range(12)

        cosT = tables[:, 0:ST * P].rearrange("p (s t) -> p s t", s=ST)
        sinT = tables[:, ST * P:].rearrange("p (s t) -> p s t", s=ST)
        rt = Arena(tables)
        rw = rt.take(KT * 36).rearrange("p (k n) -> p k n", k=KT)
        lgt = rt.take(NT * 36).rearrange("p (i n) -> p i n", i=NT)
        ohg = rt.take(NT * G).rearrange("p (i g) -> p i g", g=G)
        d4 = rt.take(NT * G).rearrange("p (i g) -> p i g", g=G)
        les = rt.take(NT * EPG).rearrange("p (i e) -> p i e", e=EPG)
        oh = [rt.take(NT * EPG).rearrange("p (i e) -> p i e", e=EPG) for _ in range(2)]
        t8 = rt.take(NT * EPG).rearrange("p (i e) -> p i e", e=EPG)
        m4, mm, m1, m2, pgr, gs = (rt.take(NT) for _ in range(6))
        gate = [rt.take(NT) for _ in range(2)]
        destf = rt.take(2 * NT).rearrange("p (k i) -> p k i", k=2)
        nblk, bend, base = (rt.take(E) for _ in range(3))
        eidf = rt.take(BLOCKS)
        slotf = rt.take(P)
        slotc = rt.take(BLOCKS + 1)
        slotm = rt.take(BLOCKS + 1)
        rb = Arena(arena1)
        prod = rb.take(NT * E).rearrange("p (i g e) -> p i g e", g=G, e=EPG)
        oe = [rb.take(NT * E).rearrange("p (i g e) -> p i g e", g=G, e=EPG) for _ in range(2)]
        asg = rb.take(NT * E).rearrange("p (i e) -> p i e", e=E)
        pre = rb.take((NT + 1) * E).rearrange("p (i e) -> p i e", e=E)
        dmap = rb.take(NT * E).rearrange("p (i e) -> p i e", e=E)
        cmp = rb.take(BLOCKS * E)
        ia = Arena(ints)
        asgid = ia.take(2 * NT).rearrange("p (k i) -> p k i", k=2)
        dest = ia.take(2 * NT).rearrange("p (k i) -> p k i", k=2)
        eid = ia.take(BLOCKS)
        npairs = ia.take(1)
        slot_out = ia.take(BLOCKS + 1)
        slot_in = ia.take(BLOCKS + 1)
        curidx = [ia.take(1) for _ in range(2)]
        curout = [ia.take(1) for _ in range(2)]
        slots_rows = ia.take(P)

        psA = ctx.enter_context(nc.psum_tensor("psA", [P, 1536], F32))
        psB = ctx.enter_context(nc.psum_tensor("psB", [P, 1536], F32))
        psC = ctx.enter_context(nc.psum_tensor("psC", [P, 1024], F32))
        AB = [psA, psB]
        CH = [(0, 512), (512, 1024), (1024, T)]

        s_params, s_hist, s_cache, s_bias = sem("params_in"), sem("histories_in"), sem("cache_in"), sem("bias_in")
        s_x = [sem(f"x{k}_in") for k in range(KT)]
        s_w = [sem(f"w_in_slot{k}") for k in range(4)]
        s_wvd, s_s5w, s_pww = sem("w_vdt_in"), sem("s5_weights_in"), sem("pointwise_in")
        s_out = sem("states_out")
        s_wout, s_gffn = sem("w_out_in"), sem("g_ffn_in")
        s_xtok = [sem(f"x_rows{k}_in") for k in range(2)]
        s_hst = [sem(f"hn_rows{k}_out") for k in range(2)]
        s_slotz, s_scat, s_slotin = sem("slots_cleared"), sem("slots_scattered"), sem("slots_in")
        s_wgu = [sem(f"gate_up{k}_in") for k in range(2)]
        s_wd = [sem(f"down{k}_in") for k in range(2)]
        s_xg = [sem(f"gathered{k}") for k in range(2)]
        s_os = [sem(f"expert_rows{k}_out") for k in range(2)]
        s_og = [sem(f"expert_rows{k}_back") for k in range(2)]
        s_yo, s_gfin = [sem(f"y_rows{k}_out") for k in range(2)], sem("g_final_in")
        zeroed = sem("buffers_zeroed")
        nrm_act = steps("norm_act", *["sq"] * KT, "ln", "rs")
        nrm_pe = sem("norm_pe")
        xn_dve = sem("xn_ready")
        proj = sem("proj_done")
        ev = sem("proj_moved")
        gated = sem("conv_input_gated")
        vd_pe, vd_ev = sem("vdt_done"), sem("vdt_moved")
        dtp_dve = steps("dt_dve", "raw", "abs", "dt", "a", "nacs", "decin")
        dtp_act = steps("dt_act", "e", "ln", "aexp", "dec", "etot")
        dtp_pe = sem("dt_cumsums")
        cv_dve = steps("conv4_dve", "t0", "t1", "t2", "t3")
        cv_act = sem("conv4_silu")
        tailed = sem("conv_tail_copied")
        ssd_pe = steps("ssd_pe", "bc", "cb", "tr", "y", "st")
        ssd_act = steps("ssd_act", "ebc", "decay", "btok")
        ssd_dve = steps("ssd_dve", "dm", "m", "xdt", "ce", "state", "yd")
        ssd_pool = steps("ssd_pool", "ua", "xdd")
        yg_dve = steps("ssd_out_dve", "gate0", "gate1", "norm")
        yg_act = steps("ssd_out_act", "sq0", "sq1", "ln0", "rs0", "ln1", "rs1")
        yg_pe = sem("ssd_out_pe")
        dw_dve = sem("dwconv_taps")
        cm_act = steps("ccm_act", "v0", "v1", "sq0", "sq1", "ln", "rs", "silu0", "silu1", "out0", "out1")
        cm_pe = steps("ccm_pe", "mu", "var", "pw0", "pw1")
        cm_dve = steps("ccm_dve", "cen0", "cen1", "n0", "n1")
        at_s, at_pt, at_pv = sem("att_scores"), sem("att_probsT"), sem("att_out")
        at_add, at_max, at_rinv, at_diag = sem("att_biased"), sem("att_max"), sem("att_rinv"), sem("att_diag")
        at_exp, at_ptc, at_ovc = sem("att_exp"), sem("att_probsT_moved"), sem("att_out_moved")
        p5_dve, p5_act, p5_pe = sem("s5_setup_dve"), sem("s5_setup_act"), sem("s5_setup_pe")
        s5_x, s5_y = sem("s5_inputs"), sem("s5_outputs")
        s5_dve = steps("s5_dve", "p0", "u0", "p1", "u1", "scan", "carry", "end")
        s5_yd = sem("s5_y_moved")
        s5_pool = steps("s5_pool", "m0", "re", "m1", "im")
        glu_act = steps("glu_act", "gelu0", "gelu1", "sig0", "sig1")
        glu_pe = steps("glu_pe", "gb0", "gb1", "ga0", "ga1")
        glu_dve = sem("glu_dve")
        wo_pe = sem("h_products")
        tr_pe, lg_pe = sem("hn_transposed"), sem("logits")
        wo_dve = steps("h_dve", "add", "hn")
        wo_act = steps("h_act", "sq", "ln", "rs")
        hte = sem("hnT_moved")
        lge = sem("logits_moved")
        rt_dve, rt_act, rt_pe, rt_pool = sem("route_dve"), sem("route_act"), sem("route_pe"), sem("route_pool")
        indirect_go = sem("indirect_go")
        slots_ready, idxc, outc = sem("slots_ready"), sem("index_copied"), sem("out_index_copied")
        m_xt, m_xte, m_gu, m_sil, m_hm, m_ht, m_hte, m_dn, m_dnA, m_dnD, m_free = (
            [sem(f"moe_{n}{k}") for k in range(2)]
            for n in ("xT", "xT_moved", "gate_up", "silu", "product", "productT", "productT_moved", "down",
                      "down_moved_act", "down_moved_dve",
                      "rows_free"))
        f_dve = steps("final_dve", "add1", "add2", "y")
        f_act = steps("final_act", "sq", "ln", "rs")

        block = ctx.enter_context(nc.Block())

        TILES = ([("xbc", j) for j in range(4)] + [("k", 0), ("k", 1), ("g", 0), ("g", 1), ("a", 0), ("a", 1),
                 ("q", 0), ("q", 1), ("z", 0), ("z", 1), ("ud", 0), ("ud", 1)])
        EV_AT = {}
        for _j, _t in enumerate(TILES):
            if _t[0] != "a":
                EV_AT[_j] = len(EV_AT) + 1
        A0 = TILES.index(("a", 0))

        def tile_moved(eng, j):
            if TILES[j][0] == "a":
                eng.wait_ge(gated, j - A0 + 1)
            else:
                eng.wait_ge(ev, EV_AT[j])

        def tok(i):
            return slice(i * P, i * P + NTOK[i])

        def band(i):
            if i == NT - 1:
                return 1024, [(8 + n, P) for n in range(4)] + [(12, TS)], 0
            lo = max(0, i - 4)
            return lo * P, [(n, P) for n in range(lo, i + 1)], (4 - (i - lo)) * P

        ROUNDS = [(i, h) for i in range(NT) for h in range(HEADS)]

        @block.sync
        def _(sp):
            sp.dma_start(cst[:, :], a["params"]).then_inc(s_params, 16)
            sp.dma_start(mats[:, :], a["mats"]).then_inc(s_params, 16)
            sp.dma_start(asgid, a["asgid"]).then_inc(s_params, 16)
            for k in range(KT):
                sp.dma_start(xn[:, k, :], a["xT"][k * P:(k + 1) * P, :]).then_inc(s_x[k], 16)
                if k < 4:
                    sp.dma_start(wring[:, k, :], a["w_cm"][k]).then_inc(s_w[k], 16)
            sp.dma_start(wvd, a["w_vd"]).then_inc(s_wvd, 16)
            sp.dma_start(xb[:, :, CW - 1 + TP:CW - 1 + TP + CW - 1], a["ssd_hist"]).then_inc(s_hist, 16)
            sp.dma_start(vb[:, :, DW - 1 + TP:DW - 1 + TP + DW - 1], a["ccm_hist"]).then_inc(s_hist, 16)
            sp.dma_start(state[1], a["ssd_h0"]).then_inc(s_hist, 16)
            sp.dma_start(kt[:, :, 1024:1536], a["k_cache"]).then_inc(s_cache, 16)
            sp.dma_start(vt[:, 8:12, :], a["v_cache"]).then_inc(s_cache, 16)
            for j in range(4, len(TILES)):
                sp.wait_ge(proj, j - 3)
                sp.dma_start(wring[:, j % 4, :], a["w_cm"][j]).then_inc(s_w[j % 4], 16)
            sp.wait_ge(nrm_pe, KT)
            sp.dma_start(bias, a["bias"]).then_inc(s_bias, 16)
            sp.dma_start(pww, a["pw_w"]).then_inc(s_pww, 16)
            sp.wait_ge(proj, len(TILES))
            sp.dma_start(s5raw, a["s5_w"]).then_inc(s_s5w, 16)
            sp.dma_start(glu_w, a["glu_w"]).then_inc(s_s5w, 16)
            sp.wait_ge(tailed, 1)
            sp.dma_start(o["ssd_tail"], tail).then_inc(s_out, 16)
            sp.wait_ge(gated, 2)
            sp.dma_start(o["ccm_p"], vb[:, :, TP:TP + DW - 1]).then_inc(s_out, 16)
            sp.dma_start(o["ccm_s"], vb[:, :, VBW - (DW - 1):VBW]).then_inc(s_out, 16)
            sp.wait_ge(ev, len(EV_AT))
            sp.dma_start(o["k_p"], kt[:, :, TP - WIN:TP]).then_inc(s_out, 16)
            sp.dma_start(o["k_s"], kt[:, :, 1536:1600]).then_inc(s_out, 16)
            sp.wait_ge(vd_ev, NT)
            sp.dma_start(o["v_p"], vt[:, 4:8, :]).then_inc(s_out, 16)
            sp.dma_start(o["v_s"], vt[0:TS, 12, :]).then_inc(s_out, 16)
            sp.wait_ge(*ssd_dve.at(NT - 1, "state"))
            sp.dma_start(o["ssd_p"], state[0]).then_inc(s_out, 16)
            sp.dma_start(o["ssd_s"], state[1]).then_inc(s_out, 16)
            sp.wait_ge(*s5_dve.at(NT - 1, "end"))
            sp.dma_start(o["s5_end"], s5end).then_inc(s_out, 16)
            sp.wait_ge(glu_dve, 2)
            sp.wait_ge(*yg_dve.at(0, "norm"))
            sp.dma_start(w_out, a["w_out"]).then_inc(s_wout, 16)
            sp.dma_start(gffn, a["g_ffn"]).then_inc(s_gffn, 16)
            sp.dma_start(rw, a["w_route"]).then_inc(s_gffn, 16)
            for i in range(NT):
                if i >= 2:
                    sp.wait_ge(*wo_dve.at(i - 2, "add"))
                sp.dma_start(xtok[i % 2][0:NTOK[i], :], a["x_rows"][tok(i), :]).then_inc(s_xtok[i % 2], 16)
                if i >= 1:
                    sp.wait_ge(*wo_dve.at(i - 1, "hn"))
                    sp.dma_start(hn_dram[tok(i - 1), :], hn[(i - 1) % 2][0:NTOK[i - 1], :]
                                 ).then_inc(s_hst[(i - 1) % 2], 16)
            sp.wait_ge(*wo_dve.at(NT - 1, "hn"))
            sp.dma_start(hn_dram[tok(NT - 1), :], hn[(NT - 1) % 2][0:TS, :]).then_inc(s_hst[(NT - 1) % 2], 16)
            sp.wait_ge(rt_dve, RT["routed"])
            pairs = sp.value_load(npairs[0:1, :], min_val=0, max_val=BLOCKS // 2)
            with sp.Fori(0, BLOCKS // 2) as i:
                with sp.If(pairs > i):
                    for r in range(2):
                        e = sp.value_load(eid[0:1, ds(2 * i + r, 1)], min_val=0, max_val=E - 1)
                        sp.wait_ge(m_gu[r], i + 1)
                        sp.dma_start(wg[r], a["w_gate"][ds(e, 1), :, :].rearrange("o (p k) n -> (o p) k n", k=KT)
                                     ).then_inc(s_wgu[r], 16)
                        sp.dma_start(wu[r], a["w_up"][ds(e, 1), :, :].rearrange("o (p k) n -> (o p) k n", k=KT)
                                     ).then_inc(s_wgu[r], 16)
                        sp.wait_ge(m_dn[r], i + 1)
                        sp.dma_start(wd[r], a["w_down"][ds(e, 1), :, :].rearrange("o (p k) n -> (o p) k n", k=4)
                                     ).then_inc(s_wd[r], 16)
            sp.dma_start(gfin, a["g_final"]).then_inc(s_gfin, 16)
            for i in range(NT):
                sp.wait_ge(*f_dve.at(i, "y"))
                dst = o["y_p"][tok(i), :] if i < NT - 1 else o["y_s"]
                sp.dma_start(dst, yrow[i % 2][0:NTOK[i], :]).then_inc(s_yo[i % 2], 16)
            sp.wait_ge(s_out, 16 * 10)
            sp.wait_ge(s_yo[0], 16 * 5)
            sp.wait_ge(s_yo[1], 16 * 4)

        @block.tensor
        def _(te):
            te.wait_ge(s_params, 48)
            for k in range(KT):
                te.wait_ge(*nrm_act.at(0, "sq") if k == 0 else (nrm_act.sem, k + 1))
                for c, (lo, hi) in enumerate(CH):
                    mm = te.matmul(psB[:, lo:hi], ones, sq[k % 2][:, lo:hi], start=(k == 0), stop=(k == KT - 1))
                mm.then_inc(nrm_pe, 1)
            for j in range(len(TILES)):
                te.wait_ge(s_w[j % 4], 16 * (j // 4 + 1))
                if j >= 2:
                    tile_moved(te, j - 2)
                for k in range(KT):
                    if j == 0:
                        te.wait_ge(xn_dve, k + 1)
                    for lo, hi in CH:
                        mm = te.matmul(AB[j % 2][:, lo:hi], wring[:, j % 4, k * P:(k + 1) * P], xn[:, k, lo:hi],
                                       start=(k == 0), stop=(k == KT - 1))
                mm.then_inc(proj, 1)
            te.wait_ge(s_wvd, 16)
            for i in range(NT):
                if i >= 2:
                    te.wait_ge(vd_ev, i - 1)
                for k in range(KT):
                    mm = te.matmul(psC[0:NTOK[i], 512 * (i % 2):512 * (i % 2) + VD], xn[:, k, tok(i)], wvd[:, k, :],
                                   start=(k == 0), stop=(k == KT - 1))
                mm.then_inc(vd_pe, 1)
            te.wait_ge(*dtp_dve.at(0, "a"))
            te.wait_ge(vd_ev, NT)
            L8 = slice(0, TS)
            te.matmul(psC[:, 0:32], upper, aa[:, 0:8, :], start=True, stop=True)
            te.matmul(psC[:, 32:36], upper[L8, :], aa[L8, 8, :], start=True, stop=True)
            te.matmul(psC[:, 512:544], ones, aa[:, 0:8, :], start=True, stop=True)
            te.matmul(psC[:, 544:548], ones[L8, :], aa[L8, 8, :], start=True, stop=True).then_inc(dtp_pe, 1)
            te.wait_ge(cv_act, 4)
            te.wait_ge(*dtp_act.at(0, "etot"))
            te.wait_ge(s_hist, 48)
            for c in range(NT):
                L = NTOK[c]
                te.wait_ge(*ssd_pool.at(c, "ua"))
                if c:
                    te.wait_ge(*ssd_dve.at(c - 1, "dm"))
                    te.wait_ge(*ssd_act.at(c - 1, "ebc"))
                te.matmul(psA[:, 0:512], ones[0:L, :], ua[0:L], start=True, stop=True).then_inc(*ssd_pe.of("bc"))
                if c:
                    te.wait_ge(*ssd_dve.at(c - 1, "m"))
                te.matmul(psA[0:L, 512:512 + L], xb[0:64, 2, tok(c)], xb[0:64, 3, tok(c)], start=True, stop=True)
                te.matmul(psB[0:L, 0:L], xb[64:128, 2, tok(c)], xb[64:128, 3, tok(c)], start=True, stop=True
                          ).then_inc(*ssd_pe.of("cb"))
                if c:
                    te.wait_ge(*ssd_dve.at(c - 1, "xdt"))
                    te.wait_ge(*ssd_act.at(c - 1, "btok"))
                for j in range(3):
                    at = j * P if j < 2 else 512
                    mm = te.transpose(psC[0:L, at:at + P], xb[:, j, tok(c)], ident)
                mm.then_inc(*ssd_pe.of("tr"))
                te.wait_ge(*ssd_dve.at(c, "ce"))
                if c:
                    te.wait_ge(*ssd_dve.at(c - 1, "yd"))
                st = state[1 if c == NT - 1 else 0]
                for h in range(HEADS):
                    g, hh = divmod(h, 2)
                    y = psB[hh * 64:hh * 64 + 64, 512 * (1 + g):512 * (1 + g) + L]
                    mm = te.matmul(y, xdt[:, h * 64:h * 64 + 64], dm[:, h, 0:L], start=True, stop=(c == 0))
                    if c:
                        mm = te.matmul(y, st[g * 64:g * 64 + 64, hh * 64:hh * 64 + 64],
                                       ce[g * 64:g * 64 + 64, h, 0:L], start=False, stop=True)
                mm.then_inc(*ssd_pe.of("y"))
                te.wait_ge(*ssd_pool.at(c, "xdd"))
                te.wait_ge(*ssd_act.at(c, "btok"))
                for g in range(2):
                    mm = te.matmul(psA[g * 64:g * 64 + 64, 1024:1152], btok[0:L, g * 64:g * 64 + 64],
                                   xdd[0:L, g * P:(g + 1) * P], start=True, stop=True)
                mm.then_inc(*ssd_pe.of("st"))
            te.wait_ge(*ssd_dve.at(NT - 1, "yd"))
            for g in range(2):
                te.wait_ge(*yg_act.at(0, f"sq{g}"))
                for lo, hi in CH:
                    mm = te.matmul(AB[g][:, lo:hi], ones, sg[:, g, lo:hi], start=True, stop=True)
                mm.then_inc(yg_pe, 1)
            te.wait_ge(*cm_act.at(0, "v1"))
            for j in range(2):
                for lo, hi in CH:
                    mm = te.matmul(psA[:, lo:hi], ones, vc[:, j, lo:hi], start=(j == 0), stop=(j == 1))
            mm.then_inc(*cm_pe.of("mu"))
            te.wait_ge(*cm_act.at(0, "sq1"))
            for j in range(2):
                for lo, hi in CH:
                    mm = te.matmul(psB[:, lo:hi], ones, sg[:, j, lo:hi], start=(j == 0), stop=(j == 1))
            mm.then_inc(*cm_pe.of("var"))
            te.wait_ge(s_pww, 16)
            te.wait_ge(*cm_act.at(0, "silu1"))
            for m in range(2):
                for k in range(2):
                    for lo, hi in CH:
                        mm = te.matmul(AB[m][:, lo:hi], pww[:, k, m * P:(m + 1) * P], vc[:, k, lo:hi],
                                       start=(k == 0), stop=(k == 1))
                mm.then_inc(*cm_pe.of(f"pw{m}"))
            te.wait_ge(*cm_act.at(0, "out1"))
            te.wait_ge(s_cache, 32)

            def scores(r):
                i, h = ROUNDS[r]
                pair, hh = divmod(h, 2)
                k0, tiles, _ = band(i)
                nk = sum(w for _, w in tiles)
                rows = slice(hh * 64, hh * 64 + 64)
                if r >= 2:
                    te.wait_ge(at_add, r - 1)
                for lo in range(0, nk, 512):
                    hi = min(lo + 512, nk)
                    mm = te.matmul(AB[r % 2][0:NTOK[i], lo:hi], mix[rows, Q + pair, tok(i)],
                                   kt[rows, pair, k0 + lo:k0 + hi], start=True, stop=True)
                mm.then_inc(at_s, 1)

            def outputs(r):
                i, h = ROUNDS[r]
                hh = h % 2
                _, tiles, _ = band(i)
                nq = NTOK[i]
                te.wait_ge(at_diag, r + 1)
                te.wait_ge(at_exp, r + 1)
                if r >= 1:
                    te.wait_ge(at_ptc, r)
                for n, (_, w) in enumerate(tiles):
                    mm = te.matmul(psC[0:w, n * nq:(n + 1) * nq], pr[r % 2][0:nq, n * P:n * P + w],
                                   diag[r % 2][0:nq, 0:nq], start=True, stop=True)
                mm.then_inc(at_pt, 1)
                te.wait_ge(at_ptc, r + 1)
                if r >= 2:
                    te.wait_ge(at_ovc, r - 1)
                for n, (v, w) in enumerate(tiles):
                    mm = te.matmul(AB[r % 2][hh * 64:hh * 64 + 64, 1024:1024 + nq], vt[0:w, v, h * 64:h * 64 + 64],
                                   pts[r % 2][0:w, n * nq:(n + 1) * nq], start=(n == 0), stop=(n == len(tiles) - 1))
                mm.then_inc(at_pv, 1)

            scores(0)
            for r in range(len(ROUNDS)):
                if r + 1 < len(ROUNDS):
                    scores(r + 1)
                outputs(r)
            te.wait_ge(p5_dve, P5["bb"])
            te.wait_ge(at_ptc, len(ROUNDS))
            for m in range(2):
                for j in range(2):
                    mm = te.transpose(psC[:, (2 * m + j) * P:(2 * m + j + 1) * P],
                                      bb[m].rearrange("p s c -> p (s c)")[:, j * P:(j + 1) * P], ident)
            mm.then_inc(p5_pe, 1)
            te.wait_ge(p5_act, P5A["bbT"])
            te.wait_ge(at_ovc, len(ROUNDS))

            def s5_in(c):
                L = NTOK[c]
                if c:
                    te.wait_ge(*s5_dve.at(c - 1, "p1"))
                for q in range(4):
                    for jt in range(2):
                        for m in range(2):
                            at = 512 * (q % 2) + (2 * jt + m) * P
                            mm = te.matmul(AB[q // 2][:, at:at + L], bbT[m][32 * q:32 * q + 32, jt, :],
                                           mix[32 * q:32 * q + 32, UD + jt, tok(c)], start=True, stop=True)
                mm.then_inc(s5_x, 1)

            def s5_out(c):
                L = NTOK[c]
                te.wait_ge(*s5_pool.at(c, "im"))
                if c:
                    te.wait_ge(s5_yd, c)
                for s in range(ST):
                    jt, q = divmod(s, 4)
                    for m in range(2):
                        mm = te.matmul(psC[32 * q:32 * q + 32, 512 * jt:512 * jt + L], cc[m][:, s, :],
                                       s5h[m][:, s, 0:L], start=(m == 0), stop=(m == 1))
                mm.then_inc(s5_y, 1)

            s5_in(0)
            for c in range(NT):
                if c + 1 < NT:
                    s5_in(c + 1)
                s5_out(c)
            te.wait_ge(s5_yd, NT)
            te.wait_ge(*glu_act.at(0, "gelu1"))
            for m, name in ((2, "gb0"), (3, "gb1"), (0, "ga0"), (1, "ga1")):
                if m < 2:
                    te.wait_ge(*glu_act.at(0, f"sig{m}"))
                for k in range(2):
                    for lo, hi in CH:
                        mm = te.matmul(AB[m % 2][:, lo:hi], glu_w[:, k, m * P:(m + 1) * P], gel[:, k, lo:hi],
                                       start=(k == 0), stop=(k == 1))
                mm.then_inc(*glu_pe.of(name))
            te.wait_ge(s_wout, 16)
            te.wait_ge(glu_dve, 2)

            def h_tile(i):
                if i >= 2:
                    te.wait_ge(*wo_dve.at(i - 2, "add"))
                for n in range(2):
                    for k in range(KT):
                        mm = te.matmul(AB[i % 2][0:NTOK[i], n * 512:(n + 1) * 512], mix[:, k, tok(i)],
                                       w_out[:, k, n * 512:(n + 1) * 512], start=(k == 0), stop=(k == KT - 1))
                mm.then_inc(wo_pe, 1)

            def logit_tile(i):
                te.wait_ge(*wo_dve.at(i, "hn"))
                if i:
                    te.wait_ge(hte, i)
                for k in range(KT):
                    mm = te.transpose(psC[:, k * P:k * P + NTOK[i]], hn[i % 2][0:NTOK[i], k * P:(k + 1) * P],
                                      ident[0:NTOK[i], 0:NTOK[i]])
                mm.then_inc(tr_pe, 1)
                te.wait_ge(hte, i + 1)
                if i >= 2:
                    te.wait_ge(lge, i - 1)
                for k in range(KT):
                    mm = te.matmul(AB[i % 2][0:NTOK[i], 1024:1060], hnT[:, k, 0:NTOK[i]], rw[:, k, :],
                                   start=(k == 0), stop=(k == KT - 1))
                mm.then_inc(lg_pe, 1)

            te.wait_ge(s_gffn, 32)
            h_tile(0)
            for i in range(NT):
                if i + 1 < NT:
                    h_tile(i + 1)
                logit_tile(i)
            te.wait_ge(rt_dve, RT["pre"])
            te.matmul(psA[:, 0:NT * E], upper, asg, start=True, stop=False)
            te.matmul(psA[:, 0:NT * E], ones, pre[:, 0:NT, :], start=False, stop=True)
            te.matmul(psB[:, 0:E], ones, pre[:, NT, :], start=True, stop=True).then_inc(rt_pe, 1)
            te.wait_ge(rt_dve, RT["slotf"])
            te.transpose(psC[:, 0:BLOCKS + 1], slotf[0:BLOCKS + 1, :], ident[0:BLOCKS + 1, 0:BLOCKS + 1]
                         ).then_inc(rt_pe, 1)

            def turn_rows(b, n):
                te.wait_ge(s_xg[b], 16 * n)
                for k in range(KT):
                    mm = te.transpose(psC[:, k * P:(k + 1) * P], xg[b].rearrange("p (m k) -> p k m", k=KT)[:, k, :],
                                      ident)
                mm.then_inc(m_xt[b], 1)

            te.wait_ge(slots_ready, 1)
            turn_rows(0, 1)
            pairs = te.value_load(npairs[0:1, :], min_val=0, max_val=BLOCKS // 2)
            with te.Fori(0, BLOCKS // 2) as i:
                with te.If(pairs > i):
                    for r in range(2):
                        te.wait_ge(m_xte[r], i + 2)
                        te.wait_ge(s_wgu[r], 32 * i + 32)
                        te.wait_ge(m_hm[1 - r], i + r + 1)
                        for w, at in ((wg[r], 0), (wu[r], 512)):
                            for k in range(KT):
                                mm = te.matmul(psA[:, at:at + FF], xgT[r][:, k, :], w[:, k, :],
                                               start=(k == 0), stop=(k == KT - 1))
                        mm.then_inc(m_gu[r], 1)
                        turn_rows(1 - r, i + 1 + r)
                        te.wait_ge(m_hm[r], i + 2)
                        te.wait_ge(m_hte[1 - r], i + r + 1)
                        for k in range(4):
                            mm = te.transpose(psA[:, 1024 + k * P:1024 + (k + 1) * P],
                                              hmid[r].rearrange("p (m k) -> p k m", k=4)[:, k, :], ident)
                        mm.then_inc(m_ht[r], 1)
                        te.wait_ge(m_hte[r], i + 2)
                        te.wait_ge(s_wd[r], 16 * i + 16)
                        te.wait_ge(m_dnA[1 - r], i + r + 1)
                        te.wait_ge(m_dnD[1 - r], i + r + 1)
                        for n in range(2):
                            for k in range(4):
                                mm = te.matmul(psB[:, n * 512:(n + 1) * 512], actg[r][:, k * P:(k + 1) * P],
                                               wd[r][:, k, n * 512:(n + 1) * 512], start=(k == 0), stop=(k == 3))
                        mm.then_inc(m_dn[r], 1)

        @block.scalar
        def _(ac):
            ac.wait_ge(s_params, 48)
            for k in range(KT):
                ac.wait_ge(s_x[k], 16)
                if k >= 2:
                    ac.wait_ge(nrm_pe, k - 1)
                ac.activation(sq[k % 2], xn[:, k, :], ACT.Square).then_inc(*nrm_act.of("sq"))
            ac.wait_ge(nrm_pe, KT)
            ac.activation(psB[:, 0:T], psB[:, 0:T], ACT.Ln, scale=1.0 / D, bias=col("eps")).then_inc(*nrm_act.of("ln"))
            ac.wait_ge(nrm_act.sem, KT + 1)
            ac.activation(psB[:, 0:T], psB[:, 0:T], ACT.Exp, scale=-0.5).then_inc(*nrm_act.of("rs"))
            ac.wait_ge(zeroed, 3)
            for j, (kind, n) in enumerate(TILES):
                if kind == "a":
                    continue
                ac.wait_ge(proj, j + 1)
                ps = AB[j % 2]
                if kind == "xbc":
                    ac.copy(xb[:, n, CW - 1:CW - 1 + TP], ps[:, 0:TP])
                    last = ac.copy(xb[:, n, XBW - TS:XBW], ps[:, TP:T])
                elif kind == "k":
                    ac.copy(kt[:, n, 0:TP], ps[:, 0:TP])
                    last = ac.copy(kt[:, n, 1536:1600], ps[:, TP:T])
                elif kind == "g":
                    last = ac.activation(sg[:, n, :], ps[:, 0:T], ACT.Sigmoid)
                elif kind == "q":
                    last = ac.copy(mix[:, Q + n, :], ps[:, 0:T])
                elif kind == "z":
                    last = ac.activation(mix[:, Z + n, :], ps[:, 0:T], ACT.Silu)
                else:
                    last = ac.copy(mix[:, UD + n, :], ps[:, 0:T])
                last.then_inc(ev, 1)
            for i in range(NT):
                ac.wait_ge(vd_pe, i + 1)
                M, at = NTOK[i], 512 * (i % 2)
                ac.copy(vt[0:M, i if i < NT - 1 else 12, :], psC[0:M, at:at + 256])
                ac.copy(dtr[0:M, i, :], psC[0:M, at + 256:at + VD]).then_inc(vd_ev, 1)
            ac.wait_ge(tailed, 1)
            for j in range(4):
                ac.wait_ge(*cv_dve.at(j, "t3"))
                ac.activation(xb[:, j, 0:TP], AB[j % 2][:, 0:TP], ACT.Silu, bias=col("conv_b", j))
                ac.activation(xb[:, j, TP:T], AB[j % 2][:, TP + CW - 1:T + CW - 1], ACT.Silu, bias=col("conv_b", j)
                              ).then_inc(cv_act, 1)
            ac.wait_ge(*dtp_dve.at(0, "abs"))
            ac.activation(dta, dta, ACT.Exp, scale=-1.0).then_inc(*dtp_act.of("e"))
            ac.wait_ge(*dtp_act.at(0, "e"))
            ac.activation(dta, dta, ACT.Ln, bias=col("one")).then_inc(*dtp_act.of("ln"))
            ac.activation(aexp, col("a_log", 0, 4), ACT.Exp).then_inc(*dtp_act.of("aexp"))
            ac.wait_ge(*dtp_dve.at(0, "decin"))
            ac.activation(dec, dec, ACT.Exp).then_inc(*dtp_act.of("dec"))
            ac.activation(etot.rearrange("p i h -> p (i h)"), psC[:, 512:548], ACT.Exp).then_inc(*dtp_act.of("etot"))
            for c in range(NT):
                L = NTOK[c]
                ac.wait_ge(*ssd_pe.at(c, "bc"))
                if c:
                    ac.wait_ge(*ssd_dve.at(c - 1, "ce"))
                ac.activation(ebc.rearrange("p h t -> p (h t)"), psA[:, 0:512], ACT.Exp).then_inc(*ssd_act.of("ebc"))
                ac.wait_ge(*ssd_dve.at(c, "dm"))
                for h in range(HEADS):
                    last = ac.activation(dm[0:L, h, 0:L], dm[0:L, h, 0:L], ACT.Exp, bias=nacs[0:L, c, h:h + 1])
                last.then_inc(*ssd_act.of("decay"))
                ac.wait_ge(*ssd_pe.at(c, "tr"))
                if c:
                    ac.wait_ge(*ssd_pe.at(c - 1, "st"))
                ac.copy(btok[0:L, :], psC[0:L, 512:640]).then_inc(*ssd_act.of("btok"))
            for g in range(2):
                ac.wait_ge(*yg_dve.at(0, f"gate{g}"))
                ac.activation(sg[:, g, :], xb[:, g, 0:T], ACT.Square).then_inc(*yg_act.of(f"sq{g}"))
            for g in range(2):
                ac.wait_ge(yg_pe, g + 1)
                ac.activation(AB[g][:, 0:T], AB[g][:, 0:T], ACT.Ln, scale=1.0 / P, bias=col("eps")
                              ).then_inc(*yg_act.of(f"ln{g}"))
                ac.wait_ge(*yg_act.at(0, f"ln{g}"))
                ac.activation(AB[g][:, 0:T], AB[g][:, 0:T], ACT.Exp, scale=-0.5).then_inc(*yg_act.of(f"rs{g}"))
            for j in range(2):
                ac.wait_ge(dw_dve, DW * (j + 1))
                ac.activation(vc[:, j, 0:TP], AB[j][:, 0:TP], ACT.Identity, bias=col("dw_b", j))
                ac.activation(vc[:, j, TP:T], AB[j][:, TP + DW - 1:T + DW - 1], ACT.Identity, bias=col("dw_b", j)
                              ).then_inc(*cm_act.of(f"v{j}"))
            for j in range(2):
                ac.wait_ge(*cm_dve.at(0, f"cen{j}"))
                ac.activation(sg[:, j, :], vc[:, j, :], ACT.Square).then_inc(*cm_act.of(f"sq{j}"))
            ac.wait_ge(*cm_pe.at(0, "var"))
            ac.activation(psB[:, 0:T], psB[:, 0:T], ACT.Ln, scale=1.0 / 256, bias=col("eps")).then_inc(*cm_act.of("ln"))
            ac.wait_ge(*cm_act.at(0, "ln"))
            ac.activation(psB[:, 0:T], psB[:, 0:T], ACT.Exp, scale=-0.5).then_inc(*cm_act.of("rs"))
            for j in range(2):
                ac.wait_ge(*cm_dve.at(0, f"n{j}"))
                ac.activation(vc[:, j, :], vc[:, j, :], ACT.Silu, scale=col("ln_g", j), bias=col("ln_b", j)
                              ).then_inc(*cm_act.of(f"silu{j}"))
            for m in range(2):
                ac.wait_ge(*cm_pe.at(0, f"pw{m}"))
                ac.activation(mix[:, CA + m, :], AB[m][:, 0:T], ACT.Identity, bias=col("pw_b", m)
                              ).then_inc(*cm_act.of(f"out{m}"))

            def probs(r):
                i, h = ROUNDS[r]
                nq, nk = NTOK[i], sum(w for _, w in band(i)[1])
                ac.wait_ge(at_max, r + 1)
                if r >= 2:
                    ac.wait_ge(at_pt, r - 1)
                ac.activation(pr[r % 2][0:nq, 0:nk], sc[r % 2][0:nq, 0:nk], ACT.Exp, bias=nmx[0:nq, r:r + 1],
                              accum_out=rsum[0:nq, r:r + 1]).then_inc(at_exp, 1)

            def move_probs(r):
                i, h = ROUNDS[r]
                pair, hh = divmod(h, 2)
                nq, tiles = NTOK[i], band(i)[1]
                full = [w for _, w in tiles].count(P)
                ac.wait_ge(at_pt, r + 1)
                if r >= 2:
                    ac.wait_ge(at_pv, r - 1)
                last = ac.copy(pts[r % 2][:, 0:full * nq], psC[:, 0:full * nq])
                if full < len(tiles):
                    last = ac.copy(pts[r % 2][0:TS, full * nq:(full + 1) * nq], psC[0:TS, full * nq:(full + 1) * nq])
                last.then_inc(at_ptc, 1)
                ac.wait_ge(at_pv, r + 1)
                rows = slice(hh * 64, hh * 64 + 64)
                ac.copy(mix[rows, Q + pair, tok(i)], AB[r % 2][rows, 1024:1024 + nq]).then_inc(at_ovc, 1)

            probs(0)
            for r in range(len(ROUNDS)):
                if r + 1 < len(ROUNDS):
                    probs(r + 1)
                move_probs(r)
            ac.activation(s5p[:, DT, :], col("log_dt", 0, 8), ACT.Exp).then_inc(p5_act, 1)
            ac.wait_ge(p5_dve, P5["lrdt"])
            ac.activation(s5p[:, MAG, :], s5p[:, T0, :], ACT.Exp).then_inc(p5_act, 1)
            ac.wait_ge(p5_dve, P5["angles"])
            ac.activation(s5p[:, SIN, :], s5p[:, TH, :], ACT.Sin).then_inc(p5_act, 1)
            ac.activation(s5p[:, COS, :], s5p[:, T1, :], ACT.Sin).then_inc(p5_act, 1)
            ac.wait_ge(p5_pe, 1)
            for m in range(2):
                last = ac.copy(bbT[m].rearrange("p j n -> p (j n)"), psC[:, 2 * m * P:(2 * m + 2) * P])
            last.then_inc(p5_act, 1)
            for j in range(2):
                ac.wait_ge(s5_yd, NT)
                ac.activation(gel[:, j, :], gel[:, j, :], ACT.Gelu_apprx_tanh).then_inc(*glu_act.of(f"gelu{j}"))
            for j in range(2):
                ac.wait_ge(*glu_pe.at(0, f"gb{j}"))
                ac.activation(vc[:, j, :], AB[j][:, 0:T], ACT.Sigmoid, bias=col("glu_b", 2 + j)
                              ).then_inc(*glu_act.of(f"sig{j}"))
            for i in range(NT):
                M = NTOK[i]
                ac.wait_ge(*wo_dve.at(i, "add"))
                if i >= 2:
                    ac.wait_ge(tr_pe, i - 1)
                    ac.wait_ge(s_hst[i % 2], 16 * (i // 2))
                ac.activation(hn[i % 2][0:M, :], hres[0:M, i, :], ACT.Square, accum_out=ssum[0:M, i:i + 1]
                              ).then_inc(*wo_act.of("sq"))
                ac.wait_ge(*wo_act.at(i, "sq"))
                ac.activation(hrs[0:M, i:i + 1], ssum[0:M, i:i + 1], ACT.Ln, scale=1.0 / D, bias=col("eps")[0:M]
                              ).then_inc(*wo_act.of("ln"))
                ac.wait_ge(*wo_act.at(i, "ln"))
                ac.activation(hrs[0:M, i:i + 1], hrs[0:M, i:i + 1], ACT.Exp, scale=-0.5).then_inc(*wo_act.of("rs"))
                ac.wait_ge(tr_pe, i + 1)
                if i:
                    ac.wait_ge(lg_pe, i)
                ac.copy(hnT[:, :, 0:M], psC[:, :].rearrange("p (k n) -> p k n", k=KT)[:, :, 0:M]).then_inc(hte, 1)
                ac.wait_ge(lg_pe, i + 1)
                if i == 0:
                    ac.wait_ge(zeroed, 4)
                ac.copy(lgt[0:M, i, :], AB[i % 2][0:M, 1024:1060]).then_inc(lge, 1)
            ac.wait_ge(rt_dve, RT["d4"])
            ac.activation(prod[:, :, :, 0], d4, ACT.Exp).then_inc(rt_act, 1)
            ac.wait_ge(rt_dve, RT["dm"])
            ac.activation(gs, gs, ACT.Exp).then_inc(rt_act, 1)
            ac.wait_ge(rt_dve, RT["routed"])
            pairs = ac.value_load(npairs[0:1, :], min_val=0, max_val=BLOCKS // 2)
            with ac.Fori(0, BLOCKS // 2) as i:
                with ac.If(pairs > i):
                    for r in range(2):
                        ac.wait_ge(m_gu[r], i + 2)
                        ac.wait_ge(m_dn[r], i + 1)
                        ac.activation(actg[r], psA[:, 0:FF], ACT.Silu).then_inc(m_sil[r], 1)
                        ac.wait_ge(m_ht[r], i + 2)
                        ac.copy(actg[r], psA[:, 1024:1536]).then_inc(m_hte[r], 1)
                        ac.wait_ge(m_dn[r], i + 2)
                        ac.wait_ge(m_free[r], i + 1)
                        ac.copy(orow[r][:, 0:512], psB[:, 0:512]).then_inc(m_dnA[r], 1)
            ac.wait_ge(s_os[0], 16 * pairs)
            ac.wait_ge(s_os[1], 16 * pairs)

            def rows_back(i):
                if i >= 2:
                    ac.wait_ge(*f_dve.at(i - 2, "add2"))
                for k in range(2):
                    ac.dma_start(og[i % 2][k][0:NTOK[i], :], out_dram[k * T + i * P:k * T + i * P + NTOK[i], :]
                                 ).then_inc(s_og[i % 2], 16)

            rows_back(0)
            for i in range(NT):
                M = NTOK[i]
                if i + 1 < NT:
                    rows_back(i + 1)
                ac.wait_ge(*f_dve.at(i, "add2"))
                if i >= 2:
                    ac.wait_ge(*f_dve.at(i - 2, "y"))
                ac.activation(sqrow[i % 2][0:M, :], hres[0:M, i, :], ACT.Square, accum_out=ssum[0:M, i:i + 1]
                              ).then_inc(*f_act.of("sq"))
                ac.wait_ge(*f_act.at(i, "sq"))
                ac.activation(hrs[0:M, i:i + 1], ssum[0:M, i:i + 1], ACT.Ln, scale=1.0 / D, bias=col("eps")[0:M]
                              ).then_inc(*f_act.of("ln"))
                ac.wait_ge(*f_act.at(i, "ln"))
                ac.activation(hrs[0:M, i:i + 1], hrs[0:M, i:i + 1], ACT.Exp, scale=-0.5).then_inc(*f_act.of("rs"))

        @block.vector
        def _(ve):
            ve.wait_ge(s_params, 48)
            ve.wait_ge(nrm_act.sem, KT + 2)
            for k in range(KT):
                ve.scalar_tensor_tensor(out=xn[:, k, :], in0=xn[:, k, :], scalar=col("g_mix", k), in1=psB[:, 0:T],
                                        op0=ALU.mult, op1=ALU.mult).then_inc(xn_dve, 1)
            ve.wait_ge(zeroed, 3)
            for n in range(2):
                j = A0 + n
                ve.wait_ge(proj, j + 1)
                ve.wait_ge(ev, EV_AT[TILES.index(("g", n))])
                ve.tensor_tensor(vb[:, n, DW - 1:DW - 1 + TP], AB[j % 2][:, 0:TP], sg[:, n, 0:TP], ALU.mult)
                ve.tensor_tensor(vb[:, n, VBW - TS:VBW], AB[j % 2][:, TP:T], sg[:, n, TP:T], ALU.mult
                                 ).then_inc(gated, 1)
            ve.wait_ge(ev, len(EV_AT))
            ve.wait_ge(s_hist, 48)
            NC4 = T + CW - 1
            for j in range(4):
                acc = AB[j % 2][:, 0:NC4]
                if j >= 2:
                    ve.wait_ge(cv_act, j - 1)
                ve.tensor_scalar(acc, xb[:, j, 0:NC4], col("conv_w", 4 * j), None, ALU.mult
                                 ).then_inc(*cv_dve.of("t0"))
                for t in range(1, CW):
                    ve.wait_ge(*cv_dve.at(j, f"t{t - 1}"))
                    ve.scalar_tensor_tensor(out=acc, in0=xb[:, j, t:t + NC4], scalar=col("conv_w", 4 * j + t),
                                            in1=acc, op0=ALU.mult, op1=ALU.add).then_inc(*cv_dve.of(f"t{t}"))
            ve.wait_ge(vd_ev, NT)
            ve.tensor_tensor(dtr, dtr, bc(col("dt_bias", 0, 4), 1, NT), ALU.add).then_inc(*dtp_dve.of("raw"))
            ve.wait_ge(*dtp_dve.at(0, "raw"))
            ve.scalar_tensor_tensor(out=dta, in0=dtr, scalar=-1.0, in1=dtr, op0=ALU.mult, op1=ALU.max
                                    ).then_inc(*dtp_dve.of("abs"))
            ve.wait_ge(*dtp_act.at(0, "aexp"))
            ve.scalar_tensor_tensor(out=dtt, in0=dtr, scalar=0.0, in1=dta, op0=ALU.max, op1=ALU.add
                                    ).then_inc(*dtp_dve.of("dt"))
            ve.wait_ge(*dtp_dve.at(0, "dt"))
            ve.scalar_tensor_tensor(out=aa, in0=dtt, scalar=-1.0, in1=bc(aexp, 1, NT), op0=ALU.mult, op1=ALU.mult
                                    ).then_inc(*dtp_dve.of("a"))
            ve.wait_ge(dtp_pe, 1)
            ve.tensor_scalar(nacs.rearrange("p i h -> p (i h)"), psC[:, 0:36], -1.0, None, ALU.mult
                             ).then_inc(*dtp_dve.of("nacs"))
            ve.wait_ge(*dtp_dve.at(0, "nacs"))
            ve.tensor_tensor(dec.rearrange("p i h -> p (i h)"), psC[:, 512:548], nacs.rearrange("p i h -> p (i h)"),
                             ALU.add).then_inc(*dtp_dve.of("decin"))
            ve.wait_ge(cv_act, 4)
            for c in range(NT):
                L = NTOK[c]
                ve.wait_ge(*ssd_act.at(c, "ebc"))
                if c:
                    ve.wait_ge(*ssd_pe.at(c - 1, "y"))
                ve.tensor_tensor(dm[0:L, :, :], psA[0:L, 0:512].rearrange("p (h t) -> p h t", h=4),
                                 bc(negmask[0:L, :], 1, 4), ALU.add).then_inc(*ssd_dve.of("dm"))
                ve.wait_ge(*ssd_act.at(c, "decay"))
                ve.wait_ge(*ssd_pe.at(c, "cb"))
                ve.tensor_tensor(dm[0:L, 0:2, 0:L], dm[0:L, 0:2, 0:L], bc(psA[0:L, 512:512 + L], 1, 2), ALU.mult)
                ve.tensor_tensor(dm[0:L, 2:4, 0:L], dm[0:L, 2:4, 0:L], bc(psB[0:L, 0:L], 1, 2), ALU.mult
                                 ).then_inc(*ssd_dve.of("m"))
                ve.wait_ge(*ssd_pe.at(c, "tr"))
                if c:
                    ve.wait_ge(*ssd_pool.at(c - 1, "xdd"))
                if L < P:
                    ve.memset(xdt[L:P], 0.0)
                ve.tensor_tensor(xdt[0:L].rearrange("p (h d) -> p h d", h=4),
                                 psC[0:L, 0:256].rearrange("p (h d) -> p h d", h=4), bc(dtt[0:L, c, :], 2, 64),
                                 ALU.mult).then_inc(*ssd_dve.of("xdt"))
                ve.wait_ge(*ssd_act.at(c, "ebc"))
                for g in range(2):
                    rows = slice(g * 64, g * 64 + 64)
                    last = ve.tensor_tensor(ce[rows, 2 * g:2 * g + 2, 0:L], bc(xb[rows, 3, tok(c)], 1, 2),
                                            ebc[rows, 2 * g:2 * g + 2, 0:L], ALU.mult)
                last.then_inc(*ssd_dve.of("ce"))
                ve.wait_ge(*ssd_pe.at(c, "st"))
                st = state[1 if c == NT - 1 else 0]
                for h in range(HEADS):
                    g, hh = divmod(h, 2)
                    rows, cols = slice(g * 64, g * 64 + 64), slice(hh * 64, hh * 64 + 64)
                    new = psA[rows, 1024 + hh * 64:1024 + hh * 64 + 64]
                    if c == 0:
                        last = ve.tensor_copy(st[rows, cols], new)
                    else:
                        last = ve.scalar_tensor_tensor(out=st[rows, cols], in0=st[rows, cols],
                                                       scalar=etot[rows, c, h:h + 1], in1=new,
                                                       op0=ALU.mult, op1=ALU.add)
                last.then_inc(*ssd_dve.of("state"))
                for g in range(2):
                    last = ve.scalar_tensor_tensor(out=xb[:, g, tok(c)], in0=xb[:, g, tok(c)],
                                                   scalar=col("ssd_d", g), in1=psB[:, 512 * (1 + g):512 * (1 + g) + L],
                                                   op0=ALU.mult, op1=ALU.add)
                last.then_inc(*ssd_dve.of("yd"))
            ve.wait_ge(*ssd_dve.at(NT - 1, "yd"))
            for g in range(2):
                ve.tensor_tensor(xb[:, g, 0:T], xb[:, g, 0:T], mix[:, Z + g, :], ALU.mult).then_inc(*yg_dve.of(f"gate{g}"))
            for g in range(2):
                ve.wait_ge(*yg_act.at(0, f"rs{g}"))
                last = ve.scalar_tensor_tensor(out=mix[:, Z + g, :], in0=xb[:, g, 0:T], scalar=col("norm_w", g),
                                               in1=AB[g][:, 0:T], op0=ALU.mult, op1=ALU.mult)
            last.then_inc(*yg_dve.of("norm"))
            ve.wait_ge(*yg_dve.at(0, "norm"))
            NCD = T + DW - 1
            for j in range(2):
                acc = AB[j][:, 0:NCD]
                ve.tensor_scalar(acc, vb[:, j, 0:NCD], col("dw_w", DW * j), None, ALU.mult).then_inc(dw_dve, 1)
                for t in range(1, DW):
                    ve.wait_ge(dw_dve, DW * j + t)
                    ve.scalar_tensor_tensor(out=acc, in0=vb[:, j, t:t + NCD], scalar=col("dw_w", DW * j + t),
                                            in1=acc, op0=ALU.mult, op1=ALU.add).then_inc(dw_dve, 1)
            ve.wait_ge(*cm_pe.at(0, "mu"))
            for j in range(2):
                ve.scalar_tensor_tensor(out=vc[:, j, :], in0=psA[:, 0:T], scalar=-1.0 / 256, in1=vc[:, j, :],
                                        op0=ALU.mult, op1=ALU.add).then_inc(*cm_dve.of(f"cen{j}"))
            ve.wait_ge(*cm_act.at(0, "rs"))
            for j in range(2):
                ve.tensor_tensor(vc[:, j, :], vc[:, j, :], psB[:, 0:T], ALU.mult).then_inc(*cm_dve.of(f"n{j}"))

            def biased(r):
                i, h = ROUNDS[r]
                _, tiles, b0 = band(i)
                nq, nk = NTOK[i], sum(w for _, w in tiles)
                ve.wait_ge(at_s, r + 1)
                if r >= 2:
                    ve.wait_ge(at_exp, r - 1)
                ve.scalar_tensor_tensor(out=sc[r % 2][0:nq, 0:nk], in0=AB[r % 2][0:nq, 0:nk], scalar=ATT_SCALE,
                                        in1=bias[0:nq, h, b0:b0 + nk], op0=ALU.mult, op1=ALU.add).then_inc(at_add, 1)
                ve.wait_ge(at_add, r + 1)
                ve.tensor_reduce(nmx[0:nq, r:r + 1], sc[r % 2][0:nq, 0:nk], AX.X, ALU.max, negate=True
                                 ).then_inc(at_max, 1)

            def diagonal(r):
                nq = NTOK[ROUNDS[r][0]]
                ve.wait_ge(at_exp, r + 1)
                ve.reciprocal(rinv[0:nq, r:r + 1], rsum[0:nq, r:r + 1]).then_inc(at_rinv, 1)
                ve.wait_ge(at_rinv, r + 1)
                if r >= 2:
                    ve.wait_ge(at_pt, r - 1)
                ve.tensor_scalar(diag[r % 2][0:nq, 0:nq], ident[0:nq, 0:nq], rinv[0:nq, r:r + 1], None, ALU.mult
                                 ).then_inc(at_diag, 1)

            ve.wait_ge(s_bias, 16)
            ve.wait_ge(*cm_pe.at(0, "pw1"))
            biased(0)
            for r in range(len(ROUNDS)):
                if r + 1 < len(ROUNDS):
                    biased(r + 1)
                diagonal(r)
            n5 = [0]

            def link5(ins, name=None):
                ins.then_inc(p5_dve, 1)
                n5[0] += 1
                assert name is None or P5[name] == n5[0], (name, n5[0])
                ve.wait_ge(p5_dve, n5[0])

            def c5(n):
                return s5p[:, n, :]
            lre, lim = col("lam_re", 0, 8), col("lam_im", 0, 8)
            ve.wait_ge(s_s5w, 32)
            ve.wait_ge(p5_act, 1)
            link5(ve.tensor_tensor(c5(T0), lre, c5(DT), ALU.mult), "lrdt")
            link5(ve.tensor_tensor(c5(TH), lim, c5(DT), ALU.mult))
            link5(ve.tensor_scalar(c5(T1), c5(TH), 1.0 / (2 * math.pi), 12582912.0, ALU.mult, ALU.add))
            link5(ve.tensor_scalar(c5(T1), c5(T1), -12582912.0, None, ALU.add))
            link5(ve.scalar_tensor_tensor(out=c5(TH), in0=c5(T1), scalar=-6.28125, in1=c5(TH), op0=ALU.mult,
                                          op1=ALU.add))
            link5(ve.scalar_tensor_tensor(out=c5(TH), in0=c5(T1), scalar=-(2 * math.pi - 6.28125), in1=c5(TH),
                                          op0=ALU.mult, op1=ALU.add))
            link5(ve.tensor_scalar(c5(TH), c5(TH), 3.141592, -3.141592, ALU.min, ALU.max))
            link5(ve.scalar_tensor_tensor(out=c5(T1), in0=c5(TH), scalar=-1.0, in1=c5(TH), op0=ALU.mult, op1=ALU.max))
            link5(ve.tensor_scalar(c5(T1), c5(T1), -1.0, math.pi / 2, ALU.mult, ALU.add), "angles")
            ve.wait_ge(p5_act, 4)
            link5(ve.tensor_tensor(c5(AR), c5(MAG), c5(COS), ALU.mult))
            link5(ve.tensor_tensor(c5(AI), c5(MAG), c5(SIN), ALU.mult))
            link5(ve.tensor_tensor(c5(T0), lre, lre, ALU.mult))
            link5(ve.tensor_tensor(c5(T1), lim, lim, ALU.mult))
            link5(ve.tensor_tensor(c5(T0), c5(T0), c5(T1), ALU.add))
            link5(ve.reciprocal(c5(T2), c5(T0)))
            link5(ve.scalar_tensor_tensor(out=c5(T0), in0=c5(AR), scalar=-1.0, in1=lre, op0=ALU.add, op1=ALU.mult))
            link5(ve.tensor_tensor(c5(T1), c5(AI), lim, ALU.mult))
            link5(ve.tensor_tensor(c5(T0), c5(T0), c5(T1), ALU.add))
            link5(ve.tensor_tensor(c5(CR), c5(T0), c5(T2), ALU.mult))
            link5(ve.scalar_tensor_tensor(out=c5(T0), in0=c5(AR), scalar=-1.0, in1=lim, op0=ALU.add, op1=ALU.mult))
            link5(ve.tensor_tensor(c5(T1), c5(AI), lre, ALU.mult))
            link5(ve.tensor_tensor(c5(T1), c5(T1), c5(T0), ALU.subtract))
            link5(ve.tensor_tensor(c5(CI), c5(T1), c5(T2), ALU.mult))
            ve.wait_ge(proj, len(TILES))
            for m in range(2):
                link5(ve.memset(bb[m], 0.0))
                link5(ve.memset(cc[m], 0.0))
            t5 = [s5t[m].rearrange("p s t -> p (s t)")[:, 0:ST * 16].rearrange("p (s c) -> p s c", s=ST)
                  for m in range(2)]
            for m, op in ((0, ALU.subtract), (1, ALU.add)):
                link5(ve.tensor_tensor(t5[0], s5w[:, m, :, :], bc(c5(CR), 2, 16), ALU.mult))
                link5(ve.tensor_tensor(t5[1], s5w[:, 1 - m, :, :], bc(c5(CI), 2, 16), ALU.mult))
                for g in range(2):
                    rows = slice(g * 64, g * 64 + 64)
                    link5(ve.tensor_tensor(bb[m][rows, :, g * 16:g * 16 + 16], t5[0][rows], t5[1][rows], op))
            for m, sgn in ((0, 1.0), (1, -1.0)):
                for g in range(2):
                    rows = slice(g * 64, g * 64 + 64)
                    link5(ve.tensor_scalar(cc[m][rows, :, g * 16:g * 16 + 16], s5w[rows, 2 + m, :, :], sgn, None,
                                           ALU.mult), "bb" if m + g == 2 else None)
            link5(ve.tensor_copy(cosT[:, :, 0:1], c5(COS).unsqueeze(2)))
            link5(ve.tensor_copy(sinT[:, :, 0:1], c5(SIN).unsqueeze(2)))
            k = 1
            while k < P:
                cl = cosT[:, :, k - 1:k].broadcast_to([P, ST, k])
                sl = sinT[:, :, k - 1:k].broadcast_to([P, ST, k])
                lo, hi = slice(0, k), slice(k, 2 * k)
                link5(ve.tensor_tensor(s5t[0][:, :, lo], cosT[:, :, lo], cl, ALU.mult))
                link5(ve.tensor_tensor(s5t[1][:, :, lo], sinT[:, :, lo], sl, ALU.mult))
                link5(ve.tensor_tensor(cosT[:, :, hi], s5t[0][:, :, lo], s5t[1][:, :, lo], ALU.subtract))
                link5(ve.tensor_tensor(s5t[0][:, :, lo], cosT[:, :, lo], sl, ALU.mult))
                link5(ve.tensor_tensor(s5t[1][:, :, lo], sinT[:, :, lo], cl, ALU.mult))
                link5(ve.tensor_tensor(sinT[:, :, hi], s5t[0][:, :, lo], s5t[1][:, :, lo], ALU.add),
                      "tables" if k == 64 else None)
                k *= 2

            def views(x, half, L):
                return x.rearrange("p (j q) t -> p q j t", j=2)[:, 2 * half:2 * half + 2, :, 0:L]

            def s5_result(c):
                L = NTOK[c]
                ve.wait_ge(s5_y, c + 1)
                for jt in range(2):
                    last = ve.scalar_tensor_tensor(out=gel[:, jt, tok(c)], in0=mix[:, UD + jt, tok(c)],
                                                   scalar=col("s5_d", jt), in1=psC[:, 512 * jt:512 * jt + L],
                                                   op0=ALU.mult, op1=ALU.add)
                last.then_inc(s5_yd, 1)

            def s5_input(c, half, m):
                x = AB[half][:, 0:1024].rearrange("p (q j m t) -> p q j m t", q=2, j=2, m=2)
                return x[:, :, :, m, 0:NTOK[c]]
            ve.wait_ge(p5_act, P5A["bbT"])
            for c in range(NT):
                L = NTOK[c]
                ve.wait_ge(s5_x, c + 1)
                for half in range(2):
                    ve.tensor_tensor(views(s5t[0], half, L), s5_input(c, half, 0), views(cosT, half, L), ALU.mult)
                    last = ve.tensor_tensor(views(s5t[1], half, L), s5_input(c, half, 1), views(sinT, half, L), ALU.mult)
                last.then_inc(*s5_dve.of("p0"))
                ve.wait_ge(*s5_dve.at(c, "p0"))
                ve.tensor_tensor(s5u[0][:, :, 0:L], s5t[0][:, :, 0:L], s5t[1][:, :, 0:L], ALU.add
                                 ).then_inc(*s5_dve.of("u0"))
                ve.wait_ge(*s5_dve.at(c, "u0"))
                for half in range(2):
                    ve.tensor_tensor(views(s5t[0], half, L), s5_input(c, half, 1), views(cosT, half, L), ALU.mult)
                    last = ve.tensor_tensor(views(s5t[1], half, L), s5_input(c, half, 0), views(sinT, half, L), ALU.mult)
                last.then_inc(*s5_dve.of("p1"))
                ve.wait_ge(*s5_dve.at(c, "p1"))
                ve.tensor_tensor(s5u[1][:, :, 0:L], s5t[0][:, :, 0:L], s5t[1][:, :, 0:L], ALU.subtract
                                 ).then_inc(*s5_dve.of("u1"))
                ve.wait_ge(*s5_dve.at(c, "u1"))
                if c:
                    ve.wait_ge(*s5_pool.at(c - 1, "im"))
                r = 1 if c == NT - 1 else 0
                for s in range(ST):
                    for m in range(2):
                        if c == 0:
                            init = 0.0
                        elif c == NT - 1:
                            init = col("h0_re" if m == 0 else "h0_im", s)
                        else:
                            init = s5end[:, 0, m, s:s + 1]
                        last = ve.tensor_tensor_scan(s5g[m][:, s, 0:L], s5p[:, MAG, s:s + 1].broadcast_to([P, L]),
                                                     s5u[m][:, s, 0:L], init, ALU.mult, ALU.add)
                last.then_inc(*s5_dve.of("scan"))
                ve.wait_ge(*s5_dve.at(c, "scan"))
                ce_, se_ = cosT[:, :, L - 1], sinT[:, :, L - 1]
                gr, gi = s5g[0][:, :, L - 1], s5g[1][:, :, L - 1]
                for x, (p0, p1) in enumerate(((gr, ce_), (gi, se_), (gr, se_), (gi, ce_))):
                    last = ve.tensor_tensor(cmul[:, x, :], p0, p1, ALU.mult)
                last.then_inc(*s5_dve.of("carry"))
                ve.wait_ge(*s5_dve.at(c, "carry"))
                ve.tensor_tensor(s5end[:, r, 0, :], cmul[:, 0, :], cmul[:, 1, :], ALU.subtract)
                ve.tensor_tensor(s5end[:, r, 1, :], cmul[:, 2, :], cmul[:, 3, :], ALU.add).then_inc(*s5_dve.of("end"))
                ve.wait_ge(*s5_dve.at(c, "end"))
                if c:
                    s5_result(c - 1)
            s5_result(NT - 1)
            for m in range(2):
                ve.wait_ge(*glu_pe.at(0, f"ga{m}"))
                ve.scalar_tensor_tensor(out=mix[:, UD + m, :], in0=AB[m][:, 0:T], scalar=col("glu_b", m),
                                        in1=vc[:, m, :], op0=ALU.add, op1=ALU.mult).then_inc(glu_dve, 1)
            for i in range(NT):
                M = NTOK[i]
                if i == 0:
                    ve.wait_ge(s_out, 16 * 10)
                    ve.wait_ge(s_gffn, 32)
                ve.wait_ge(wo_pe, i + 1)
                ve.wait_ge(s_xtok[i % 2], 16 * (i // 2 + 1))
                ve.tensor_tensor(hres[0:M, i, :], AB[i % 2][0:M, 0:D], xtok[i % 2][0:M, :], ALU.add
                                 ).then_inc(*wo_dve.of("add"))
                ve.wait_ge(*wo_act.at(i, "rs"))
                ve.scalar_tensor_tensor(out=hn[i % 2][0:M, :], in0=hres[0:M, i, :], scalar=hrs[0:M, i:i + 1],
                                        in1=gffn[0:M, :], op0=ALU.mult, op1=ALU.mult).then_inc(*wo_dve.of("hn"))
            nr = [0]

            def linkr(ins, name=None):
                ins.then_inc(rt_dve, 1)
                nr[0] += 1
                assert name is None or RT[name] == nr[0], (name, nr[0])
                ve.wait_ge(rt_dve, nr[0])

            def first(onehot, marks, order, best, n):
                linkr(ve.tensor_tensor(marks, marks, bc(order, 1, NT), ALU.mult))
                linkr(ve.tensor_reduce(best, marks, AX.X, ALU.max))
                linkr(ve.tensor_tensor(onehot, marks, bc(best, 2, n), ALU.is_equal))

            ve.wait_ge(lge, NT)
            l4 = lgt[:, :, 0:G]
            l32 = lgt[:, :, G:G + E].rearrange("p i (g e) -> p i g e", g=G)
            linkr(ve.tensor_reduce(m4, l4, AX.X, ALU.max))
            linkr(ve.tensor_tensor(d4, l4, bc(m4, 2, G), ALU.subtract), "d4")
            linkr(ve.tensor_scalar(ohg, d4, 0.0, None, ALU.is_ge))
            first(ohg, ohg, col("order4", 0, G), mm, G)
            ve.wait_ge(rt_act, 1)
            linkr(ve.tensor_reduce(pgr, prod[:, :, :, 0], AX.X, ALU.add))
            linkr(ve.reciprocal(pgr, pgr))
            linkr(ve.tensor_tensor(prod, l32, bc(ohg, 3, EPG), ALU.mult))
            linkr(ve.tensor_reduce(les, prod.rearrange("p i g e -> p i e g"), AX.X, ALU.add))
            linkr(ve.tensor_reduce(m1, les, AX.X, ALU.max))
            linkr(ve.tensor_tensor(t8, les, bc(m1, 2, EPG), ALU.is_ge))
            first(oh[0], t8, col("order8", 0, EPG), mm, EPG)
            linkr(ve.scalar_tensor_tensor(out=les, in0=oh[0], scalar=NEG, in1=les, op0=ALU.mult, op1=ALU.add))
            linkr(ve.tensor_reduce(m2, les, AX.X, ALU.max))
            linkr(ve.tensor_tensor(t8, les, bc(m2, 2, EPG), ALU.is_ge))
            first(oh[1], t8, col("order8", 0, EPG), mm, EPG)
            linkr(ve.tensor_tensor(gs, m2, m1, ALU.subtract), "dm")
            for k in range(2):
                linkr(ve.tensor_tensor(oe[k], bc(ohg, 3, EPG), bc(oh[k], 2, G), ALU.mult))
            linkr(ve.memset(oe[0][TS:P, NT - 1], 0.0))
            linkr(ve.memset(oe[1][TS:P, NT - 1], 0.0))
            flat = [x.rearrange("p i g e -> p i (g e)") for x in oe]
            linkr(ve.tensor_tensor(asg, flat[0], flat[1], ALU.add))
            linkr(ve.memset(pre[:, 0, :], 0.0))
            for i in range(NT):
                linkr(ve.tensor_tensor(pre[:, i + 1, :], pre[:, i, :], asg[:, i, :], ALU.add),
                      "pre" if i == NT - 1 else None)
            ve.wait_ge(rt_act, 2)
            linkr(ve.tensor_scalar(m1, gs, 1.0, None, ALU.add))
            linkr(ve.reciprocal(m1, m1))
            linkr(ve.tensor_tensor(gate[0], m1, pgr, ALU.mult))
            linkr(ve.tensor_tensor(gate[1], gate[0], gs, ALU.mult))
            ve.wait_ge(rt_pe, 1)
            c3 = cmp[:, 0:E * THR].rearrange("p (e n) -> p e n", n=THR)
            linkr(ve.tensor_tensor(c3, bc(psB[:, 0:E], 2, THR), bc(col("thr", 0, THR), 1, E), ALU.is_gt))
            linkr(ve.tensor_reduce(nblk, c3, AX.X, ALU.add))
            linkr(ve.tensor_tensor_scan(bend, ones[:, 0:E], nblk, 0.0, ALU.mult, ALU.add))
            linkr(ve.tensor_tensor(base, bend, nblk, ALU.subtract))
            linkr(ve.tensor_scalar(base, base, float(P), -1.0, ALU.mult, ALU.add))
            linkr(ve.tensor_tensor(dmap, psA[:, 0:NT * E].rearrange("p (i e) -> p i e", e=E), bc(base, 1, NT),
                                   ALU.add))
            for k in range(2):
                linkr(ve.tensor_tensor(prod.rearrange("p i g e -> p i (g e)"), flat[k], dmap, ALU.mult))
                linkr(ve.tensor_reduce(destf[:, k, :], prod.rearrange("p i g e -> p i (g e)"), AX.X, ALU.add))
            linkr(ve.tensor_copy(dest, destf), "dest")
            c2 = cmp[0:1, :].rearrange("p (b e) -> p b e", e=E)
            linkr(ve.tensor_tensor(c2, bc(bend[0:1, :], 1, BLOCKS), bc(col("iota", 0, BLOCKS)[0:1, :], 2, E), ALU.is_le))
            linkr(ve.tensor_reduce(eidf[0:1, :], c2, AX.X, ALU.add))
            linkr(ve.tensor_scalar(eidf[0:1, :], eidf[0:1, :], float(E - 1), None, ALU.min))
            linkr(ve.tensor_copy(eid[0:1, :], eidf[0:1, :]))
            even = col("iota", 0, BLOCKS)[0:1, :].rearrange("p (i two) -> p i two", two=2)[:, :, 0]
            linkr(ve.tensor_tensor(slotf[0:1, 0:BLOCKS // 2], even,
                                   bend[0:1, E - 1:E].broadcast_to([1, BLOCKS // 2]), ALU.is_lt))
            linkr(ve.tensor_reduce(slotf[0:1, BLOCKS:BLOCKS + 1], slotf[0:1, 0:BLOCKS // 2], AX.X, ALU.add))
            linkr(ve.tensor_copy(npairs[0:1, :], slotf[0:1, BLOCKS:BLOCKS + 1]), "routed")
            ve.wait_ge(s_slotin, 16)
            linkr(ve.tensor_copy(slotf[0:BLOCKS + 1, :], slots_rows[0:BLOCKS + 1, :]), "slotf")
            ve.wait_ge(rt_pe, 2)
            linkr(ve.tensor_copy(slotc, psC[:, 0:BLOCKS + 1]))
            linkr(ve.tensor_scalar(slotm, slotc, float(T), float(-T), ALU.is_ge, ALU.mult))
            linkr(ve.tensor_tensor(slotm, slotm, slotc, ALU.add))
            ve.tensor_copy(slot_out, slotc)
            ve.tensor_copy(slot_in, slotm).then_inc(slots_ready, 1)
            ve.wait_ge(slots_ready, 1)

            def rows_moved(b, n):
                ve.wait_ge(m_xt[b], n + 1)
                ve.tensor_copy(xgT[b].rearrange("p k n -> p (k n)"), psC[:, :]).then_inc(m_xte[b], 1)

            rows_moved(0, 1)
            pairs = ve.value_load(npairs[0:1, :], min_val=0, max_val=BLOCKS // 2)
            with ve.Fori(0, BLOCKS // 2) as i:
                with ve.If(pairs > i):
                    for r in range(2):
                        rows_moved(1 - r, i + 1 + r)
                        ve.wait_ge(m_sil[r], i + 2)
                        ve.wait_ge(m_ht[r], i + 1)
                        ve.tensor_tensor(hmid[r], psA[:, 512:1024], actg[r], ALU.mult).then_inc(m_hm[r], 1)
                        ve.wait_ge(m_dn[r], i + 2)
                        ve.wait_ge(m_free[r], i + 1)
                        ve.tensor_copy(orow[r][:, 512:1024], psB[:, 512:1024]).then_inc(m_dnD[r], 1)
            ve.wait_ge(s_gfin, 16)
            for i in range(NT):
                M = NTOK[i]
                ve.wait_ge(s_og[i % 2], 32 * (i // 2 + 1))
                for k in range(2):
                    ve.scalar_tensor_tensor(out=hres[0:M, i, :], in0=og[i % 2][k][0:M, :], scalar=gate[k][0:M, i:i + 1],
                                            in1=hres[0:M, i, :], op0=ALU.mult, op1=ALU.add
                                            ).then_inc(*f_dve.of(f"add{k + 1}"))
                    ve.wait_ge(*f_dve.at(i, f"add{k + 1}"))
                ve.wait_ge(*f_act.at(i, "rs"))
                if i >= 2:
                    ve.wait_ge(s_yo[i % 2], 16 * (i // 2))
                ve.scalar_tensor_tensor(out=yrow[i % 2][0:M, :], in0=hres[0:M, i, :], scalar=hrs[0:M, i:i + 1],
                                        in1=gfin[0:M, :], op0=ALU.mult, op1=ALU.mult).then_inc(*f_dve.of("y"))

        @block.gpsimd
        def _(po):
            for x in (m_xt, m_xte, m_gu, m_sil, m_hm, m_ht, m_hte, m_dn, m_dnA, m_dnD, m_free):
                for k in range(2):
                    po.sem_inc(x[k], 1)
            po.memset(xb[:, :, 0:CW - 1], 0.0).then_inc(zeroed, 1)
            po.memset(vb[:, :, 0:DW - 1], 0.0).then_inc(zeroed, 1)
            po.memset(dtr, 0.0).then_inc(zeroed, 1)
            po.wait_ge(ev, 4)
            po.wait_ge(s_hist, 48)
            po.tensor_copy(tail[:, :, 0, :], xb[:, :, TP:TP + CW - 1])
            po.tensor_copy(tail[:, :, 1, :], xb[:, :, XBW - (CW - 1):XBW]).then_inc(tailed, 1)
            po.wait_ge(s_params, 48)
            po.wait_ge(*dtp_act.at(0, "etot"))
            po.wait_ge(*dtp_dve.at(0, "a"))
            for c in range(NT):
                L = NTOK[c]
                if c:
                    po.wait_ge(*ssd_pe.at(c - 1, "bc"))
                po.tensor_tensor(ua[0:L], bc(upper[0:L, :], 1, 4), bc(aa[0:L, c, :], 2, P), ALU.mult
                                 ).then_inc(*ssd_pool.of("ua"))
                po.wait_ge(*ssd_dve.at(c, "xdt"))
                if c:
                    po.wait_ge(*ssd_pe.at(c - 1, "st"))
                po.tensor_tensor(xdd[0:L].rearrange("p (h d) -> p h d", h=4),
                                 xdt[0:L].rearrange("p (h d) -> p h d", h=4), bc(dec[0:L, c, :], 2, 64), ALU.mult
                                 ).then_inc(*ssd_pool.of("xdd"))
            po.wait_ge(p5_dve, P5["tables"])
            for c in range(NT):
                L = NTOK[c]
                po.wait_ge(*s5_dve.at(c, "scan"))
                if c:
                    po.wait_ge(s5_y, c)
                x = [t[:, :, 0:L] for t in (s5g[0], s5g[1], cosT, sinT, s5v[0], s5v[1], s5h[0], s5h[1])]
                po.tensor_tensor(x[4], x[0], x[2], ALU.mult)
                po.tensor_tensor(x[5], x[1], x[3], ALU.mult).then_inc(*s5_pool.of("m0"))
                po.wait_ge(*s5_pool.at(c, "m0"))
                po.tensor_tensor(x[6], x[4], x[5], ALU.subtract).then_inc(*s5_pool.of("re"))
                po.wait_ge(*s5_pool.at(c, "re"))
                po.tensor_tensor(x[4], x[0], x[3], ALU.mult)
                po.tensor_tensor(x[5], x[1], x[2], ALU.mult).then_inc(*s5_pool.of("m1"))
                po.wait_ge(*s5_pool.at(c, "m1"))
                po.tensor_tensor(x[7], x[4], x[5], ALU.add).then_inc(*s5_pool.of("im"))
            po.wait_ge(*s5_pool.at(NT - 1, "im"))
            po.wait_ge(*s5_dve.at(NT - 1, "end"))
            po.memset(lgt[:, NT - 1, :], 0.0).then_inc(zeroed, 1)
            po.memset(curidx[0], 0).then_inc(rt_pool, 1)
            po.iota(slots_rows[0:BLOCKS + 1, :], [[1, P]], base=2 * T, channel_multiplier=0).then_inc(rt_pool, 1)
            po.wait_ge(rt_pool, 2)
            po.dma_start(slot_dram.rearrange("(b p) o -> b (p o)", p=P), slots_rows[0:BLOCKS + 1, :]).then_inc(s_slotz, 16)
            po.wait_ge(rt_dve, RT["dest"])
            po.wait_ge(s_slotz, 16)
            for k in range(2):
                for i in range(NT):
                    M = NTOK[i]
                    po.indirect_dma_start(slot_dram, bass.IndirectOffsetOnAxis(ap=dest[0:M, k, i:i + 1], axis=0),
                                          asgid[0:M, k, i:i + 1], None).then_inc(s_scat, 16)
            po.wait_ge(s_scat, 16 * 2 * NT)
            po.dma_start(slots_rows[0:BLOCKS + 1, :], slot_dram.rearrange("(b p) o -> b (p o)", p=P)).then_inc(s_slotin, 16)
            po.wait_ge(slots_ready, 1)
            po.wait_ge(s_hst[0], 16 * 5)
            po.wait_ge(s_hst[1], 16 * 4)

            last_in, last_out = po.to_reg(T - 1), po.to_reg(2 * T - 1)

            def gather(b, n, blk):
                po.wait_ge(m_xt[b], n + 1)
                po.tensor_copy(curidx[b], slot_in[:, blk:blk + 1] if isinstance(blk, int) else slot_in[:, ds(blk, 1)]
                               ).then_inc(idxc, 1)
                po.wait_ge(idxc, 1 if isinstance(blk, int) else blk + 1)
                po.sem_inc(indirect_go, 1)
                po.indirect_dma_start(xg[b], None, hn_dram, bass.IndirectOffsetOnAxis(ap=curidx[b], axis=0),
                                      bounds_check=last_in, oob_is_err=False).then_inc(s_xg[b], 16)

            gather(0, 0, 0)
            pairs = po.value_load(npairs[0:1, :], min_val=0, max_val=BLOCKS // 2)
            with po.Fori(0, BLOCKS // 2) as i:
                with po.If(pairs > i):
                    for r in range(2):
                        gather(1 - r, i + r, 2 * i + r + 1)
                        po.wait_ge(m_dnA[r], i + 2)
                        po.wait_ge(m_dnD[r], i + 2)
                        po.tensor_copy(curout[r], slot_out[:, ds(2 * i + r, 1)]).then_inc(outc, 1)
                        po.wait_ge(outc, 2 * i + r + 1)
                        po.sem_inc(indirect_go, 1)
                        po.indirect_dma_start(out_dram, bass.IndirectOffsetOnAxis(ap=curout[r], axis=0), orow[r], None,
                                              bounds_check=last_out, oob_is_err=False).then_inc(s_os[r], 16)
                    for r in range(2):
                        po.wait_ge(s_os[r], 16 * i + 16)
                        po.sem_inc(m_free[r], 1)


_OUTS = {"y_p": (TP, D), "y_s": (TS, D), "ssd_p": (P, P), "ssd_s": (P, P), "ssd_tail": (P, 24),
         "ccm_p": (P, 2, DW - 1), "ccm_s": (P, 2, DW - 1), "k_p": (P, 2, WIN), "k_s": (P, 2, TS),
         "v_p": (P, 4, 256), "v_s": (TS, 256), "s5_end": (P, 4 * ST)}


def _pack(x):
    import numpy as np

    x = {n: np.asarray(v) for n, v in x.items()}

    def chan(v, n):
        return np.moveaxis(v.reshape((n, P) + v.shape[1:]), 0, 1)

    def states(v):
        return np.moveaxis(v.reshape((ST, P) + v.shape[2:]), 0, 1)

    def every(v):
        return np.broadcast_to(v.reshape(1, -1), (P, v.size))
    w_in = x["w_in"][0]
    at = {"z": 0, "xbc": 256, "a": 772, "g": 1028, "q": 1284, "k": 1540, "ud": 2052}
    order = [("xbc", j) for j in range(4)] + [(n, j) for n in ("k", "g", "a", "q", "z", "ud") for j in range(2)]
    f = np.float32
    parts = {
        "g_mix": chan(x["g_mix"][0], 8), "conv_w": chan(x["ssd_conv_w"][0].T, 4), "conv_b": chan(x["ssd_conv_b"][0], 4),
        "dw_w": chan(x["ccm_dw_w"][0].T, 2), "dw_b": chan(x["ccm_dw_b"][0], 2), "ln_g": chan(x["ccm_ln_g"][0], 2),
        "ln_b": chan(x["ccm_ln_b"][0], 2), "pw_b": chan(x["ccm_pw_b"][0], 2),
        "ssd_d": chan(np.repeat(x["ssd_d"][0], HD), 2), "norm_w": chan(x["ssd_norm_w"][0], 2),
        "glu_b": chan(x["s5_glu_b"][0], 4), "lam_re": states(x["s5_lam_re"][0]), "lam_im": states(x["s5_lam_im"][0]),
        "log_dt": states(np.repeat(x["s5_log_dt"][0][:, None], 64, 1)), "h0_re": states(x["state_s5_re"][0, 0]),
        "h0_im": states(x["state_s5_im"][0, 0]), "s5_d": chan(x["s5_d"][0].reshape(256), 2),
        "dt_bias": every(x["ssd_dt_bias"][0]), "a_log": every(x["ssd_a_log"][0]),
        "eps": np.full((P, 1), EPS, f), "one": np.ones((P, 1), f),
        "thr": every(np.arange(THR, dtype=f) * P), "iota": every(np.arange(BLOCKS, dtype=f)),
        "order4": every(np.arange(G, 0, -1).astype(f)), "order8": every(np.arange(EPG, 0, -1).astype(f)),
    }
    j, t = np.arange(P)[:, None], np.arange(P)[None, :]
    mats = np.concatenate([np.eye(P, dtype=f), np.ones((P, P), f), (j <= t).astype(f),
                           np.where(j > t, f(NEG), f(0))], axis=1)
    q, c = np.arange(P)[:, None], np.arange(BANDW)[None, :]
    seen = (c // 64 <= q // 64 + 8) & (c // 64 >= q // 64)
    idx = np.where(seen, np.clip(WIN + q - c, -128, 128) + 128, 257)
    table = np.concatenate([x["att_rel_bias"][0], np.full((HEADS, 1), NEG, f)], axis=1)
    s5w = [states(x[n][0]) for n in ("s5_b_re", "s5_b_im")] + \
          [states(np.moveaxis(x[n][0], 1, 2)) for n in ("s5_c_re", "s5_c_im")]
    rows = np.concatenate([x["x_prompt"][0], x["x_sample"][0]], axis=0)
    return {
        "params": np.concatenate([parts[n].reshape(P, w) for n, w in FIELDS], axis=1),
        "mats": mats, 
        "asgid": (np.arange(2)[None, :, None] * T + np.arange(NT)[None, None, :] * P + j[:, :, None]).astype(np.int32),
        "xT": rows.T, "x_rows": rows,
        "w_cm": np.stack([np.moveaxis(w_in[:, at[n] + i * P:at[n] + (i + 1) * P].reshape(KT, P, P), 0, 1).reshape(P, D)
                          for n, i in order]),
        "w_vd": chan(np.concatenate([w_in[:, 1796:2052], w_in[:, 768:772]], axis=1), KT),
        "ssd_hist": chan(x["state_ssd_conv"][0, 0].T, 4), "ccm_hist": chan(x["state_ccm_conv"][0, 0].T, 2),
        "ssd_h0": x["state_ssd"][0, 0].reshape(2, 2, HD, 64).transpose(0, 3, 1, 2).reshape(P, P),
        "k_cache": chan(x["cache_att_k"][0, 0].reshape(WIN, 256).T, 2),
        "v_cache": chan(x["cache_att_v"][0, 0].reshape(WIN, 256), 4),
        "bias": np.moveaxis(table[:, idx], 0, 1), "pw_w": chan(x["ccm_pw_w"][0], 2),
        "s5_w": np.stack(s5w, axis=1).reshape(P, -1), "glu_w": chan(x["s5_glu_w"][0], 2),
        "w_out": chan(x["w_out"][0], KT), "g_ffn": every(x["g_ffn"][0]), "g_final": every(x["g_final"]),
        "w_route": chan(np.concatenate([x["moe_w_group"][0], np.moveaxis(x["moe_w_expert"][0], 0, 1).reshape(D, E)],
                                       axis=1), KT),
        "w_gate": x["moe_w_gate"][0], "w_up": x["moe_w_up"][0], "w_down": x["moe_w_down"][0],
    }


def kernel(**inputs):
    import numpy as np
    import concourse.bacc as bacc
    from concourse.bass_utils import run_bass_kernel_spmd

    nc = bacc.Bacc("TRN2", target_bir_lowering=False, num_devices=1)
    arrays, a, o = {}, {}, {}
    for name, v in _pack(inputs).items():
        arrays["in_" + name] = v = np.ascontiguousarray(v)
        a[name] = nc.dram_tensor("in_" + name, v.shape, mybir.dt.from_np(v.dtype), kind="ExternalInput").ap()
    for name, shape in _OUTS.items():
        o[name] = nc.dram_tensor("out_" + name, shape, F32, kind="ExternalOutput").ap()
    encoder_step(nc, a, o)
    res = run_bass_kernel_spmd(nc, [arrays], core_ids=[0]).results[0]
    r = {name: np.asarray(res["out_" + name]).reshape(shape) for name, shape in _OUTS.items()}

    def state(v):
        return np.ascontiguousarray(v.reshape(2, 64, 2, HD).transpose(0, 2, 3, 1)).reshape(1, 1, 4, HD, 64)

    def rows(v, w):
        return np.ascontiguousarray(np.moveaxis(v, 0, 1).reshape(-1, w).T)
    tail = r["ssd_tail"].reshape(P, 4, 2, 3)
    end = r["s5_end"].reshape(P, 2, 2, ST)

    def s5(s, m):
        return np.ascontiguousarray(end[:, s, m, :].T).reshape(1, 1, 16, 64)
    return (r["y_p"].reshape(1, TP, D), r["y_s"].reshape(1, TS, D), state(r["ssd_p"]), state(r["ssd_s"]),
            rows(tail[:, :, 0], 3).reshape(1, 1, 3, 512), rows(tail[:, :, 1], 3).reshape(1, 1, 3, 512),
            rows(r["ccm_p"], DW - 1).reshape(1, 1, DW - 1, 256), rows(r["ccm_s"], DW - 1).reshape(1, 1, DW - 1, 256),
            rows(r["k_p"], WIN).reshape(1, 1, WIN, 4, HD), rows(r["k_s"], TS).reshape(1, 1, TS, 4, HD),
            np.ascontiguousarray(np.moveaxis(r["v_p"], 0, 1)).reshape(1, 1, WIN, 4, HD),
            r["v_s"].reshape(1, 1, TS, 4, HD), s5(0, 0), s5(1, 0), s5(0, 1), s5(1, 1))
```

```python
import math
from contextlib import ExitStack

import concourse.bass as bass
from concourse import mybir

F32 = mybir.dt.float32
I32 = mybir.dt.int32
ALU = mybir.AluOpType
ACT = mybir.ActivationFunctionType
AX = mybir.AxisListType
ds = bass.ds

P = 128
D = 1024
KT = D // P
TP, TS = 1024, 64
T = TP + TS
NT = TP // P + 1
NTOK = [P] * (NT - 1) + [TS]
HEADS, HD = 4, 64
EPS = 1e-6
ATT_SCALE = HD ** -0.5
WIN = 512
BANDW = WIN + P
CW, DW = 4, 31
XBW = (CW - 1) + TP + (CW - 1) + TS
VBW = (DW - 1) + TP + (DW - 1) + TS
VD = 260
ST = 8
NEG = -1e30
G, EPG = 4, 8
E = G * EPG
FF = 512
THR = -(-T // P)
BLOCKS = 48
NB = BLOCKS + 3
SLOTS = NB * P

FIELDS = [("g_mix", 8), ("conv_w", 16), ("conv_b", 4), ("dw_w", 62), ("dw_b", 2), ("ln_g", 2), ("ln_b", 2),
          ("pw_b", 2), ("ssd_d", 2), ("norm_w", 2), ("glu_b", 4), ("lam_re", 8), ("lam_im", 8), ("log_dt", 8),
          ("h0_re", 8), ("h0_im", 8), ("s5_d", 2), ("dt_bias", 4), ("a_log", 4), ("eps", 1), ("one", 1),
          ("thr", THR), ("iota", BLOCKS), ("order4", G), ("order8", EPG)]
COL, NCOL = {}, 0
for _n, _w in FIELDS:
    COL[_n] = (NCOL, _w)
    NCOL += _w


P5 = {"lrdt": 1, "angles": 9, "tables": 67, "bb": 83}
P5A = {"bbT": 5}
RT = {"d4": 2, "dm": 22, "pre": 37, "routed": 47, "dest": 55, "slotf": 60}


class Steps:

    def __init__(self, sem, *names):
        self.sem, self.names, self.n = sem, names, 0

    def of(self, name):
        assert self.names[self.n % len(self.names)] == name, (self.names, name)
        self.n += 1
        return self.sem, 1

    def at(self, rnd, name):
        return self.sem, rnd * len(self.names) + self.names.index(name) + 1


def encoder_step(nc, a, o):
    with ExitStack() as ctx:
        def sb(name, cols, dt=F32):
            return ctx.enter_context(nc.sbuf_tensor(name, [P, cols], dt))

        def sem(name):
            return ctx.enter_context(nc.semaphore(name))

        def steps(name, *names):
            return Steps(sem(name), *names)

        def bc(x, axis, n):
            x = x.unsqueeze(axis)
            return x.broadcast_to([n if d == axis else s for d, s in enumerate(x.shape)])

        hn_dram = nc.dram_tensor("hn_rows", [T, D], F32, kind="Internal").ap()
        slot_dram = nc.dram_tensor("slot_token", [SLOTS, 1], I32, kind="Internal").ap()
        out_dram = nc.dram_tensor("expert_rows", [2 * T, D], F32, kind="Internal").ap()

        arena1 = sb("arena1", 24576)
        arena2 = sb("arena2", NT * D)
        arena3 = sb("arena3", KT * T)
        arena4 = sb("arena4", 6400)
        cst = sb("params", NCOL)
        mats = sb("mats", 4 * P)
        small = sb("small", 1150)
        tables = sb("phase_tables", 2 * ST * P)
        ints = sb("ints", 4 * NT + BLOCKS + 2 * NB + 5 + P, I32)

        def col(name, i=0, n=1):
            return cst[:, COL[name][0] + i:COL[name][0] + i + n]

        ident, ones, upper, negmask = (mats[:, i * P:(i + 1) * P] for i in range(4))

        class Arena:
            def __init__(self, t, at=0):
                self.t, self.at = t, at

            def take(self, n):
                self.at += n
                return self.t[:, self.at - n:self.at]

        a1 = Arena(arena1)
        xn = a1.take(KT * T).rearrange("p (k t) -> p k t", k=KT)
        wring = a1.take(4 * D).rearrange("p (r n) -> p r n", r=4)
        wvd = a1.take(KT * VD).rearrange("p (k n) -> p k n", k=KT)
        xb = a1.take(4 * XBW).rearrange("p (j t) -> p j t", j=4)
        sg = a1.take(2 * T).rearrange("p (j t) -> p j t", j=2)
        vc = a1.take(2 * T).rearrange("p (j t) -> p j t", j=2)
        pww = a1.take(2 * 256).rearrange("p (k n) -> p k n", k=2)
        cvs = a1.take(4 * TS).rearrange("p (j t) -> p j t", j=4)
        s5 = Arena(arena1)

        def s5take():
            return s5.take(D).rearrange("p (s t) -> p s t", s=ST)
        s5u, s5g, s5t, s5h = ([s5take(), s5take()] for _ in range(4))
        s5v = [vc[:, 0, 0:D].rearrange("p (s t) -> p s t", s=ST),
               vc[:, 1, 0:D].rearrange("p (s t) -> p s t", s=ST)]
        s5m = Arena(arena1, KT * D)
        bb = [s5m.take(ST * 32).rearrange("p (s c) -> p s c", s=ST) for _ in range(2)]
        cc = [s5m.take(ST * 32).rearrange("p (s c) -> p s c", s=ST) for _ in range(2)]
        bbT = [s5m.take(2 * P).rearrange("p (j n) -> p j n", j=2) for _ in range(2)]
        s5raw = pww.rearrange("p k n -> p (k n)")
        s5w = s5raw.rearrange("p (m s c) -> p m s c", m=4, s=ST)
        glu_w = s5m.take(2 * 512).rearrange("p (k n) -> p k n", k=2)
        gel = sg
        w_out = s5m.take(KT * D).rearrange("p (k n) -> p k n", k=KT)
        moe_w = arena1[:, :].rearrange("p (r n) -> p r n", r=2)
        wg = [moe_w[:, r, 0:4096].rearrange("p (k n) -> p k n", k=KT) for r in range(2)]
        wu = [moe_w[:, r, 4096:8192].rearrange("p (k n) -> p k n", k=KT) for r in range(2)]
        wd = [moe_w[:, r, 8192:12288].rearrange("p (k n) -> p k n", k=4) for r in range(2)]

        a2 = Arena(arena2)
        kt = a2.take(2 * 1600).rearrange("p (j t) -> p j t", j=2)
        vt = a2.take(13 * 256).rearrange("p (j n) -> p j n", j=13)
        vb = a2.take(2 * VBW).rearrange("p (j t) -> p j t", j=2)
        hres = arena2[:, :].rearrange("p (i n) -> p i n", i=NT)

        mix = arena3[:, :].rearrange("p (k t) -> p k t", k=KT)
        Z, CA, Q, UD = 0, 2, 4, 6
        a3 = Arena(arena3)
        xg = [a3.take(D) for _ in range(2)]
        xgT = [a3.take(D).rearrange("p (k n) -> p k n", k=KT) for _ in range(2)]
        actg = [a3.take(FF) for _ in range(2)]
        hmid = [a3.take(FF) for _ in range(2)]
        orow = [a3.take(D) for _ in range(2)]

        a4 = Arena(arena4)
        bias = a4.take(HEADS * BANDW).rearrange("p (h k) -> p h k", h=HEADS)
        sc, pr, pts = ([a4.take(BANDW) for _ in range(2)] for _ in range(3))
        sq = [arena4[:, i * T:(i + 1) * T] for i in range(2)]
        turns = Arena(arena4, HEADS * BANDW)
        tt = [turns.take(ST * 64).rearrange("p (s t) -> p s t", s=ST) for _ in range(2)]
        w4 = Arena(arena1)
        ua, ebc, dm, ce = (w4.take(512).rearrange("p (h t) -> p h t", h=4) for _ in range(4))
        xdt = w4.take(256)
        xdd = w4.take(256)
        btok = w4.take(P)
        v4 = Arena(arena4)
        xtok = [v4.take(D) for _ in range(2)]
        hn = [v4.take(D) for _ in range(2)]
        gffn = v4.take(D)
        hnT = v4.take(D).rearrange("p (k n) -> p k n", k=KT)
        f4 = Arena(arena4)
        gfin = f4.take(D)
        gdiag = [[f4.take(P) for _ in range(2)] for _ in range(NT)]
        f1 = Arena(arena1)
        og = [[f1.take(D) for _ in range(2)] for _ in range(NT)]
        f3 = Arena(arena3)
        yrow = [f3.take(D) for _ in range(3)]
        sqrow = [f3.take(D) for _ in range(2)]

        sm = Arena(small)
        dtr, dta, dtt, aa, nacs, dec, etot = (
            sm.take(NT * 4).rearrange("p (i h) -> p i h", h=4) for _ in range(7))
        aexp = sm.take(4)
        state = [sm.take(P) for _ in range(2)]
        tail = sm.take(24).rearrange("p (j s w) -> p j s w", j=4, s=2)
        nmx, rsum, rinv = (sm.take(NT * HEADS) for _ in range(3))
        s5p = sm.take(16 * ST).rearrange("p (n s) -> p n s", s=ST)
        s5end = sm.take(2 * 2 * ST).rearrange("p (r c s) -> p r c s", r=2, c=2)
        cmul = sm.take(4 * ST).rearrange("p (n s) -> p n s", s=ST)
        ssum, hrs = sm.take(NT), sm.take(NT)
        diag = [sm.take(P) for _ in range(2)]
        DT, MAG, TH, COS, SIN, AR, AI, CR, CI, T0, T1, T2 = range(12)

        cosT = tables[:, 0:ST * P].rearrange("p (s t) -> p s t", s=ST)
        sinT = tables[:, ST * P:].rearrange("p (s t) -> p s t", s=ST)
        rt = Arena(tables)
        rw = rt.take(KT * 36).rearrange("p (k n) -> p k n", k=KT)
        lgt = rt.take(NT * 36).rearrange("p (i n) -> p i n", i=NT)
        ohg = rt.take(NT * G).rearrange("p (i g) -> p i g", g=G)
        d4 = rt.take(NT * G).rearrange("p (i g) -> p i g", g=G)
        les = rt.take(NT * EPG).rearrange("p (i e) -> p i e", e=EPG)
        oh = [rt.take(NT * EPG).rearrange("p (i e) -> p i e", e=EPG) for _ in range(2)]
        t8 = rt.take(NT * EPG).rearrange("p (i e) -> p i e", e=EPG)
        m4, mm, m1, m2, pgr, gs = (rt.take(NT) for _ in range(6))
        gate = [rt.take(NT) for _ in range(2)]
        destf = rt.take(2 * NT).rearrange("p (k i) -> p k i", k=2)
        nblk, bend, base = (rt.take(E) for _ in range(3))
        eidf = rt.take(BLOCKS)
        slotf = rt.take(P)
        slotc = rt.take(NB)
        slotm = rt.take(NB)
        rb = Arena(arena1, 2 * KT * FF)
        prod = rb.take(NT * E).rearrange("p (i g e) -> p i g e", g=G, e=EPG)
        oe = [rb.take(NT * E).rearrange("p (i g e) -> p i g e", g=G, e=EPG) for _ in range(2)]
        asg = rb.take(NT * E).rearrange("p (i e) -> p i e", e=E)
        pre = rb.take((NT + 1) * E).rearrange("p (i e) -> p i e", e=E)
        dmap = rb.take(NT * E).rearrange("p (i e) -> p i e", e=E)
        cmp = rb.take(BLOCKS * E)
        ia = Arena(ints)
        asgid = ia.take(2 * NT).rearrange("p (k i) -> p k i", k=2)
        dest = ia.take(2 * NT).rearrange("p (k i) -> p k i", k=2)
        eid = ia.take(BLOCKS)
        npairs = ia.take(1)
        slot_out = ia.take(NB)
        slot_in = ia.take(NB)
        curidx = [ia.take(1) for _ in range(2)]
        curout = [ia.take(1) for _ in range(2)]
        slots_rows = ia.take(P)

        psA = ctx.enter_context(nc.psum_tensor("psA", [P, 1536], F32))
        psB = ctx.enter_context(nc.psum_tensor("psB", [P, 1536], F32))
        psC = ctx.enter_context(nc.psum_tensor("psC", [P, 1024], F32))
        AB = [psA, psB]
        fin = [psA, psB, psC]
        CH = [(0, 512), (512, 1024), (1024, T)]

        s_params, s_hist, s_cache, s_bias = sem("params_in"), sem("histories_in"), sem("cache_in"), sem("bias_in")
        s_x = [sem(f"x{k}_in") for k in range(KT)]
        s_w = [sem(f"w_in_slot{k}") for k in range(4)]
        s_wvd, s_s5w, s_pww = sem("w_vdt_in"), sem("s5_weights_in"), sem("pointwise_in")
        s_out = sem("states_out")
        s_wout, s_gffn = sem("w_out_in"), sem("g_ffn_in")
        s_xtok = [sem(f"x_rows{k}_in") for k in range(2)]
        s_hst = [sem(f"hn_rows{k}_out") for k in range(2)]
        s_slotz, s_scat, s_slotin = sem("slots_cleared"), sem("slots_scattered"), sem("slots_in")
        s_wgu = [sem(f"gate_up{k}_in") for k in range(2)]
        s_wd = [sem(f"down{k}_in") for k in range(2)]
        s_xg = [sem(f"gathered{k}") for k in range(2)]
        s_os = [sem(f"expert_rows{k}_out") for k in range(2)]
        s_og = [sem(f"expert_rows{i}_back") for i in range(NT)]
        s_yo, s_gfin = [sem(f"y_rows{k}_out") for k in range(3)], sem("g_final_in")
        zeroed = sem("buffers_zeroed")
        nrm_act = steps("norm_act", *["sq"] * KT, "ln", "rs")
        nrm_pe = sem("norm_pe")
        xn_dve = sem("xn_ready")
        proj = sem("proj_done")
        ev = sem("proj_moved")
        gated = sem("conv_input_gated")
        vd_pe, vd_ev = sem("vdt_done"), sem("vdt_moved")
        dtp_dve = steps("dt_dve", "raw", "abs", "dt", "a", "nacs", "decin")
        dtp_act = steps("dt_act", "e", "ln", "aexp", "dec", "etot")
        dtp_pe = sem("dt_cumsums")
        cv_dve = sem("conv4_taps")
        cv_act = sem("conv4_silu")
        tailed = sem("conv_tail_copied")
        ssd_pe = steps("ssd_pe", "bc", "tr", "y", "st")
        ssd_act = steps("ssd_act", "ebc", "decay")
        ssd_dve = steps("ssd_dve", "dm", "m", "xdt", "btok", "ce", "state", "yd")
        ssd_pool = steps("ssd_pool", "ua", "xdd")
        yg_dve = steps("ssd_out_dve", "gate0", "gate1", "norm0", "norm1")
        yg_act = steps("ssd_out_act", "sq0", "sq1", "ln0", "rs0", "ln1", "rs1")
        yg_pe = sem("ssd_out_pe")
        dw_dve = sem("dwconv_taps")
        cm_act = steps("ccm_act", "sq0", "sq1", "ln", "rs", "silu0", "silu1", "out0", "out1")
        cm_pe = steps("ccm_pe", "mu", "var", "pw0", "pw1")
        cm_dve = steps("ccm_dve", "cen0", "cen1", "n0", "n1")
        at_s, at_pt, at_pv = sem("att_scores"), sem("att_probsT"), sem("att_out")
        at_add, at_max, at_rinv, at_diag = sem("att_biased"), sem("att_max"), sem("att_rinv"), sem("att_diag")
        at_exp, at_ptc, at_ovc = sem("att_exp"), sem("att_probsT_moved"), sem("att_out_moved")
        p5_dve, p5_act, p5_pe = sem("s5_setup_dve"), sem("s5_setup_act"), sem("s5_setup_pe")
        s5_x, s5_y = sem("s5_inputs"), sem("s5_outputs")
        s5_dve = steps("s5_dve", "half0", "half1", "u1", "u0", "scan", "carry", "end")
        s5_yd = sem("s5_y_moved")
        s5_pool = steps("s5_pool", "m0", "re", "m1", "im")
        glu_act = steps("glu_act", "gelu0", "gelu1", "sig0", "sig1")
        glu_pe = steps("glu_pe", "gb0", "gb1", "ga0", "ga1")
        glu_dve = sem("glu_dve")
        wo_pe = sem("h_products")
        tr_pe, lg_pe = sem("hn_transposed"), sem("logits")
        wo_dve = steps("h_dve", "add", "hn")
        wo_act = steps("h_act", "sq", "ln", "rs")
        hte = sem("hnT_moved")
        lge = sem("logits_moved")
        rt_dve, rt_act, rt_pe, rt_pool = sem("route_dve"), sem("route_act"), sem("route_pe"), sem("route_pool")
        indirect_go = sem("indirect_go")
        slots_ready, idxc, outc = sem("slots_ready"), sem("index_copied"), sem("out_index_copied")
        m_xt, m_xte, m_gu, m_sil, m_hm, m_ht, m_hte, m_dn, m_dnA, m_dnD, m_free = (
            [sem(f"moe_{n}{k}") for k in range(2)]
            for n in ("xT", "xT_moved", "gate_up", "silu", "product", "productT", "productT_moved", "down",
                      "down_moved_act", "down_moved_dve",
                      "rows_free"))
        f_pe, f_diag = sem("final_sums"), sem("gates_on_diagonal")
        f_dve_sum, f_dve_y = sem("final_summed"), sem("final_y")
        f_act = steps("final_act", "sq", "ln", "rs")

        block = ctx.enter_context(nc.Block())

        TILES = [("g", 0), ("g", 1), ("a", 0), ("a", 1), ("xbc", 0), ("xbc", 1), ("xbc", 2), ("xbc", 3),
                 ("k", 0), ("k", 1), ("q", 0), ("q", 1), ("z", 0), ("z", 1), ("ud", 0), ("ud", 1)]
        EV_AT = {}
        for _j, _t in enumerate(TILES):
            if _t[0] != "a":
                EV_AT[_j] = len(EV_AT) + 1
        A0 = TILES.index(("a", 0))
        S5_AT = 6
        CV_AT = 12

        def tile_moved(eng, j):
            if TILES[j][0] == "a":
                eng.wait_ge(gated, j - A0 + 1)
            else:
                eng.wait_ge(ev, EV_AT[j])

        def tok(i):
            return slice(i * P, i * P + NTOK[i])

        def band(i):
            if i == NT - 1:
                return 1024, [(8 + n, P) for n in range(4)] + [(12, TS)], 0
            lo = max(0, i - 4)
            return lo * P, [(n, P) for n in range(lo, i + 1)], (4 - (i - lo)) * P

        ROUNDS = [(i, h) for i in range(NT) for h in range(HEADS)]
        TAIL = 2 * NT
        S5_FIRST = TAIL + 5
        S5_ROUND = {S5_FIRST + c * (len(ROUNDS) - 1 - S5_FIRST) // (NT - 1): c for c in range(NT)}

        @block.sync
        def _(sp):
            sp.dma_start(cst[:, :], a["params"]).then_inc(s_params, 16)
            sp.dma_start(mats[:, :], a["mats"]).then_inc(s_params, 16)
            sp.dma_start(asgid, a["asgid"]).then_inc(s_params, 16)
            for k in range(KT):
                sp.dma_start(xn[:, k, :], a["xT"][k * P:(k + 1) * P, :]).then_inc(s_x[k], 16)
                if k < 4:
                    sp.dma_start(wring[:, k, :], a["w_cm"][k]).then_inc(s_w[k], 16)
            sp.dma_start(wvd, a["w_vd"]).then_inc(s_wvd, 16)
            sp.dma_start(xb[:, :, CW - 1 + TP:CW - 1 + TP + CW - 1], a["ssd_hist"]).then_inc(s_hist, 16)
            sp.dma_start(vb[:, :, DW - 1 + TP:DW - 1 + TP + DW - 1], a["ccm_hist"]).then_inc(s_hist, 16)
            sp.dma_start(state[1], a["ssd_h0"]).then_inc(s_hist, 16)
            sp.dma_start(kt[:, :, 1024:1536], a["k_cache"]).then_inc(s_cache, 16)
            sp.dma_start(vt[:, 8:12, :], a["v_cache"]).then_inc(s_cache, 16)
            for j in range(4, len(TILES)):
                sp.wait_ge(proj, j - 3)
                sp.dma_start(wring[:, j % 4, :], a["w_cm"][j]).then_inc(s_w[j % 4], 16)
            sp.wait_ge(nrm_pe, KT)
            sp.dma_start(bias, a["bias"]).then_inc(s_bias, 16)
            sp.dma_start(pww, a["pw_w"]).then_inc(s_pww, 16)
            sp.wait_ge(proj, len(TILES))
            sp.dma_start(glu_w, a["glu_w"]).then_inc(s_s5w, 16)
            sp.wait_ge(*cm_pe.at(0, "pw1"))
            sp.dma_start(s5raw, a["s5_w"]).then_inc(s_s5w, 16)
            sp.wait_ge(tailed, 1)
            sp.dma_start(o["ssd_tail"], tail).then_inc(s_out, 16)
            sp.wait_ge(gated, 2)
            sp.dma_start(o["ccm_p"], vb[:, :, TP:TP + DW - 1]).then_inc(s_out, 16)
            sp.dma_start(o["ccm_s"], vb[:, :, VBW - (DW - 1):VBW]).then_inc(s_out, 16)
            sp.wait_ge(ev, len(EV_AT))
            sp.dma_start(o["k_p"], kt[:, :, TP - WIN:TP]).then_inc(s_out, 16)
            sp.dma_start(o["k_s"], kt[:, :, 1536:1600]).then_inc(s_out, 16)
            sp.wait_ge(vd_ev, NT)
            sp.dma_start(o["v_p"], vt[:, 4:8, :]).then_inc(s_out, 16)
            sp.dma_start(o["v_s"], vt[0:TS, 12, :]).then_inc(s_out, 16)
            sp.wait_ge(*ssd_dve.at(NT - 1, "state"))
            sp.dma_start(o["ssd_p"], state[0]).then_inc(s_out, 16)
            sp.dma_start(o["ssd_s"], state[1]).then_inc(s_out, 16)
            sp.wait_ge(*yg_dve.at(0, "norm1"))
            sp.dma_start(w_out, a["w_out"]).then_inc(s_wout, 16)
            sp.wait_ge(*s5_dve.at(NT - 1, "end"))
            sp.dma_start(o["s5_end"], s5end).then_inc(s_out, 16)
            sp.wait_ge(at_ovc, len(ROUNDS))
            sp.dma_start(gffn, a["g_ffn"]).then_inc(s_gffn, 16)
            sp.wait_ge(*s5_pool.at(NT - 1, "im"))
            sp.dma_start(rw, a["w_route"]).then_inc(s_gffn, 16)
            for i in range(NT):
                if i >= 2:
                    sp.wait_ge(*wo_dve.at(i - 2, "add"))
                sp.dma_start(xtok[i % 2][0:NTOK[i], :], a["x_rows"][tok(i), :]).then_inc(s_xtok[i % 2], 16)
                if i >= 1:
                    sp.wait_ge(*wo_dve.at(i - 1, "hn"))
                    sp.dma_start(hn_dram[tok(i - 1), :], hn[(i - 1) % 2][0:NTOK[i - 1], :]
                                 ).then_inc(s_hst[(i - 1) % 2], 16)
            sp.wait_ge(*wo_dve.at(NT - 1, "hn"))
            sp.dma_start(hn_dram[tok(NT - 1), :], hn[(NT - 1) % 2][0:TS, :]).then_inc(s_hst[(NT - 1) % 2], 16)
            sp.wait_ge(rt_dve, RT["routed"])
            pairs = sp.value_load(npairs[0:1, :], min_val=1, max_val=BLOCKS // 2)
            def gate_up_in(r, i):
                e = sp.value_load(eid[0:1, ds(2 * i + r, 1)], min_val=0, max_val=E - 1)
                sp.wait_ge(m_gu[r], i + 1)
                sp.dma_start(wg[r], a["w_gate"][ds(e, 1), :, :].rearrange("o (p k) n -> (o p) k n", k=KT)
                             ).then_inc(s_wgu[r], 16)
                sp.dma_start(wu[r], a["w_up"][ds(e, 1), :, :].rearrange("o (p k) n -> (o p) k n", k=KT)
                             ).then_inc(s_wgu[r], 16)

            def down_in(r, i):
                e = sp.value_load(eid[0:1, ds(2 * i + r, 1)], min_val=0, max_val=E - 1)
                sp.wait_ge(m_dn[r], i + 1)
                sp.dma_start(wd[r], a["w_down"][ds(e, 1), :, :].rearrange("o (p k) n -> (o p) k n", k=4)
                             ).then_inc(s_wd[r], 16)

            gate_up_in(0, 0)
            sp.wait_ge(s_xg[0], 16)
            gate_up_in(1, 0)
            down_in(0, 0)
            with sp.Fori(1, BLOCKS // 2) as i:
                with sp.If(pairs > i):
                    gate_up_in(0, i)
                    down_in(1, i - 1)
                    gate_up_in(1, i)
                    down_in(0, i)
            down_in(1, pairs - 1)
            sp.dma_start(gfin, a["g_final"]).then_inc(s_gfin, 16)
            sp.wait_ge(s_os[0], 16 * pairs)
            sp.wait_ge(s_os[1], 16 * pairs)
            for i in range(NT):
                for k in range(2):
                    sp.dma_start(og[i][k][0:NTOK[i], :], out_dram[k * T + i * P:k * T + i * P + NTOK[i], :]
                                 ).then_inc(s_og[i], 16)
            for i in range(NT):
                sp.wait_ge(f_dve_y, i + 1)
                dst = o["y_p"][tok(i), :] if i < NT - 1 else o["y_s"]
                sp.dma_start(dst, yrow[i % 3][0:NTOK[i], :]).then_inc(s_yo[i % 3], 16)
            sp.wait_ge(s_out, 16 * 10)
            for k in range(3):
                sp.wait_ge(s_yo[k], 16 * 3)

        @block.tensor
        def _(te):
            te.wait_ge(s_params, 48)
            for k in range(KT):
                te.wait_ge(*nrm_act.at(0, "sq") if k == 0 else (nrm_act.sem, k + 1))
                for c, (lo, hi) in enumerate(CH):
                    mm = te.matmul(psB[:, lo:hi], ones, sq[k % 2][:, lo:hi], start=(k == 0), stop=(k == KT - 1))
                mm.then_inc(nrm_pe, 1)
            for j in range(len(TILES)):
                te.wait_ge(s_w[j % 4], 16 * (j // 4 + 1))
                if j >= 2:
                    tile_moved(te, j - 2)
                for k in range(KT):
                    if j == 0:
                        te.wait_ge(xn_dve, k + 1)
                    for lo, hi in CH:
                        mm = te.matmul(AB[j % 2][:, lo:hi], wring[:, j % 4, k * P:(k + 1) * P], xn[:, k, lo:hi],
                                       start=(k == 0), stop=(k == KT - 1))
                mm.then_inc(proj, 1)
            te.wait_ge(s_wvd, 16)
            te.wait_ge(dw_dve, 2 * 2 * DW)
            te.wait_ge(cv_act, 4)
            tile_moved(te, len(TILES) - 2)
            for j in range(2):
                for lo, hi in CH:
                    mm = te.matmul(psA[:, lo:hi], ones, vc[:, j, lo:hi], start=(j == 0), stop=(j == 1))
            mm.then_inc(*cm_pe.of("mu"))
            for i in range(NT):
                if i == 4:
                    te.wait_ge(*cm_act.at(0, "sq1"))
                    tile_moved(te, len(TILES) - 1)
                    for j in range(2):
                        for lo, hi in CH:
                            mm = te.matmul(psB[:, lo:hi], ones, sg[:, j, lo:hi], start=(j == 0), stop=(j == 1))
                    mm.then_inc(*cm_pe.of("var"))
                if i >= 2:
                    te.wait_ge(vd_ev, i - 1)
                for k in range(KT):
                    mm = te.matmul(psC[0:NTOK[i], 512 * (i % 2):512 * (i % 2) + VD], xn[:, k, tok(i)], wvd[:, k, :],
                                   start=(k == 0), stop=(k == KT - 1))
                mm.then_inc(vd_pe, 1)
            te.wait_ge(s_pww, 16)
            te.wait_ge(*cm_act.at(0, "silu1"))
            for m in range(2):
                for k in range(2):
                    for lo, hi in CH:
                        mm = te.matmul(AB[m][:, lo:hi], pww[:, k, m * P:(m + 1) * P], vc[:, k, lo:hi],
                                       start=(k == 0), stop=(k == 1))
                mm.then_inc(*cm_pe.of(f"pw{m}"))
            te.wait_ge(*dtp_dve.at(0, "a"))
            te.wait_ge(vd_ev, NT)
            L8 = slice(0, TS)
            te.matmul(psC[:, 0:32], upper, aa[:, 0:8, :], start=True, stop=True)
            te.matmul(psC[:, 32:36], upper[L8, :], aa[L8, 8, :], start=True, stop=True)
            te.matmul(psC[:, 512:544], ones, aa[:, 0:8, :], start=True, stop=True)
            te.matmul(psC[:, 544:548], ones[L8, :], aa[L8, 8, :], start=True, stop=True).then_inc(dtp_pe, 1)
            def ssd_sums(c):
                te.wait_ge(*ssd_pool.at(c, "ua"))
                if c:
                    te.wait_ge(*ssd_dve.at(c - 1, "state"))
                te.matmul(psB[:, 0:512], ones[0:NTOK[c], :], ua[0:NTOK[c]], start=True, stop=True
                          ).then_inc(*ssd_pe.of("bc"))

            def ssd_inner(c):
                L = NTOK[c]
                if c:
                    te.wait_ge(*ssd_dve.at(c - 1, "yd"))
                for g in range(2):
                    te.matmul(psB[0:L, 512 * (1 + g):512 * (1 + g) + L], xb[g * 64:g * 64 + 64, 2, tok(c)],
                              xb[g * 64:g * 64 + 64, 3, tok(c)], start=True, stop=True)
                for j in range(3):
                    at = 640 + j * P if j < 2 else 1152
                    mm = te.transpose(psB[0:L, at:at + P], xb[:, j, tok(c)], ident)
                mm.then_inc(*ssd_pe.of("tr"))

            def ssd_outer(c):
                L = NTOK[c]
                te.wait_ge(*ssd_dve.at(c, "ce"))
                st = state[1 if c == NT - 1 else 0]
                for h in range(HEADS):
                    g, hh = divmod(h, 2)
                    y = psB[hh * 64:hh * 64 + 64, 896 + 512 * g:896 + 512 * g + L]
                    mm = te.matmul(y, xdt[:, h * 64:h * 64 + 64], dm[:, h, 0:L], start=True, stop=(c == 0))
                    if c:
                        mm = te.matmul(y, st[g * 64:g * 64 + 64, hh * 64:hh * 64 + 64],
                                       ce[g * 64:g * 64 + 64, h, 0:L], start=False, stop=True)
                mm.then_inc(*ssd_pe.of("y"))
                te.wait_ge(*ssd_pool.at(c, "xdd"))
                for g in range(2):
                    mm = te.matmul(psB[g * 64:g * 64 + 64, 0:P], btok[0:L, g * 64:g * 64 + 64],
                                   xdd[0:L, g * P:(g + 1) * P], start=True, stop=True)
                mm.then_inc(*ssd_pe.of("st"))

            def group_sums(g):
                te.wait_ge(*yg_act.at(0, f"sq{g}"))
                if g:
                    te.wait_ge(*yg_dve.at(0, "norm0"))
                for lo, hi in CH:
                    mm = te.matmul(psB[:, lo:hi], ones, sg[:, g, lo:hi], start=True, stop=True)
                mm.then_inc(yg_pe, 1)

            def s5_turn():
                te.wait_ge(p5_dve, P5["bb"])
                for m in range(2):
                    for j in range(2):
                        mm = te.transpose(psB[:, (2 * m + j) * P:(2 * m + j + 1) * P],
                                          bb[m].rearrange("p s c -> p (s c)")[:, j * P:(j + 1) * P], ident)
                mm.then_inc(p5_pe, 1)

            def s5_in(c, half):
                L = NTOK[c]
                if c + half == 0:
                    te.wait_ge(p5_act, P5A["bbT"])
                elif half:
                    te.wait_ge(*s5_dve.at(c, "half0"))
                else:
                    te.wait_ge(*s5_dve.at(c - 1, "half1"))
                for q in (2 * half, 2 * half + 1):
                    for jt in range(2):
                        for m in range(2):
                            at = 512 * (q % 2) + (2 * jt + m) * P
                            mm = te.matmul(psB[:, at:at + L], bbT[m][32 * q:32 * q + 32, jt, :],
                                           mix[32 * q:32 * q + 32, UD + jt, tok(c)], start=True, stop=True)
                mm.then_inc(s5_x, 1)

            def s5_out(c):
                L = NTOK[c]
                te.wait_ge(*s5_pool.at(c, "im"))
                if c:
                    te.wait_ge(s5_yd, c)
                for s in range(ST):
                    jt, q = divmod(s, 4)
                    for m in range(2):
                        at = 1024 + jt * P
                        mm = te.matmul(psB[32 * q:32 * q + 32, at:at + L], cc[m][:, s, :],
                                       s5h[m][:, s, 0:L], start=(m == 0), stop=(m == 1))
                mm.then_inc(s5_y, 1)

            def scores(r):
                i, h = ROUNDS[r]
                pair, hh = divmod(h, 2)
                k0, tiles, _ = band(i)
                nk = sum(w for _, w in tiles)
                rows = slice(hh * 64, hh * 64 + 64)
                if r:
                    te.wait_ge(at_add, r)
                for lo in range(0, nk, 512):
                    hi = min(lo + 512, nk)
                    mm = te.matmul(psA[0:NTOK[i], lo:hi], mix[rows, Q + pair, tok(i)],
                                   kt[rows, pair, k0 + lo:k0 + hi], start=True, stop=True)
                mm.then_inc(at_s, 1)

            def turn_probs(r):
                i, h = ROUNDS[r]
                _, tiles, _ = band(i)
                nq = NTOK[i]
                te.wait_ge(at_diag, r + 1)
                te.wait_ge(at_exp, r + 1)
                if r >= 1:
                    te.wait_ge(at_ptc, r)
                for n, (_, w) in enumerate(tiles):
                    mm = te.matmul(psC[0:w, n * nq:(n + 1) * nq], pr[r % 2][0:nq, n * P:n * P + w],
                                   diag[r % 2][0:nq, 0:nq], start=True, stop=True)
                mm.then_inc(at_pt, 1)

            def outputs(r):
                i, h = ROUNDS[r]
                hh, nq = h % 2, NTOK[i]
                _, tiles, _ = band(i)
                te.wait_ge(at_ptc, r + 1)
                if r:
                    te.wait_ge(at_ovc, r)
                for n, (v, w) in enumerate(tiles):
                    mm = te.matmul(psA[hh * 64:hh * 64 + 64, 1024:1024 + nq], vt[0:w, v, h * 64:h * 64 + 64],
                                   pts[r % 2][0:w, n * nq:(n + 1) * nq], start=(n == 0), stop=(n == len(tiles) - 1))
                mm.then_inc(at_pv, 1)

            te.wait_ge(*cm_act.at(0, "out1"))
            te.wait_ge(*dtp_act.at(0, "etot"))
            te.wait_ge(s_hist, 48)
            te.wait_ge(s_cache, 32)
            scores(0)
            scores(1)
            for r in range(len(ROUNDS)):
                c, second = divmod(r, 2)
                if not second and 1 <= c <= NT:
                    ssd_outer(c - 1)
                if r in (TAIL + 2, TAIL + 3):
                    group_sums(r - TAIL - 2)
                if r == TAIL + 4:
                    s5_turn()
                    s5_in(0, 0)
                if r in S5_ROUND:
                    s5_in(S5_ROUND[r], 1)
                turn_probs(r)
                if r + 2 < len(ROUNDS):
                    scores(r + 2)
                if r in S5_ROUND and S5_ROUND[r] + 1 < NT:
                    s5_in(S5_ROUND[r] + 1, 0)
                outputs(r)
                if not second and c < NT:
                    ssd_sums(c)
                    ssd_inner(c)
                if r in S5_ROUND and S5_ROUND[r]:
                    s5_out(S5_ROUND[r] - 1)
            s5_out(NT - 1)
            te.wait_ge(at_ovc, len(ROUNDS))
            te.wait_ge(s5_yd, NT)
            te.wait_ge(*glu_act.at(0, "gelu1"))
            for m, name in ((2, "gb0"), (3, "gb1"), (0, "ga0"), (1, "ga1")):
                if m < 2:
                    te.wait_ge(*glu_act.at(0, f"sig{m}"))
                for k in range(2):
                    for lo, hi in CH:
                        mm = te.matmul(AB[m % 2][:, lo:hi], glu_w[:, k, m * P:(m + 1) * P], gel[:, k, lo:hi],
                                       start=(k == 0), stop=(k == 1))
                mm.then_inc(*glu_pe.of(name))
            te.wait_ge(s_wout, 16)
            te.wait_ge(glu_dve, 2)

            def h_tile(i):
                if i >= 2:
                    te.wait_ge(*wo_dve.at(i - 2, "add"))
                for n in range(2):
                    for k in range(KT):
                        mm = te.matmul(AB[i % 2][0:NTOK[i], n * 512:(n + 1) * 512], mix[:, k, tok(i)],
                                       w_out[:, k, n * 512:(n + 1) * 512], start=(k == 0), stop=(k == KT - 1))
                mm.then_inc(wo_pe, 1)

            def logit_tile(i):
                te.wait_ge(*wo_dve.at(i, "hn"))
                if i:
                    te.wait_ge(hte, i)
                for k in range(KT):
                    mm = te.transpose(psC[:, k * P:k * P + NTOK[i]], hn[i % 2][0:NTOK[i], k * P:(k + 1) * P],
                                      ident[0:NTOK[i], 0:NTOK[i]])
                mm.then_inc(tr_pe, 1)
                te.wait_ge(hte, i + 1)
                if i >= 2:
                    te.wait_ge(lge, i - 1)
                for k in range(KT):
                    mm = te.matmul(AB[i % 2][0:NTOK[i], 1024:1060], hnT[:, k, 0:NTOK[i]], rw[:, k, :],
                                   start=(k == 0), stop=(k == KT - 1))
                mm.then_inc(lg_pe, 1)

            te.wait_ge(s_gffn, 32)
            h_tile(0)
            for i in range(NT):
                if i + 1 < NT:
                    h_tile(i + 1)
                logit_tile(i)
            te.wait_ge(rt_dve, RT["pre"])
            te.matmul(psA[:, 0:NT * E], upper, asg, start=True, stop=False)
            te.matmul(psA[:, 0:NT * E], ones, pre[:, 0:NT, :], start=False, stop=True)
            te.matmul(psB[:, 0:E], ones, pre[:, NT, :], start=True, stop=True).then_inc(rt_pe, 1)
            te.wait_ge(rt_dve, RT["slotf"])
            te.transpose(psC[:, 0:NB], slotf[0:NB, :], ident[0:NB, 0:NB]
                         ).then_inc(rt_pe, 1)

            def turn_rows(b, n):
                te.wait_ge(s_xg[b], 16 * n)
                for k in range(KT):
                    mm = te.transpose(psC[:, k * P:(k + 1) * P], xg[b].rearrange("p (m k) -> p k m", k=KT)[:, k, :],
                                      ident)
                mm.then_inc(m_xt[b], 1)

            def gate_up(r, i):
                te.wait_ge(m_xte[r], i + 2)
                te.wait_ge(s_wgu[r], 32 * i + 32)
                te.wait_ge(m_hm[1 - r], i + r + 1)
                for w, at in ((wg[r], 0), (wu[r], 512)):
                    for k in range(KT):
                        mm = te.matmul(psA[:, at:at + FF], xgT[r][:, k, :], w[:, k, :],
                                       start=(k == 0), stop=(k == KT - 1))
                mm.then_inc(m_gu[r], 1)

            def turn_product(r, i):
                te.wait_ge(m_hm[r], i + 2)
                te.wait_ge(m_hte[1 - r], i + r + 1)
                for k in range(4):
                    mm = te.transpose(psA[:, 1024 + k * P:1024 + (k + 1) * P],
                                      hmid[r].rearrange("p (m k) -> p k m", k=4)[:, k, :], ident)
                mm.then_inc(m_ht[r], 1)

            def down(r, i):
                te.wait_ge(m_hte[r], i + 2)
                te.wait_ge(s_wd[r], 16 * i + 16)
                te.wait_ge(m_dnA[1 - r], i + r + 1)
                te.wait_ge(m_dnD[1 - r], i + r + 1)
                for n in range(2):
                    for k in range(4):
                        mm = te.matmul(psB[:, n * 512:(n + 1) * 512], actg[r][:, k * P:(k + 1) * P],
                                       wd[r][:, k, n * 512:(n + 1) * 512], start=(k == 0), stop=(k == 3))
                mm.then_inc(m_dn[r], 1)

            def block_products(r, i, first=False):
                gate_up(r, i)
                turn_rows(1 - r, i + 1 + r)
                if not first:
                    down(1 - r, i - 1 + r)
                turn_product(r, i)

            te.wait_ge(slots_ready, 1)
            turn_rows(0, 1)
            pairs = te.value_load(npairs[0:1, :], min_val=1, max_val=BLOCKS // 2)
            block_products(0, 0, first=True)
            block_products(1, 0)
            with te.Fori(1, BLOCKS // 2) as i:
                with te.If(pairs > i):
                    for r in range(2):
                        block_products(r, i)
            down(1, pairs - 1)
            te.wait_ge(f_diag, 1)
            te.wait_ge(m_dnA[1], pairs + 1)
            te.wait_ge(m_dnD[1], pairs + 1)
            for i in range(NT):
                M = NTOK[i]
                te.wait_ge(s_og[i], 32)
                if i >= 3:
                    te.wait_ge(f_dve_y, i - 2)
                for n in range(2):
                    for k in range(2):
                        mm = te.matmul(fin[i % 3][0:M, n * 512:(n + 1) * 512], gdiag[i][k][0:M, 0:M],
                                       og[i][k][0:M, n * 512:(n + 1) * 512], start=(k == 0), stop=(k == 1))
                mm.then_inc(f_pe, 1)

        @block.scalar
        def _(ac):
            ac.wait_ge(s_params, 48)
            for k in range(KT):
                ac.wait_ge(s_x[k], 16)
                if k >= 2:
                    ac.wait_ge(nrm_pe, k - 1)
                ac.activation(sq[k % 2], xn[:, k, :], ACT.Square).then_inc(*nrm_act.of("sq"))
            ac.wait_ge(nrm_pe, KT)
            ac.activation(psB[:, 0:T], psB[:, 0:T], ACT.Ln, scale=1.0 / D, bias=col("eps")).then_inc(*nrm_act.of("ln"))
            ac.wait_ge(nrm_act.sem, KT + 1)
            ac.activation(psB[:, 0:T], psB[:, 0:T], ACT.Exp, scale=-0.5).then_inc(*nrm_act.of("rs"))
            ac.activation(s5p[:, DT, :], col("log_dt", 0, 8), ACT.Exp).then_inc(p5_act, 1)
            ac.wait_ge(zeroed, 3)
            for j, (kind, n) in enumerate(TILES):
                if kind == "a":
                    continue
                ac.wait_ge(proj, j + 1)
                ps = AB[j % 2]
                if kind == "xbc":
                    ac.copy(xb[:, n, CW - 1:CW - 1 + TP], ps[:, 0:TP])
                    last = ac.copy(xb[:, n, XBW - TS:XBW], ps[:, TP:T])
                elif kind == "k":
                    ac.copy(kt[:, n, 0:TP], ps[:, 0:TP])
                    last = ac.copy(kt[:, n, 1536:1600], ps[:, TP:T])
                elif kind == "g":
                    last = ac.activation(sg[:, n, :], ps[:, 0:T], ACT.Sigmoid)
                elif kind == "q":
                    last = ac.copy(mix[:, Q + n, :], ps[:, 0:T])
                elif kind == "z":
                    last = ac.activation(mix[:, Z + n, :], ps[:, 0:T], ACT.Silu)
                else:
                    last = ac.copy(mix[:, UD + n, :], ps[:, 0:T])
                last.then_inc(ev, 1)
                if j == S5_AT:
                    ac.wait_ge(p5_dve, P5["lrdt"])
                    ac.activation(s5p[:, MAG, :], s5p[:, T0, :], ACT.Exp).then_inc(p5_act, 1)
                    ac.wait_ge(p5_dve, P5["angles"])
                    ac.activation(s5p[:, SIN, :], s5p[:, TH, :], ACT.Sin).then_inc(p5_act, 1)
                    ac.activation(s5p[:, COS, :], s5p[:, T1, :], ACT.Sin).then_inc(p5_act, 1)
                if j >= CV_AT:
                    n = j - CV_AT
                    ac.wait_ge(tailed, 1)
                    ac.wait_ge(cv_dve, 2 * CW * (n + 1))
                    ac.activation(xb[:, n, 0:TP], psC[:, 0:TP], ACT.Silu)
                    ac.activation(xb[:, n, TP:T], cvs[:, n, :], ACT.Silu).then_inc(cv_act, 1)

            def vd_moved(i):
                ac.wait_ge(vd_pe, i + 1)
                M, at = NTOK[i], 512 * (i % 2)
                ac.copy(vt[0:M, i if i < NT - 1 else 12, :], psC[0:M, at:at + 256])
                ac.copy(dtr[0:M, i, :], psC[0:M, at + 256:at + VD]).then_inc(vd_ev, 1)

            vd_moved(0)
            vd_moved(1)
            for j in range(2):
                ac.wait_ge(*cm_dve.at(0, f"cen{j}"))
                ac.activation(sg[:, j, :], vc[:, j, :], ACT.Square).then_inc(*cm_act.of(f"sq{j}"))
            vd_moved(2)
            vd_moved(3)
            ac.wait_ge(*cm_pe.at(0, "var"))
            ac.activation(psB[:, 0:T], psB[:, 0:T], ACT.Ln, scale=1.0 / 256, bias=col("eps")).then_inc(*cm_act.of("ln"))
            ac.wait_ge(*cm_act.at(0, "ln"))
            ac.activation(psB[:, 0:T], psB[:, 0:T], ACT.Exp, scale=-0.5).then_inc(*cm_act.of("rs"))
            vd_moved(4)
            vd_moved(5)
            for j in range(2):
                ac.wait_ge(*cm_dve.at(0, f"n{j}"))
                ac.activation(vc[:, j, :], vc[:, j, :], ACT.Silu, scale=col("ln_g", j), bias=col("ln_b", j)
                              ).then_inc(*cm_act.of(f"silu{j}"))
            for i in range(6, NT):
                vd_moved(i)
            for m in range(2):
                ac.wait_ge(*cm_pe.at(0, f"pw{m}"))
                ac.activation(mix[:, CA + m, :], AB[m][:, 0:T], ACT.Identity, bias=col("pw_b", m)
                              ).then_inc(*cm_act.of(f"out{m}"))
            ac.wait_ge(*dtp_dve.at(0, "abs"))
            ac.activation(dta, dta, ACT.Exp, scale=-1.0).then_inc(*dtp_act.of("e"))
            ac.wait_ge(*dtp_act.at(0, "e"))
            ac.activation(dta, dta, ACT.Ln, bias=col("one")).then_inc(*dtp_act.of("ln"))
            ac.activation(aexp, col("a_log", 0, 4), ACT.Exp).then_inc(*dtp_act.of("aexp"))
            ac.wait_ge(*dtp_dve.at(0, "decin"))
            ac.activation(dec, dec, ACT.Exp).then_inc(*dtp_act.of("dec"))
            ac.activation(etot.rearrange("p i h -> p (i h)"), psC[:, 512:548], ACT.Exp).then_inc(*dtp_act.of("etot"))

            def ssd_ebc(c):
                ac.wait_ge(*ssd_pe.at(c, "bc"))
                if c:
                    ac.wait_ge(*ssd_dve.at(c - 1, "ce"))
                ac.activation(ebc.rearrange("p h t -> p (h t)"), psB[:, 0:512], ACT.Exp).then_inc(*ssd_act.of("ebc"))

            def ssd_decay(c):
                L = NTOK[c]
                ac.wait_ge(*ssd_dve.at(c, "dm"))
                for h in range(HEADS):
                    last = ac.activation(dm[0:L, h, 0:L], dm[0:L, h, 0:L], ACT.Exp, bias=nacs[0:L, c, h:h + 1])
                last.then_inc(*ssd_act.of("decay"))

            def group_squares(g):
                ac.wait_ge(*yg_dve.at(0, f"gate{g}"))
                ac.activation(sg[:, g, :], xb[:, g, 0:T], ACT.Square).then_inc(*yg_act.of(f"sq{g}"))

            def group_rms(g):
                ac.wait_ge(yg_pe, g + 1)
                ac.activation(psB[:, 0:T], psB[:, 0:T], ACT.Ln, scale=1.0 / P, bias=col("eps")
                              ).then_inc(*yg_act.of(f"ln{g}"))
                ac.wait_ge(*yg_act.at(0, f"ln{g}"))
                ac.activation(psB[:, 0:T], psB[:, 0:T], ACT.Exp, scale=-0.5).then_inc(*yg_act.of(f"rs{g}"))

            def probs(r):
                i, h = ROUNDS[r]
                nq, nk = NTOK[i], sum(w for _, w in band(i)[1])
                ac.wait_ge(at_max, r + 1)
                if r >= 2:
                    ac.wait_ge(at_pt, r - 1)
                ac.activation(pr[r % 2][0:nq, 0:nk], sc[r % 2][0:nq, 0:nk], ACT.Exp, bias=nmx[0:nq, r:r + 1],
                              accum_out=rsum[0:nq, r:r + 1]).then_inc(at_exp, 1)

            def move_probs(r):
                i, h = ROUNDS[r]
                nq, tiles = NTOK[i], band(i)[1]
                full = [w for _, w in tiles].count(P)
                ac.wait_ge(at_pt, r + 1)
                if r >= 2:
                    ac.wait_ge(at_pv, r - 1)
                last = ac.copy(pts[r % 2][:, 0:full * nq], psC[:, 0:full * nq])
                if full < len(tiles):
                    last = ac.copy(pts[r % 2][0:TS, full * nq:(full + 1) * nq], psC[0:TS, full * nq:(full + 1) * nq])
                last.then_inc(at_ptc, 1)

            def move_output(r):
                i, h = ROUNDS[r]
                pair, hh = divmod(h, 2)
                rows = slice(hh * 64, hh * 64 + 64)
                ac.wait_ge(at_pv, r + 1)
                ac.copy(mix[rows, Q + pair, tok(i)], psA[rows, 1024:1024 + NTOK[i]]).then_inc(at_ovc, 1)

            probs(0)
            for r in range(len(ROUNDS)):
                c, second = divmod(r, 2)
                if second and c < NT:
                    ssd_decay(c)
                if r == TAIL + 2:
                    group_squares(0)
                    group_squares(1)
                if r + 1 < len(ROUNDS):
                    probs(r + 1)
                if r in (TAIL + 2, TAIL + 3):
                    group_rms(r - TAIL - 2)
                if r == TAIL + 4:
                    ac.wait_ge(p5_pe, 1)
                    for m in range(2):
                        last = ac.copy(bbT[m].rearrange("p j n -> p (j n)"), psB[:, 2 * m * P:(2 * m + 2) * P])
                    last.then_inc(p5_act, 1)
                move_probs(r)
                move_output(r)
                if not second and c < NT:
                    ssd_ebc(c)
            for j in range(2):
                ac.wait_ge(s5_yd, NT)
                ac.activation(gel[:, j, :], gel[:, j, :], ACT.Gelu_apprx_tanh).then_inc(*glu_act.of(f"gelu{j}"))
            for j in range(2):
                ac.wait_ge(*glu_pe.at(0, f"gb{j}"))
                ac.activation(vc[:, j, :], AB[j][:, 0:T], ACT.Sigmoid, bias=col("glu_b", 2 + j)
                              ).then_inc(*glu_act.of(f"sig{j}"))
            for i in range(NT):
                M = NTOK[i]
                ac.wait_ge(*wo_dve.at(i, "add"))
                if i >= 2:
                    ac.wait_ge(tr_pe, i - 1)
                    ac.wait_ge(s_hst[i % 2], 16 * (i // 2))
                ac.activation(hn[i % 2][0:M, :], hres[0:M, i, :], ACT.Square, accum_out=ssum[0:M, i:i + 1]
                              ).then_inc(*wo_act.of("sq"))
                ac.wait_ge(*wo_act.at(i, "sq"))
                ac.activation(hrs[0:M, i:i + 1], ssum[0:M, i:i + 1], ACT.Ln, scale=1.0 / D, bias=col("eps")[0:M]
                              ).then_inc(*wo_act.of("ln"))
                ac.wait_ge(*wo_act.at(i, "ln"))
                ac.activation(hrs[0:M, i:i + 1], hrs[0:M, i:i + 1], ACT.Exp, scale=-0.5).then_inc(*wo_act.of("rs"))
                ac.wait_ge(tr_pe, i + 1)
                if i:
                    ac.wait_ge(lg_pe, i)
                ac.copy(hnT[:, :, 0:M], psC[:, :].rearrange("p (k n) -> p k n", k=KT)[:, :, 0:M]).then_inc(hte, 1)
                ac.wait_ge(lg_pe, i + 1)
                if i == 0:
                    ac.wait_ge(zeroed, 4)
                ac.copy(lgt[0:M, i, :], AB[i % 2][0:M, 1024:1060]).then_inc(lge, 1)
            ac.wait_ge(rt_dve, RT["d4"])
            ac.activation(prod[:, :, :, 0], d4, ACT.Exp).then_inc(rt_act, 1)
            ac.wait_ge(rt_dve, RT["dm"])
            ac.activation(gs, gs, ACT.Exp).then_inc(rt_act, 1)
            def activated(r, i):
                ac.wait_ge(m_gu[r], i + 2)
                ac.wait_ge(m_dn[r], i + 1)
                ac.activation(actg[r], psA[:, 0:FF], ACT.Silu).then_inc(m_sil[r], 1)

            def product_moved(r, i):
                ac.wait_ge(m_ht[r], i + 2)
                ac.copy(actg[r], psA[:, 1024:1536]).then_inc(m_hte[r], 1)

            def result_moved(r, i):
                ac.wait_ge(m_dn[r], i + 2)
                ac.wait_ge(m_free[r], i + 1)
                ac.copy(orow[r][:, 0:512], psB[:, 0:512]).then_inc(m_dnA[r], 1)

            def block_moves(r, i, first=False):
                activated(r, i)
                if not first:
                    result_moved(1 - r, i - 1 + r)
                product_moved(r, i)

            ac.wait_ge(rt_dve, RT["routed"])
            pairs = ac.value_load(npairs[0:1, :], min_val=1, max_val=BLOCKS // 2)
            block_moves(0, 0, first=True)
            block_moves(1, 0)
            with ac.Fori(1, BLOCKS // 2) as i:
                with ac.If(pairs > i):
                    for r in range(2):
                        block_moves(r, i)
            result_moved(1, pairs - 1)
            for i in range(NT):
                M = NTOK[i]
                ac.wait_ge(f_dve_sum, i + 1)
                ac.activation(sqrow[i % 2][0:M, :], fin[i % 3][0:M, 0:D], ACT.Square, accum_out=ssum[0:M, i:i + 1]
                              ).then_inc(*f_act.of("sq"))
                ac.wait_ge(*f_act.at(i, "sq"))
                ac.activation(hrs[0:M, i:i + 1], ssum[0:M, i:i + 1], ACT.Ln, scale=1.0 / D, bias=col("eps")[0:M]
                              ).then_inc(*f_act.of("ln"))
                ac.wait_ge(*f_act.at(i, "ln"))
                ac.activation(hrs[0:M, i:i + 1], hrs[0:M, i:i + 1], ACT.Exp, scale=-0.5).then_inc(*f_act.of("rs"))

        @block.vector
        def _(ve):
            ve.wait_ge(s_params, 48)
            ve.wait_ge(nrm_act.sem, KT + 2)
            for k in range(KT):
                ve.scalar_tensor_tensor(out=xn[:, k, :], in0=xn[:, k, :], scalar=col("g_mix", k), in1=psB[:, 0:T],
                                        op0=ALU.mult, op1=ALU.mult).then_inc(xn_dve, 1)
            n5 = [0]

            def link5(ins, name=None):
                ins.then_inc(p5_dve, 1)
                n5[0] += 1
                assert name is None or P5[name] == n5[0], (name, n5[0])
                ve.wait_ge(p5_dve, n5[0])

            def c5(n):
                return s5p[:, n, :]
            lre, lim = col("lam_re", 0, 8), col("lam_im", 0, 8)
            ve.wait_ge(p5_act, 1)
            link5(ve.tensor_tensor(c5(T0), lre, c5(DT), ALU.mult), "lrdt")
            link5(ve.tensor_tensor(c5(TH), lim, c5(DT), ALU.mult))
            link5(ve.tensor_scalar(c5(T1), c5(TH), 1.0 / (2 * math.pi), 12582912.0, ALU.mult, ALU.add))
            link5(ve.tensor_scalar(c5(T1), c5(T1), -12582912.0, None, ALU.add))
            link5(ve.scalar_tensor_tensor(out=c5(TH), in0=c5(T1), scalar=-6.28125, in1=c5(TH), op0=ALU.mult,
                                          op1=ALU.add))
            link5(ve.scalar_tensor_tensor(out=c5(TH), in0=c5(T1), scalar=-(2 * math.pi - 6.28125), in1=c5(TH),
                                          op0=ALU.mult, op1=ALU.add))
            link5(ve.tensor_scalar(c5(TH), c5(TH), 3.141592, -3.141592, ALU.min, ALU.max))
            link5(ve.scalar_tensor_tensor(out=c5(T1), in0=c5(TH), scalar=-1.0, in1=c5(TH), op0=ALU.mult, op1=ALU.max))
            link5(ve.tensor_scalar(c5(T1), c5(T1), -1.0, math.pi / 2, ALU.mult, ALU.add), "angles")
            ve.wait_ge(zeroed, 3)
            for n in range(2):
                j = A0 + n
                ve.wait_ge(proj, j + 1)
                ve.wait_ge(ev, EV_AT[TILES.index(("g", n))])
                ve.tensor_tensor(vb[:, n, DW - 1:DW - 1 + TP], AB[j % 2][:, 0:TP], sg[:, n, 0:TP], ALU.mult)
                ve.tensor_tensor(vb[:, n, VBW - TS:VBW], AB[j % 2][:, TP:T], sg[:, n, TP:T], ALU.mult
                                 ).then_inc(gated, 1)
            def tap(x, w, b, t, width, out, count, sample_out):
                for acc, dst, at, n, k in ((psC[:, 0:TP], out, 0, TP, 0),
                                           (sample_out, sample_out, TP + width - 1, TS, 1)):
                    if t == 0:
                        ins = ve.tensor_scalar(acc, x[:, at:at + n], w(0), b, ALU.mult, ALU.add)
                    else:
                        ve.wait_ge(count[0], count[1] + 2 * t - 1 + k)
                        ins = ve.scalar_tensor_tensor(out=dst if t == width - 1 else acc, in0=x[:, at + t:at + t + n],
                                                      scalar=w(t), in1=acc, op0=ALU.mult, op1=ALU.add)
                    ins.then_inc(count[0], 1)

            ve.wait_ge(gated, 2)
            ve.wait_ge(s_hist, 48)
            for j in range(2):
                if j:
                    ve.wait_ge(dw_dve, 2 * DW * j)
                for t in range(DW):
                    tap(vb[:, j, :], lambda t: col("dw_w", DW * j + t), col("dw_b", j), t, DW, vc[:, j, 0:TP],
                        (dw_dve, 2 * DW * j), vc[:, j, TP:T])

            def conv4(j):
                ve.wait_ge(ev, EV_AT[TILES.index(("xbc", j))])
                if j:
                    ve.wait_ge(cv_act, j)
                else:
                    ve.wait_ge(dw_dve, 2 * 2 * DW)
                for t in range(CW):
                    tap(xb[:, j, :], lambda t: col("conv_w", 4 * j + t), col("conv_b", j), t, CW, psC[:, 0:TP],
                        (cv_dve, 2 * CW * j), cvs[:, j, :])

            conv4(0)
            ve.wait_ge(p5_act, 4)
            link5(ve.tensor_tensor(c5(AR), c5(MAG), c5(COS), ALU.mult))
            link5(ve.tensor_tensor(c5(AI), c5(MAG), c5(SIN), ALU.mult))
            link5(ve.tensor_tensor(c5(T0), lre, lre, ALU.mult))
            link5(ve.tensor_tensor(c5(T1), lim, lim, ALU.mult))
            link5(ve.tensor_tensor(c5(T0), c5(T0), c5(T1), ALU.add))
            link5(ve.reciprocal(c5(T2), c5(T0)))
            link5(ve.scalar_tensor_tensor(out=c5(T0), in0=c5(AR), scalar=-1.0, in1=lre, op0=ALU.add, op1=ALU.mult))
            link5(ve.tensor_tensor(c5(T1), c5(AI), lim, ALU.mult))
            link5(ve.tensor_tensor(c5(T0), c5(T0), c5(T1), ALU.add))
            link5(ve.tensor_tensor(c5(CR), c5(T0), c5(T2), ALU.mult))
            link5(ve.scalar_tensor_tensor(out=c5(T0), in0=c5(AR), scalar=-1.0, in1=lim, op0=ALU.add, op1=ALU.mult))
            link5(ve.tensor_tensor(c5(T1), c5(AI), lre, ALU.mult))
            link5(ve.tensor_tensor(c5(T1), c5(T1), c5(T0), ALU.subtract))
            link5(ve.tensor_tensor(c5(CI), c5(T1), c5(T2), ALU.mult))
            link5(ve.tensor_copy(cosT[:, :, 0:1], c5(COS).unsqueeze(2)))
            link5(ve.tensor_copy(sinT[:, :, 0:1], c5(SIN).unsqueeze(2)))
            k = 1
            while k < P:
                cl = cosT[:, :, k - 1:k].broadcast_to([P, ST, k])
                sl = sinT[:, :, k - 1:k].broadcast_to([P, ST, k])
                lo, hi = slice(0, k), slice(k, 2 * k)
                link5(ve.tensor_tensor(tt[0][:, :, lo], cosT[:, :, lo], cl, ALU.mult))
                link5(ve.tensor_tensor(tt[1][:, :, lo], sinT[:, :, lo], sl, ALU.mult))
                link5(ve.tensor_tensor(cosT[:, :, hi], tt[0][:, :, lo], tt[1][:, :, lo], ALU.subtract))
                link5(ve.tensor_tensor(tt[0][:, :, lo], cosT[:, :, lo], sl, ALU.mult))
                link5(ve.tensor_tensor(tt[1][:, :, lo], sinT[:, :, lo], cl, ALU.mult))
                link5(ve.tensor_tensor(sinT[:, :, hi], tt[0][:, :, lo], tt[1][:, :, lo], ALU.add),
                      "tables" if k == 64 else None)
                k *= 2

            for j in range(1, 4):
                conv4(j)
            ve.wait_ge(*cm_pe.at(0, "mu"))
            for j in range(2):
                ve.scalar_tensor_tensor(out=vc[:, j, :], in0=psA[:, 0:T], scalar=-1.0 / 256, in1=vc[:, j, :],
                                        op0=ALU.mult, op1=ALU.add).then_inc(*cm_dve.of(f"cen{j}"))
            ve.wait_ge(*cm_act.at(0, "rs"))
            for j in range(2):
                ve.tensor_tensor(vc[:, j, :], vc[:, j, :], psB[:, 0:T], ALU.mult).then_inc(*cm_dve.of(f"n{j}"))
            ve.wait_ge(vd_ev, NT)
            ve.tensor_tensor(dtr, dtr, bc(col("dt_bias", 0, 4), 1, NT), ALU.add).then_inc(*dtp_dve.of("raw"))
            ve.wait_ge(*dtp_dve.at(0, "raw"))
            ve.scalar_tensor_tensor(out=dta, in0=dtr, scalar=-1.0, in1=dtr, op0=ALU.mult, op1=ALU.max
                                    ).then_inc(*dtp_dve.of("abs"))
            ve.wait_ge(*dtp_act.at(0, "aexp"))
            ve.scalar_tensor_tensor(out=dtt, in0=dtr, scalar=0.0, in1=dta, op0=ALU.max, op1=ALU.add
                                    ).then_inc(*dtp_dve.of("dt"))
            ve.wait_ge(*dtp_dve.at(0, "dt"))
            ve.scalar_tensor_tensor(out=aa, in0=dtt, scalar=-1.0, in1=bc(aexp, 1, NT), op0=ALU.mult, op1=ALU.mult
                                    ).then_inc(*dtp_dve.of("a"))
            ve.wait_ge(dtp_pe, 1)
            ve.tensor_scalar(nacs.rearrange("p i h -> p (i h)"), psC[:, 0:36], -1.0, None, ALU.mult
                             ).then_inc(*dtp_dve.of("nacs"))
            ve.wait_ge(*dtp_dve.at(0, "nacs"))
            ve.tensor_tensor(dec.rearrange("p i h -> p (i h)"), psC[:, 512:548], nacs.rearrange("p i h -> p (i h)"),
                             ALU.add).then_inc(*dtp_dve.of("decin"))

            def ssd_masked(c):
                L = NTOK[c]
                ve.wait_ge(*ssd_act.at(c, "ebc"))
                ve.tensor_tensor(dm[0:L, :, :], psB[0:L, 0:512].rearrange("p (h t) -> p h t", h=4),
                                 bc(negmask[0:L, :], 1, 4), ALU.add).then_inc(*ssd_dve.of("dm"))

            def ssd_operands(c):
                L = NTOK[c]
                ve.wait_ge(*ssd_act.at(c, "decay"))
                ve.wait_ge(*ssd_pe.at(c, "tr"))
                for g in range(2):
                    at = 512 * (1 + g)
                    last = ve.tensor_tensor(dm[0:L, 2 * g:2 * g + 2, 0:L], dm[0:L, 2 * g:2 * g + 2, 0:L],
                                            bc(psB[0:L, at:at + L], 1, 2), ALU.mult)
                last.then_inc(*ssd_dve.of("m"))
                if c:
                    ve.wait_ge(*ssd_pool.at(c - 1, "xdd"))
                if L < P:
                    ve.memset(xdt[L:P], 0.0)
                ve.tensor_tensor(xdt[0:L].rearrange("p (h d) -> p h d", h=4),
                                 psB[0:L, 640:896].rearrange("p (h d) -> p h d", h=4), bc(dtt[0:L, c, :], 2, 64),
                                 ALU.mult).then_inc(*ssd_dve.of("xdt"))
                ve.tensor_copy(btok[0:L, :], psB[0:L, 1152:1280]).then_inc(*ssd_dve.of("btok"))
                for g in range(2):
                    rows = slice(g * 64, g * 64 + 64)
                    last = ve.tensor_tensor(ce[rows, 2 * g:2 * g + 2, 0:L], bc(xb[rows, 3, tok(c)], 1, 2),
                                            ebc[rows, 2 * g:2 * g + 2, 0:L], ALU.mult)
                last.then_inc(*ssd_dve.of("ce"))

            def ssd_results(c):
                L = NTOK[c]
                ve.wait_ge(*ssd_pe.at(c, "st"))
                st = state[1 if c == NT - 1 else 0]
                for h in range(HEADS):
                    g, hh = divmod(h, 2)
                    rows, cols = slice(g * 64, g * 64 + 64), slice(hh * 64, hh * 64 + 64)
                    new = psB[rows, hh * 64:hh * 64 + 64]
                    if c == 0:
                        last = ve.tensor_copy(st[rows, cols], new)
                    else:
                        last = ve.scalar_tensor_tensor(out=st[rows, cols], in0=st[rows, cols],
                                                       scalar=etot[rows, c, h:h + 1], in1=new,
                                                       op0=ALU.mult, op1=ALU.add)
                last.then_inc(*ssd_dve.of("state"))
                for g in range(2):
                    at = 896 + 512 * g
                    last = ve.scalar_tensor_tensor(out=xb[:, g, tok(c)], in0=xb[:, g, tok(c)],
                                                   scalar=col("ssd_d", g), in1=psB[:, at:at + L],
                                                   op0=ALU.mult, op1=ALU.add)
                last.then_inc(*ssd_dve.of("yd"))

            def gated_output():
                ve.wait_ge(*ssd_dve.at(NT - 1, "yd"))
                for g in range(2):
                    ve.tensor_tensor(xb[:, g, 0:T], xb[:, g, 0:T], mix[:, Z + g, :], ALU.mult
                                     ).then_inc(*yg_dve.of(f"gate{g}"))

            def group_norm(g):
                ve.wait_ge(*yg_act.at(0, f"rs{g}"))
                ve.scalar_tensor_tensor(out=mix[:, Z + g, :], in0=xb[:, g, 0:T], scalar=col("norm_w", g),
                                        in1=psB[:, 0:T], op0=ALU.mult, op1=ALU.mult).then_inc(*yg_dve.of(f"norm{g}"))

            def biased(r):
                i, h = ROUNDS[r]
                _, tiles, b0 = band(i)
                nq, nk = NTOK[i], sum(w for _, w in tiles)
                ve.wait_ge(at_s, r + 1)
                if r >= 2:
                    ve.wait_ge(at_exp, r - 1)
                ve.scalar_tensor_tensor(out=sc[r % 2][0:nq, 0:nk], in0=psA[0:nq, 0:nk], scalar=ATT_SCALE,
                                        in1=bias[0:nq, h, b0:b0 + nk], op0=ALU.mult, op1=ALU.add).then_inc(at_add, 1)
                ve.wait_ge(at_add, r + 1)
                ve.tensor_reduce(nmx[0:nq, r:r + 1], sc[r % 2][0:nq, 0:nk], AX.X, ALU.max, negate=True
                                 ).then_inc(at_max, 1)

            def diagonal(r):
                nq = NTOK[ROUNDS[r][0]]
                ve.wait_ge(at_exp, r + 1)
                ve.reciprocal(rinv[0:nq, r:r + 1], rsum[0:nq, r:r + 1]).then_inc(at_rinv, 1)
                ve.wait_ge(at_rinv, r + 1)
                if r >= 2:
                    ve.wait_ge(at_pt, r - 1)
                ve.tensor_scalar(diag[r % 2][0:nq, 0:nq], ident[0:nq, 0:nq], rinv[0:nq, r:r + 1], None, ALU.mult
                                 ).then_inc(at_diag, 1)

            def s5_matrices():
                ve.wait_ge(proj, len(TILES))
                ve.wait_ge(s_s5w, 32)
                for m in range(2):
                    link5(ve.memset(bb[m], 0.0))
                    link5(ve.memset(cc[m], 0.0))
                t5 = [s5t[m].rearrange("p s t -> p (s t)")[:, 0:ST * 16].rearrange("p (s c) -> p s c", s=ST)
                      for m in range(2)]
                for m, op in ((0, ALU.subtract), (1, ALU.add)):
                    link5(ve.tensor_tensor(t5[0], s5w[:, m, :, :], bc(c5(CR), 2, 16), ALU.mult))
                    link5(ve.tensor_tensor(t5[1], s5w[:, 1 - m, :, :], bc(c5(CI), 2, 16), ALU.mult))
                    for g in range(2):
                        rows = slice(g * 64, g * 64 + 64)
                        link5(ve.tensor_tensor(bb[m][rows, :, g * 16:g * 16 + 16], t5[0][rows], t5[1][rows], op))
                for m, sgn in ((0, 1.0), (1, -1.0)):
                    for g in range(2):
                        rows = slice(g * 64, g * 64 + 64)
                        link5(ve.tensor_scalar(cc[m][rows, :, g * 16:g * 16 + 16], s5w[rows, 2 + m, :, :], sgn, None,
                                               ALU.mult), "bb" if m + g == 2 else None)

            def views(x, half, L):
                return x.rearrange("p (j q) t -> p q j t", j=2)[:, 2 * half:2 * half + 2, :, 0:L]

            def s5_result(c):
                L = NTOK[c]
                ve.wait_ge(s5_y, c + 1)
                for jt in range(2):
                    last = ve.scalar_tensor_tensor(out=gel[:, jt, tok(c)], in0=mix[:, UD + jt, tok(c)],
                                                   scalar=col("s5_d", jt),
                                                   in1=psB[:, 1024 + jt * P:1024 + jt * P + L],
                                                   op0=ALU.mult, op1=ALU.add)
                last.then_inc(s5_yd, 1)

            def s5_input(c, m):
                x = psB[:, 0:1024].rearrange("p (q j m t) -> p q j m t", q=2, j=2, m=2)
                return x[:, :, :, m, 0:NTOK[c]]

            def s5_turned(c, half):
                L = NTOK[c]
                ve.wait_ge(s5_x, 2 * c + half + 1)
                for dst, m, table in ((s5t[0], 0, cosT), (s5t[1], 1, sinT), (s5u[0], 1, cosT), (s5u[1], 0, sinT)):
                    last = ve.tensor_tensor(views(dst, half, L), s5_input(c, m), views(table, half, L), ALU.mult)
                last.then_inc(*s5_dve.of(f"half{half}"))

            def s5_added(c):
                L = NTOK[c]
                ve.wait_ge(*s5_dve.at(c, "half1"))
                ve.tensor_tensor(s5u[1][:, :, 0:L], s5u[0][:, :, 0:L], s5u[1][:, :, 0:L], ALU.subtract
                                 ).then_inc(*s5_dve.of("u1"))
                ve.wait_ge(*s5_dve.at(c, "u1"))
                ve.tensor_tensor(s5u[0][:, :, 0:L], s5t[0][:, :, 0:L], s5t[1][:, :, 0:L], ALU.add
                                 ).then_inc(*s5_dve.of("u0"))

            def s5_scanned(c):
                L = NTOK[c]
                ve.wait_ge(*s5_dve.at(c, "u0"))
                if c:
                    ve.wait_ge(*s5_pool.at(c - 1, "im"))
                r = 1 if c == NT - 1 else 0
                for s in range(ST):
                    for m in range(2):
                        if c == 0:
                            init = 0.0
                        elif c == NT - 1:
                            init = col("h0_re" if m == 0 else "h0_im", s)
                        else:
                            init = s5end[:, 0, m, s:s + 1]
                        last = ve.tensor_tensor_scan(s5g[m][:, s, 0:L], s5p[:, MAG, s:s + 1].broadcast_to([P, L]),
                                                     s5u[m][:, s, 0:L], init, ALU.mult, ALU.add)
                last.then_inc(*s5_dve.of("scan"))
                ve.wait_ge(*s5_dve.at(c, "scan"))
                ce_, se_ = cosT[:, :, L - 1], sinT[:, :, L - 1]
                gr, gi = s5g[0][:, :, L - 1], s5g[1][:, :, L - 1]
                for x, (p0, p1) in enumerate(((gr, ce_), (gi, se_), (gr, se_), (gi, ce_))):
                    last = ve.tensor_tensor(cmul[:, x, :], p0, p1, ALU.mult)
                last.then_inc(*s5_dve.of("carry"))
                ve.wait_ge(*s5_dve.at(c, "carry"))
                ve.tensor_tensor(s5end[:, r, 0, :], cmul[:, 0, :], cmul[:, 1, :], ALU.subtract)
                ve.tensor_tensor(s5end[:, r, 1, :], cmul[:, 2, :], cmul[:, 3, :], ALU.add).then_inc(*s5_dve.of("end"))
                ve.wait_ge(*s5_dve.at(c, "end"))

            ve.wait_ge(s_bias, 16)
            ve.wait_ge(cv_act, 4)
            biased(0)
            for r in range(len(ROUNDS)):
                c, second = divmod(r, 2)
                if r in S5_ROUND:
                    s5_turned(S5_ROUND[r], 0)
                if r + 1 < len(ROUNDS):
                    biased(r + 1)
                diagonal(r)
                if not second and 1 <= c <= NT:
                    ssd_results(c - 1)
                if second and c < NT:
                    ssd_operands(c)
                if not second and c < NT:
                    ssd_masked(c)
                if r == TAIL + 1:
                    gated_output()
                if r == TAIL + 2:
                    group_norm(0)
                if r == TAIL + 3:
                    group_norm(1)
                    s5_matrices()
                if r in S5_ROUND:
                    s5_turned(S5_ROUND[r], 1)
                    s5_added(S5_ROUND[r])
                    s5_scanned(S5_ROUND[r])
                    if S5_ROUND[r]:
                        s5_result(S5_ROUND[r] - 1)
            s5_result(NT - 1)
            for m in range(2):
                ve.wait_ge(*glu_pe.at(0, f"ga{m}"))
                ve.scalar_tensor_tensor(out=mix[:, UD + m, :], in0=AB[m][:, 0:T], scalar=col("glu_b", m),
                                        in1=vc[:, m, :], op0=ALU.add, op1=ALU.mult).then_inc(glu_dve, 1)
            for i in range(NT):
                M = NTOK[i]
                if i == 0:
                    ve.wait_ge(s_out, 16 * 10)
                    ve.wait_ge(s_gffn, 32)
                ve.wait_ge(wo_pe, i + 1)
                ve.wait_ge(s_xtok[i % 2], 16 * (i // 2 + 1))
                ve.tensor_tensor(hres[0:M, i, :], AB[i % 2][0:M, 0:D], xtok[i % 2][0:M, :], ALU.add
                                 ).then_inc(*wo_dve.of("add"))
                ve.wait_ge(*wo_act.at(i, "rs"))
                ve.scalar_tensor_tensor(out=hn[i % 2][0:M, :], in0=hres[0:M, i, :], scalar=hrs[0:M, i:i + 1],
                                        in1=gffn[0:M, :], op0=ALU.mult, op1=ALU.mult).then_inc(*wo_dve.of("hn"))
            nr = [0]

            def linkr(ins, name=None):
                ins.then_inc(rt_dve, 1)
                nr[0] += 1
                assert name is None or RT[name] == nr[0], (name, nr[0])
                ve.wait_ge(rt_dve, nr[0])

            def first(onehot, marks, order, best, n):
                linkr(ve.tensor_tensor(marks, marks, bc(order, 1, NT), ALU.mult))
                linkr(ve.tensor_reduce(best, marks, AX.X, ALU.max))
                linkr(ve.tensor_tensor(onehot, marks, bc(best, 2, n), ALU.is_equal))

            ve.wait_ge(lge, NT)
            l4 = lgt[:, :, 0:G]
            l32 = lgt[:, :, G:G + E].rearrange("p i (g e) -> p i g e", g=G)
            linkr(ve.tensor_reduce(m4, l4, AX.X, ALU.max))
            linkr(ve.tensor_tensor(d4, l4, bc(m4, 2, G), ALU.subtract), "d4")
            linkr(ve.tensor_scalar(ohg, d4, 0.0, None, ALU.is_ge))
            first(ohg, ohg, col("order4", 0, G), mm, G)
            ve.wait_ge(rt_act, 1)
            linkr(ve.tensor_reduce(pgr, prod[:, :, :, 0], AX.X, ALU.add))
            linkr(ve.reciprocal(pgr, pgr))
            linkr(ve.tensor_tensor(prod, l32, bc(ohg, 3, EPG), ALU.mult))
            linkr(ve.tensor_reduce(les, prod.rearrange("p i g e -> p i e g"), AX.X, ALU.add))
            linkr(ve.tensor_reduce(m1, les, AX.X, ALU.max))
            linkr(ve.tensor_tensor(t8, les, bc(m1, 2, EPG), ALU.is_ge))
            first(oh[0], t8, col("order8", 0, EPG), mm, EPG)
            linkr(ve.scalar_tensor_tensor(out=les, in0=oh[0], scalar=NEG, in1=les, op0=ALU.mult, op1=ALU.add))
            linkr(ve.tensor_reduce(m2, les, AX.X, ALU.max))
            linkr(ve.tensor_tensor(t8, les, bc(m2, 2, EPG), ALU.is_ge))
            first(oh[1], t8, col("order8", 0, EPG), mm, EPG)
            linkr(ve.tensor_tensor(gs, m2, m1, ALU.subtract), "dm")
            for k in range(2):
                linkr(ve.tensor_tensor(oe[k], bc(ohg, 3, EPG), bc(oh[k], 2, G), ALU.mult))
            linkr(ve.memset(oe[0][TS:P, NT - 1], 0.0))
            linkr(ve.memset(oe[1][TS:P, NT - 1], 0.0))
            flat = [x.rearrange("p i g e -> p i (g e)") for x in oe]
            linkr(ve.tensor_tensor(asg, flat[0], flat[1], ALU.add))
            linkr(ve.memset(pre[:, 0, :], 0.0))
            for i in range(NT):
                linkr(ve.tensor_tensor(pre[:, i + 1, :], pre[:, i, :], asg[:, i, :], ALU.add),
                      "pre" if i == NT - 1 else None)
            ve.wait_ge(rt_pe, 1)
            c3 = cmp[:, 0:E * THR].rearrange("p (e n) -> p e n", n=THR)
            linkr(ve.tensor_tensor(c3, bc(psB[:, 0:E], 2, THR), bc(col("thr", 0, THR), 1, E), ALU.is_gt))
            linkr(ve.tensor_reduce(nblk, c3, AX.X, ALU.add))
            linkr(ve.tensor_tensor_scan(bend, ones[:, 0:E], nblk, 0.0, ALU.mult, ALU.add))
            c2 = cmp[0:1, :].rearrange("p (b e) -> p b e", e=E)
            linkr(ve.tensor_tensor(c2, bc(bend[0:1, :], 1, BLOCKS), bc(col("iota", 0, BLOCKS)[0:1, :], 2, E), ALU.is_le))
            linkr(ve.tensor_reduce(eidf[0:1, :], c2, AX.X, ALU.add))
            linkr(ve.tensor_scalar(eidf[0:1, :], eidf[0:1, :], float(E - 1), None, ALU.min))
            linkr(ve.tensor_copy(eid[0:1, :], eidf[0:1, :]))
            even = col("iota", 0, BLOCKS)[0:1, :].rearrange("p (i two) -> p i two", two=2)[:, :, 0]
            linkr(ve.tensor_tensor(slotf[0:1, 0:BLOCKS // 2], even,
                                   bend[0:1, E - 1:E].broadcast_to([1, BLOCKS // 2]), ALU.is_lt))
            linkr(ve.tensor_reduce(slotf[0:1, BLOCKS:BLOCKS + 1], slotf[0:1, 0:BLOCKS // 2], AX.X, ALU.add))
            linkr(ve.tensor_copy(npairs[0:1, :], slotf[0:1, BLOCKS:BLOCKS + 1]), "routed")
            linkr(ve.tensor_tensor(base, bend, nblk, ALU.subtract))
            linkr(ve.tensor_scalar(base, base, float(P), -1.0, ALU.mult, ALU.add))
            linkr(ve.tensor_tensor(dmap, psA[:, 0:NT * E].rearrange("p (i e) -> p i e", e=E), bc(base, 1, NT),
                                   ALU.add))
            for k in range(2):
                linkr(ve.tensor_tensor(prod.rearrange("p i g e -> p i (g e)"), flat[k], dmap, ALU.mult))
                linkr(ve.tensor_reduce(destf[:, k, :], prod.rearrange("p i g e -> p i (g e)"), AX.X, ALU.add))
            linkr(ve.tensor_copy(dest, destf), "dest")
            ve.wait_ge(rt_act, 2)
            linkr(ve.tensor_scalar(m1, gs, 1.0, None, ALU.add))
            linkr(ve.reciprocal(m1, m1))
            linkr(ve.tensor_tensor(gate[0], m1, pgr, ALU.mult))
            linkr(ve.tensor_tensor(gate[1], gate[0], gs, ALU.mult))
            ve.wait_ge(s_slotin, 16)
            linkr(ve.tensor_copy(slotf[0:NB, :], slots_rows[0:NB, :]), "slotf")
            ve.wait_ge(rt_pe, 2)
            linkr(ve.tensor_copy(slotc, psC[:, 0:NB]))
            linkr(ve.tensor_scalar(slotm, slotc, float(T), float(-T), ALU.is_ge, ALU.mult))
            linkr(ve.tensor_tensor(slotm, slotm, slotc, ALU.add))
            ve.tensor_copy(slot_out, slotc)
            ve.tensor_copy(slot_in, slotm).then_inc(slots_ready, 1)
            ve.wait_ge(slots_ready, 1)

            def rows_moved(b, n):
                ve.wait_ge(m_xt[b], n + 1)
                ve.tensor_copy(xgT[b].rearrange("p k n -> p (k n)"), psC[:, :]).then_inc(m_xte[b], 1)

            def multiplied(r, i):
                ve.wait_ge(m_sil[r], i + 2)
                ve.wait_ge(m_ht[r], i + 1)
                ve.tensor_tensor(hmid[r], psA[:, 512:1024], actg[r], ALU.mult).then_inc(m_hm[r], 1)

            def result_half(r, i):
                ve.wait_ge(m_dn[r], i + 2)
                ve.wait_ge(m_free[r], i + 1)
                ve.tensor_copy(orow[r][:, 512:1024], psB[:, 512:1024]).then_inc(m_dnD[r], 1)

            def block_parts(r, i, first=False):
                multiplied(r, i)
                rows_moved(1 - r, i + 1 + r)
                if not first:
                    result_half(1 - r, i - 1 + r)

            rows_moved(0, 1)
            pairs = ve.value_load(npairs[0:1, :], min_val=1, max_val=BLOCKS // 2)
            block_parts(0, 0, first=True)
            block_parts(1, 0)
            ve.wait_ge(s_hst[0], 16 * 5)
            ve.wait_ge(s_hst[1], 16 * 4)
            for i in range(NT):
                for k in range(2):
                    last = ve.tensor_scalar(gdiag[i][k][0:NTOK[i], 0:NTOK[i]], ident[0:NTOK[i], 0:NTOK[i]],
                                            gate[k][0:NTOK[i], i:i + 1], None, ALU.mult)
            last.then_inc(f_diag, 1)
            with ve.Fori(1, BLOCKS // 2) as i:
                with ve.If(pairs > i):
                    for r in range(2):
                        block_parts(r, i)
            result_half(1, pairs - 1)
            ve.wait_ge(s_gfin, 16)
            ve.wait_ge(s_xg[0], 16 * pairs + 32)
            ve.wait_ge(s_xg[1], 16 * pairs + 16)

            def summed(i):
                M = NTOK[i]
                ve.wait_ge(f_pe, i + 1)
                ve.tensor_tensor(fin[i % 3][0:M, 0:D], fin[i % 3][0:M, 0:D], hres[0:M, i, :], ALU.add
                                 ).then_inc(f_dve_sum, 1)

            def final_norm(i):
                M = NTOK[i]
                ve.wait_ge(*f_act.at(i, "rs"))
                if i >= 3:
                    ve.wait_ge(s_yo[i % 3], 16 * (i // 3))
                ve.scalar_tensor_tensor(out=yrow[i % 3][0:M, :], in0=fin[i % 3][0:M, 0:D], scalar=hrs[0:M, i:i + 1],
                                        in1=gfin[0:M, :], op0=ALU.mult, op1=ALU.mult).then_inc(f_dve_y, 1)

            summed(0)
            for i in range(NT):
                if i + 1 < NT:
                    summed(i + 1)
                final_norm(i)

        @block.gpsimd
        def _(po):
            for x in (m_xt, m_xte, m_gu, m_sil, m_hm, m_ht, m_hte, m_dn, m_dnA, m_dnD, m_free):
                for k in range(2):
                    po.sem_inc(x[k], 1)
            po.memset(xb[:, :, 0:CW - 1], 0.0).then_inc(zeroed, 1)
            po.memset(vb[:, :, 0:DW - 1], 0.0).then_inc(zeroed, 1)
            po.memset(dtr, 0.0).then_inc(zeroed, 1)
            po.wait_ge(ev, EV_AT[TILES.index(("xbc", 3))])
            po.wait_ge(s_hist, 48)
            po.tensor_copy(tail[:, :, 0, :], xb[:, :, TP:TP + CW - 1])
            po.tensor_copy(tail[:, :, 1, :], xb[:, :, XBW - (CW - 1):XBW]).then_inc(tailed, 1)
            po.wait_ge(s_params, 48)
            po.wait_ge(*dtp_act.at(0, "etot"))
            po.wait_ge(*dtp_dve.at(0, "a"))
            for c in range(NT):
                L = NTOK[c]
                if c:
                    po.wait_ge(*ssd_pe.at(c - 1, "bc"))
                po.tensor_tensor(ua[0:L], bc(upper[0:L, :], 1, 4), bc(aa[0:L, c, :], 2, P), ALU.mult
                                 ).then_inc(*ssd_pool.of("ua"))
                po.wait_ge(*ssd_dve.at(c, "xdt"))
                if c:
                    po.wait_ge(*ssd_pe.at(c - 1, "st"))
                po.tensor_tensor(xdd[0:L].rearrange("p (h d) -> p h d", h=4),
                                 xdt[0:L].rearrange("p (h d) -> p h d", h=4), bc(dec[0:L, c, :], 2, 64), ALU.mult
                                 ).then_inc(*ssd_pool.of("xdd"))
            po.wait_ge(p5_dve, P5["tables"])
            for c in range(NT):
                L = NTOK[c]
                po.wait_ge(*s5_dve.at(c, "scan"))
                if c:
                    po.wait_ge(s5_y, c)
                x = [t[:, :, 0:L] for t in (s5g[0], s5g[1], cosT, sinT, s5v[0], s5v[1], s5h[0], s5h[1])]
                po.tensor_tensor(x[4], x[0], x[2], ALU.mult)
                po.tensor_tensor(x[5], x[1], x[3], ALU.mult).then_inc(*s5_pool.of("m0"))
                po.wait_ge(*s5_pool.at(c, "m0"))
                po.tensor_tensor(x[6], x[4], x[5], ALU.subtract).then_inc(*s5_pool.of("re"))
                po.wait_ge(*s5_pool.at(c, "re"))
                po.tensor_tensor(x[4], x[0], x[3], ALU.mult)
                po.tensor_tensor(x[5], x[1], x[2], ALU.mult).then_inc(*s5_pool.of("m1"))
                po.wait_ge(*s5_pool.at(c, "m1"))
                po.tensor_tensor(x[7], x[4], x[5], ALU.add).then_inc(*s5_pool.of("im"))
            po.wait_ge(*s5_pool.at(NT - 1, "im"))
            po.wait_ge(*s5_dve.at(NT - 1, "end"))
            po.memset(lgt[:, NT - 1, :], 0.0).then_inc(zeroed, 1)
            po.memset(curidx[0], 0).then_inc(rt_pool, 1)
            po.iota(slots_rows[0:NB, :], [[1, P]], base=2 * T, channel_multiplier=0).then_inc(rt_pool, 1)
            po.wait_ge(rt_pool, 2)
            po.dma_start(slot_dram.rearrange("(b p) o -> b (p o)", p=P), slots_rows[0:NB, :]).then_inc(s_slotz, 16)
            po.wait_ge(rt_dve, RT["dest"])
            po.wait_ge(s_slotz, 16)
            for k in range(2):
                for i in range(NT):
                    M = NTOK[i]
                    po.indirect_dma_start(slot_dram, bass.IndirectOffsetOnAxis(ap=dest[0:M, k, i:i + 1], axis=0),
                                          asgid[0:M, k, i:i + 1], None).then_inc(s_scat, 16)
            po.wait_ge(s_scat, 16 * 2 * NT)
            po.dma_start(slots_rows[0:NB, :], slot_dram.rearrange("(b p) o -> b (p o)", p=P)).then_inc(s_slotin, 16)
            po.wait_ge(slots_ready, 1)
            po.wait_ge(s_hst[0], 16 * 5)
            po.wait_ge(s_hst[1], 16 * 4)

            last_in, last_out = po.to_reg(T - 1), po.to_reg(2 * T - 1)

            def gather(b, n, blk):
                po.wait_ge(m_xt[b], n + 1)
                po.tensor_copy(curidx[b], slot_in[:, blk:blk + 1] if isinstance(blk, int) else slot_in[:, ds(blk, 1)]
                               ).then_inc(idxc, 1)
                po.wait_ge(idxc, blk + 1)
                po.sem_inc(indirect_go, 1)
                po.indirect_dma_start(xg[b], None, hn_dram, bass.IndirectOffsetOnAxis(ap=curidx[b], axis=0),
                                      bounds_check=last_in, oob_is_err=False).then_inc(s_xg[b], 16)

            def scatter(r, i, blk, freed=True):
                po.wait_ge(m_dnA[r], i + 2)
                po.wait_ge(m_dnD[r], i + 2)
                po.tensor_copy(curout[r], slot_out[:, ds(blk, 1)]).then_inc(outc, 1)
                po.wait_ge(outc, blk + 1)
                po.sem_inc(indirect_go, 1)
                po.indirect_dma_start(out_dram, bass.IndirectOffsetOnAxis(ap=curout[r], axis=0), orow[r], None,
                                      bounds_check=last_out, oob_is_err=False).then_inc(s_os[r], 16)
                if freed:
                    po.wait_ge(s_os[1 - r], 16 * (i + r))
                    po.sem_inc(m_free[1 - r], 1)

            gather(0, 0, 0)
            pairs = po.value_load(npairs[0:1, :], min_val=1, max_val=BLOCKS // 2)
            gather(1, 0, 1)
            gather(0, 1, 2)
            gather(1, 1, 3)
            gather(0, 2, 4)
            scatter(0, 0, 0, freed=False)
            with po.Fori(1, BLOCKS // 2) as i:
                with po.If(pairs > i):
                    gather(1, i + 1, 2 * i + 3)
                    scatter(1, i - 1, 2 * i - 1)
                    gather(0, i + 2, 2 * i + 4)
                    scatter(0, i, 2 * i)
            scatter(1, pairs - 1, 2 * pairs - 1, freed=False)


_OUTS = {"y_p": (TP, D), "y_s": (TS, D), "ssd_p": (P, P), "ssd_s": (P, P), "ssd_tail": (P, 24),
         "ccm_p": (P, 2, DW - 1), "ccm_s": (P, 2, DW - 1), "k_p": (P, 2, WIN), "k_s": (P, 2, TS),
         "v_p": (P, 4, 256), "v_s": (TS, 256), "s5_end": (P, 4 * ST)}


def _pack(x):
    import numpy as np

    x = {n: np.asarray(v) for n, v in x.items()}

    def chan(v, n):
        return np.moveaxis(v.reshape((n, P) + v.shape[1:]), 0, 1)

    def states(v):
        return np.moveaxis(v.reshape((ST, P) + v.shape[2:]), 0, 1)

    def every(v):
        return np.broadcast_to(v.reshape(1, -1), (P, v.size))
    w_in = x["w_in"][0]
    at = {"z": 0, "xbc": 256, "a": 772, "g": 1028, "q": 1284, "k": 1540, "ud": 2052}
    order = [("g", 0), ("g", 1), ("a", 0), ("a", 1)] + [("xbc", j) for j in range(4)] + \
            [(n, j) for n in ("k", "q", "z", "ud") for j in range(2)]
    f = np.float32
    parts = {
        "g_mix": chan(x["g_mix"][0], 8), "conv_w": chan(x["ssd_conv_w"][0].T, 4), "conv_b": chan(x["ssd_conv_b"][0], 4),
        "dw_w": chan(x["ccm_dw_w"][0].T, 2), "dw_b": chan(x["ccm_dw_b"][0], 2), "ln_g": chan(x["ccm_ln_g"][0], 2),
        "ln_b": chan(x["ccm_ln_b"][0], 2), "pw_b": chan(x["ccm_pw_b"][0], 2),
        "ssd_d": chan(np.repeat(x["ssd_d"][0], HD), 2), "norm_w": chan(x["ssd_norm_w"][0], 2),
        "glu_b": chan(x["s5_glu_b"][0], 4), "lam_re": states(x["s5_lam_re"][0]), "lam_im": states(x["s5_lam_im"][0]),
        "log_dt": states(np.repeat(x["s5_log_dt"][0][:, None], 64, 1)), "h0_re": states(x["state_s5_re"][0, 0]),
        "h0_im": states(x["state_s5_im"][0, 0]), "s5_d": chan(x["s5_d"][0].reshape(256), 2),
        "dt_bias": every(x["ssd_dt_bias"][0]), "a_log": every(x["ssd_a_log"][0]),
        "eps": np.full((P, 1), EPS, f), "one": np.ones((P, 1), f),
        "thr": every(np.arange(THR, dtype=f) * P), "iota": every(np.arange(BLOCKS, dtype=f)),
        "order4": every(np.arange(G, 0, -1).astype(f)), "order8": every(np.arange(EPG, 0, -1).astype(f)),
    }
    j, t = np.arange(P)[:, None], np.arange(P)[None, :]
    mats = np.concatenate([np.eye(P, dtype=f), np.ones((P, P), f), (j <= t).astype(f),
                           np.where(j > t, f(NEG), f(0))], axis=1)
    q, c = np.arange(P)[:, None], np.arange(BANDW)[None, :]
    seen = (c // 64 <= q // 64 + 8) & (c // 64 >= q // 64)
    idx = np.where(seen, np.clip(WIN + q - c, -128, 128) + 128, 257)
    table = np.concatenate([x["att_rel_bias"][0], np.full((HEADS, 1), NEG, f)], axis=1)
    s5w = [states(x[n][0]) for n in ("s5_b_re", "s5_b_im")] + \
          [states(np.moveaxis(x[n][0], 1, 2)) for n in ("s5_c_re", "s5_c_im")]
    rows = np.concatenate([x["x_prompt"][0], x["x_sample"][0]], axis=0)
    return {
        "params": np.concatenate([parts[n].reshape(P, w) for n, w in FIELDS], axis=1),
        "mats": mats, 
        "asgid": (np.arange(2)[None, :, None] * T + np.arange(NT)[None, None, :] * P + j[:, :, None]).astype(np.int32),
        "xT": rows.T, "x_rows": rows,
        "w_cm": np.stack([np.moveaxis(w_in[:, at[n] + i * P:at[n] + (i + 1) * P].reshape(KT, P, P), 0, 1).reshape(P, D)
                          for n, i in order]),
        "w_vd": chan(np.concatenate([w_in[:, 1796:2052], w_in[:, 768:772]], axis=1), KT),
        "ssd_hist": chan(x["state_ssd_conv"][0, 0].T, 4), "ccm_hist": chan(x["state_ccm_conv"][0, 0].T, 2),
        "ssd_h0": x["state_ssd"][0, 0].reshape(2, 2, HD, 64).transpose(0, 3, 1, 2).reshape(P, P),
        "k_cache": chan(x["cache_att_k"][0, 0].reshape(WIN, 256).T, 2),
        "v_cache": chan(x["cache_att_v"][0, 0].reshape(WIN, 256), 4),
        "bias": np.moveaxis(table[:, idx], 0, 1), "pw_w": chan(x["ccm_pw_w"][0], 2),
        "s5_w": np.stack(s5w, axis=1).reshape(P, -1), "glu_w": chan(x["s5_glu_w"][0], 2),
        "w_out": chan(x["w_out"][0], KT), "g_ffn": every(x["g_ffn"][0]), "g_final": every(x["g_final"]),
        "w_route": chan(np.concatenate([x["moe_w_group"][0], np.moveaxis(x["moe_w_expert"][0], 0, 1).reshape(D, E)],
                                       axis=1), KT),
        "w_gate": x["moe_w_gate"][0], "w_up": x["moe_w_up"][0], "w_down": x["moe_w_down"][0],
    }


def kernel(**inputs):
    import numpy as np
    import concourse.bacc as bacc
    from concourse.bass_utils import run_bass_kernel_spmd

    nc = bacc.Bacc("TRN2", target_bir_lowering=False, num_devices=1)
    arrays, a, o = {}, {}, {}
    for name, v in _pack(inputs).items():
        arrays["in_" + name] = v = np.ascontiguousarray(v)
        a[name] = nc.dram_tensor("in_" + name, v.shape, mybir.dt.from_np(v.dtype), kind="ExternalInput").ap()
    for name, shape in _OUTS.items():
        o[name] = nc.dram_tensor("out_" + name, shape, F32, kind="ExternalOutput").ap()
    encoder_step(nc, a, o)
    res = run_bass_kernel_spmd(nc, [arrays], core_ids=[0]).results[0]
    r = {name: np.asarray(res["out_" + name]).reshape(shape) for name, shape in _OUTS.items()}

    def state(v):
        return np.ascontiguousarray(v.reshape(2, 64, 2, HD).transpose(0, 2, 3, 1)).reshape(1, 1, 4, HD, 64)

    def rows(v, w):
        return np.ascontiguousarray(np.moveaxis(v, 0, 1).reshape(-1, w).T)
    tail = r["ssd_tail"].reshape(P, 4, 2, 3)
    end = r["s5_end"].reshape(P, 2, 2, ST)

    def s5(s, m):
        return np.ascontiguousarray(end[:, s, m, :].T).reshape(1, 1, 16, 64)
    return (r["y_p"].reshape(1, TP, D), r["y_s"].reshape(1, TS, D), state(r["ssd_p"]), state(r["ssd_s"]),
            rows(tail[:, :, 0], 3).reshape(1, 1, 3, 512), rows(tail[:, :, 1], 3).reshape(1, 1, 3, 512),
            rows(r["ccm_p"], DW - 1).reshape(1, 1, DW - 1, 256), rows(r["ccm_s"], DW - 1).reshape(1, 1, DW - 1, 256),
            rows(r["k_p"], WIN).reshape(1, 1, WIN, 4, HD), rows(r["k_s"], TS).reshape(1, 1, TS, 4, HD),
            np.ascontiguousarray(np.moveaxis(r["v_p"], 0, 1)).reshape(1, 1, WIN, 4, HD),
            r["v_s"].reshape(1, 1, TS, 4, HD), s5(0, 0), s5(1, 0), s5(0, 1), s5(1, 1))
```

```python
import math
from contextlib import ExitStack

import concourse.bass as bass
from concourse import mybir

F32 = mybir.dt.float32
I32 = mybir.dt.int32
ALU = mybir.AluOpType
ACT = mybir.ActivationFunctionType
AX = mybir.AxisListType
ds = bass.ds

P = 128
D = 1024
KT = D // P
TP, TS = 1024, 64
T = TP + TS
NT = TP // P + 1
NTOK = [P] * (NT - 1) + [TS]
HEADS, HD = 4, 64
EPS = 1e-6
ATT_SCALE = HD ** -0.5
WIN = 512
BANDW = WIN + P
CW, DW = 4, 31
XBW = (CW - 1) + TP + (CW - 1) + TS
VBW = (DW - 1) + TP + (DW - 1) + TS
VD = 260
ST = 8
NEG = -1e30
G, EPG = 4, 8
E = G * EPG
FF = 512
THR = -(-T // P)
BLOCKS = 48
NB = BLOCKS + 3

FIELDS = [("g_mix", 8), ("conv_w", 16), ("conv_b", 4), ("dw_w", 62), ("dw_b", 2), ("ln_g", 2), ("ln_b", 2),
          ("pw_b", 2), ("ssd_d", 2), ("norm_w", 2), ("glu_b", 4), ("lam_re", 8), ("lam_im", 8), ("log_dt", 8),
          ("h0_re", 8), ("h0_im", 8), ("s5_d", 2), ("dt_bias", 4), ("a_log", 4), ("eps", 1), ("one", 1),
          ("asg_row", 2 * NT), ("thr", THR), ("iota", P), ("order4", G), ("order8", EPG)]
COL, NCOL = {}, 0
for _n, _w in FIELDS:
    COL[_n] = (NCOL, _w)
    NCOL += _w


P5 = {"lrdt": 1, "angles": 9, "tables": 67, "bb": 86}
P5A = {"bbT": 5}
RT = {"d4": 2, "dm": 22, "pre": 37, "routed": 47}


class Steps:

    def __init__(self, sem, *names):
        self.sem, self.names, self.n = sem, names, 0

    def of(self, name):
        assert self.names[self.n % len(self.names)] == name, (self.names, name)
        self.n += 1
        return self.sem, 1

    def at(self, rnd, name):
        return self.sem, rnd * len(self.names) + self.names.index(name) + 1


def encoder_step(nc, a, o):
    with ExitStack() as ctx:
        def sb(name, cols, dt=F32):
            return ctx.enter_context(nc.sbuf_tensor(name, [P, cols], dt))

        def sem(name):
            return ctx.enter_context(nc.semaphore(name))

        def steps(name, *names):
            return Steps(sem(name), *names)

        def bc(x, axis, n):
            x = x.unsqueeze(axis)
            return x.broadcast_to([n if d == axis else s for d, s in enumerate(x.shape)])

        hn_dram = nc.dram_tensor("hn_rows", [T, D], F32, kind="Internal").ap()
        out_dram = nc.dram_tensor("expert_rows", [2 * T, D], F32, kind="Internal").ap()

        arena1 = sb("arena1", 24576)
        arena2 = sb("arena2", NT * D)
        arena3 = sb("arena3", KT * T)
        arena4 = sb("arena4", 6400)
        cst = sb("params", NCOL)
        mats = sb("mats", 4 * P)
        small = sb("small", 1150)
        tables = sb("phase_tables", 2 * ST * P)
        ints = sb("ints", BLOCKS + 2 * NB + 5, I32)

        def col(name, i=0, n=1):
            return cst[:, COL[name][0] + i:COL[name][0] + i + n]

        ident, ones, upper, negmask = (mats[:, i * P:(i + 1) * P] for i in range(4))

        class Arena:
            def __init__(self, t, at=0):
                self.t, self.at = t, at

            def take(self, n):
                self.at += n
                return self.t[:, self.at - n:self.at]

        a1 = Arena(arena1)
        xn = a1.take(KT * T).rearrange("p (k t) -> p k t", k=KT)
        wring = a1.take(4 * D).rearrange("p (r n) -> p r n", r=4)
        wvd = a1.take(KT * VD).rearrange("p (k n) -> p k n", k=KT)
        xb = a1.take(4 * XBW).rearrange("p (j t) -> p j t", j=4)
        sg = a1.take(2 * T).rearrange("p (j t) -> p j t", j=2)
        vc = a1.take(2 * T).rearrange("p (j t) -> p j t", j=2)
        pww = a1.take(2 * 256).rearrange("p (k n) -> p k n", k=2)
        cvs = a1.take(4 * TS).rearrange("p (j t) -> p j t", j=4)
        s5 = Arena(arena1)

        def s5take():
            return s5.take(D).rearrange("p (s t) -> p s t", s=ST)
        s5u, s5g, s5t, s5h = ([s5take(), s5take()] for _ in range(4))
        s5v = [vc[:, 0, 0:D].rearrange("p (s t) -> p s t", s=ST),
               vc[:, 1, 0:D].rearrange("p (s t) -> p s t", s=ST)]
        s5back = s5v + s5h
        s5m = Arena(arena1, KT * T)
        cc = [s5m.take(ST * 32).rearrange("p (s c) -> p s c", s=ST) for _ in range(3)]
        bbT = [s5m.take(2 * P).rearrange("p (j n) -> p j n", j=2) for _ in range(2)]
        glu_w = s5m.take(2 * 512).rearrange("p (k n) -> p k n", k=2)
        gel = sg
        w_out = s5m.take(KT * D).rearrange("p (k n) -> p k n", k=KT)
        moe_w = arena1[:, :].rearrange("p (r n) -> p r n", r=2)
        wg = [moe_w[:, r, 0:4096].rearrange("p (k n) -> p k n", k=KT) for r in range(2)]
        wu = [moe_w[:, r, 4096:8192].rearrange("p (k n) -> p k n", k=KT) for r in range(2)]
        wd = [moe_w[:, r, 8192:12288].rearrange("p (k n) -> p k n", k=4) for r in range(2)]

        a2 = Arena(arena2)
        kt = a2.take(2 * 1600).rearrange("p (j t) -> p j t", j=2)
        vt = a2.take(13 * 256).rearrange("p (j n) -> p j n", j=13)
        vb = a2.take(2 * VBW).rearrange("p (j t) -> p j t", j=2)
        hres = arena2[:, :].rearrange("p (i n) -> p i n", i=NT)

        mix = arena3[:, :].rearrange("p (k t) -> p k t", k=KT)
        Z, CA, Q, UD = 0, 2, 4, 6
        a3 = Arena(arena3)
        xg = [a3.take(D) for _ in range(2)]
        xgT = [a3.take(D).rearrange("p (k n) -> p k n", k=KT) for _ in range(2)]
        actg = [a3.take(FF) for _ in range(2)]
        hmid = [a3.take(FF) for _ in range(2)]
        orow = [a3.take(D) for _ in range(2)]

        a4 = Arena(arena4)
        bias = a4.take(HEADS * BANDW).rearrange("p (h k) -> p h k", h=HEADS)
        sc, pr, pts = ([a4.take(BANDW) for _ in range(2)] for _ in range(3))
        sq = [arena4[:, i * T:(i + 1) * T] for i in range(4)]
        rms = arena4[:, 0:T]
        turns = Arena(arena4, HEADS * BANDW)
        tt = [turns.take(ST * 64).rearrange("p (s t) -> p s t", s=ST) for _ in range(2)]
        bb = [turns.take(ST * 32).rearrange("p (s c) -> p s c", s=ST) for _ in range(2)]
        t5 = [turns.take(ST * 16).rearrange("p (s c) -> p s c", s=ST) for _ in range(2)]
        s5raw = turns.take(4 * ST * 16)
        s5w = s5raw.rearrange("p (m s c) -> p m s c", m=4, s=ST)
        w4 = Arena(arena1)
        ua, ebc, dm, ce = (w4.take(512).rearrange("p (h t) -> p h t", h=4) for _ in range(4))
        xdt = w4.take(256)
        xdd = w4.take(256)
        btok = w4.take(P)
        v4 = Arena(arena4)
        xtok = [v4.take(D) for _ in range(2)]
        hn = [v4.take(D) for _ in range(2)]
        gffn = v4.take(D)
        hnT = v4.take(D).rearrange("p (k n) -> p k n", k=KT)
        sigm = [arena4[:, at:at + T] for at in (2 * D, 5 * D)]
        f4 = Arena(arena4)
        gfin = f4.take(D)
        gdiag = [[f4.take(P) for _ in range(2)] for _ in range(NT)]
        f1 = Arena(arena1)
        og = [[f1.take(D) for _ in range(2)] for _ in range(NT)]
        f3 = Arena(arena3)
        yrow = [f3.take(D) for _ in range(3)]
        sqrow = [f3.take(D) for _ in range(2)]

        sm = Arena(small)
        dtr, dta, dtt, aa, nacs, dec, etot = (
            sm.take(NT * 4).rearrange("p (i h) -> p i h", h=4) for _ in range(7))
        aexp = sm.take(4)
        state = [sm.take(P) for _ in range(2)]
        tail = sm.take(24).rearrange("p (j s w) -> p j s w", j=4, s=2)
        nmx, rsum, rinv = (sm.take(NT * HEADS) for _ in range(3))
        s5p = sm.take(16 * ST).rearrange("p (n s) -> p n s", s=ST)
        s5end = sm.take(2 * 2 * ST).rearrange("p (r c s) -> p r c s", r=2, c=2)
        cmul = sm.take(4 * ST).rearrange("p (n s) -> p n s", s=ST)
        ssum, hrs = sm.take(NT), sm.take(NT)
        diag = [sm.take(P) for _ in range(2)]
        DT, MAG, TH, COS, SIN, AR, AI, CR, CI, T0, T1, T2 = range(12)

        cosT = tables[:, 0:ST * P].rearrange("p (s t) -> p s t", s=ST)
        sinT = tables[:, ST * P:].rearrange("p (s t) -> p s t", s=ST)
        rt = Arena(tables)
        rw = rt.take(KT * 36).rearrange("p (k n) -> p k n", k=KT)
        lgt = rt.take(NT * 36).rearrange("p (i n) -> p i n", i=NT)
        ohg = rt.take(NT * G).rearrange("p (i g) -> p i g", g=G)
        d4 = rt.take(NT * G).rearrange("p (i g) -> p i g", g=G)
        les = rt.take(NT * EPG).rearrange("p (i e) -> p i e", e=EPG)
        oh = [rt.take(NT * EPG).rearrange("p (i e) -> p i e", e=EPG) for _ in range(2)]
        t8 = rt.take(NT * EPG).rearrange("p (i e) -> p i e", e=EPG)
        m4, mm, m1, m2, pgr, gs = (rt.take(NT) for _ in range(6))
        gate = [rt.take(NT) for _ in range(2)]
        destf = rt.take(2 * NT).rearrange("p (k i) -> p k i", k=2)
        nblk, bend, base = (rt.take(E) for _ in range(3))
        eidf = rt.take(BLOCKS)
        slotf = rt.take(BLOCKS + 1)
        blkf, lowf = (rt.take(2 * NT).rearrange("p (k i) -> p k i", k=2) for _ in range(2))
        slotc = rt.take(NB)
        slotm = rt.take(NB)
        rb = Arena(arena1, 2 * KT * FF)
        prod = rb.take(NT * E).rearrange("p (i g e) -> p i g e", g=G, e=EPG)
        oe = [rb.take(NT * E).rearrange("p (i g e) -> p i g e", g=G, e=EPG) for _ in range(2)]
        asg = rb.take(NT * E).rearrange("p (i e) -> p i e", e=E)
        pre = rb.take((NT + 1) * E).rearrange("p (i e) -> p i e", e=E)
        dmap = rb.take(NT * E).rearrange("p (i e) -> p i e", e=E)
        cmp = rb.take(BLOCKS * E)
        sb1 = Arena(arena1, arena1.shape[1] // 2)
        in_low, in_blk = ([sb1.take(w) for _ in range(2 * NT)] for w in (P, NB))
        ia = Arena(ints)
        eid = ia.take(BLOCKS)
        npairs = ia.take(1)
        slot_out = ia.take(NB)
        slot_in = ia.take(NB)
        curidx = [ia.take(1) for _ in range(2)]
        curout = [ia.take(1) for _ in range(2)]

        psA = ctx.enter_context(nc.psum_tensor("psA", [P, 1536], F32))
        psB = ctx.enter_context(nc.psum_tensor("psB", [P, 1536], F32))
        psC = ctx.enter_context(nc.psum_tensor("psC", [P, 1024], F32))
        AB = [psA, psB]
        fin = [psA, psB, psC]
        hps = [psC] + [AB[i % 2] for i in range(1, NT)]
        CH = [(0, 512), (512, 1024), (1024, T)]

        s_params, s_hist, s_cache, s_bias = sem("params_in"), sem("histories_in"), sem("cache_in"), sem("bias_in")
        s_x = [sem(f"x{k}_in") for k in range(KT)]
        s_w = [sem(f"w_in_slot{k}") for k in range(4)]
        s_wvd, s_s5w, s_gluw, s_pww = sem("w_vdt_in"), sem("s5_weights_in"), sem("glu_weights_in"), sem("pointwise_in")
        s_out = sem("states_out")
        s_wout, s_gffn = sem("w_out_in"), sem("g_ffn_in")
        s_xtok = [sem(f"x_rows{k}_in") for k in range(2)]
        s_hst = [sem(f"hn_rows{k}_out") for k in range(2)]
        s_wgu = [sem(f"gate_up{k}_in") for k in range(2)]
        s_wd = [sem(f"down{k}_in") for k in range(2)]
        s_xg = [sem(f"gathered{k}") for k in range(2)]
        s_os = [sem(f"expert_rows{k}_out") for k in range(2)]
        s_og = [sem(f"expert_rows{i}_back") for i in range(NT)]
        s_yo, s_gfin = [sem(f"y_rows{k}_out") for k in range(3)], sem("g_final_in")
        zeroed = sem("buffers_zeroed")
        nrm_act = steps("norm_act", *["sq"] * KT, "ln_s", "ln", "rs")
        nrm_pe = sem("norm_pe")
        sq_pairs = sem("square_pairs")
        xg_dve, xn_dve, x_used = sem("scaled_input"), sem("xn_ready"), sem("scaled_input_used")
        g_moved, g_sig = sem("gate_tiles_moved"), sem("gate_sigmoids")
        proj = sem("proj_done")
        ev = sem("proj_moved")
        gated = sem("conv_input_gated")
        vd_pe, vd_ev = sem("vdt_done"), sem("vdt_moved")
        dtp_dve = steps("dt_dve", "raw", "abs", "dt", "a", "nacs", "decin")
        dtp_act = steps("dt_act", "e", "ln", "aexp", "dec", "etot")
        dtp_pe = sem("dt_cumsums")
        cv_dve = sem("conv4_taps")
        cv_act = sem("conv4_silu")
        tailed = sem("conv_tail_copied")
        ssd_pe = steps("ssd_pe", "bc", "tr", "y", "st")
        ssd_act = steps("ssd_act", "ebc", "decay")
        ssd_dve = steps("ssd_dve", "dm", "m", "xdt", "btok", "ce", "state", "yd")
        ssd_pool = steps("ssd_pool", "ua", "xdd")
        yg_dve = steps("ssd_out_dve", "norm0", "norm1")
        ssd_gated = sem("ssd_gated")
        yg_act = steps("ssd_out_act", "sq0", "sq1", "ln0", "ln1", "rs0", "rs1")
        yg_pe = sem("ssd_out_pe")
        dw_dve = sem("dwconv_taps")
        cm_act = steps("ccm_act", "sq0", "sq1", "ln", "rs", "silu0", "silu1", "out0", "out1")
        cm_pe = steps("ccm_pe", "mu", "var", "pw0", "pw1")
        cm_dve = steps("ccm_dve", "cen0", "cen1", "n0", "n1")
        at_s, at_pt, at_pv = sem("att_scores"), sem("att_probsT"), sem("att_out")
        at_add, at_max, at_rinv, at_diag = sem("att_biased"), sem("att_max"), sem("att_rinv"), sem("att_diag")
        at_exp, at_ptc, at_ovc = sem("att_exp"), sem("att_probsT_moved"), sem("att_out_moved")
        p5_dve, p5_act, p5_pe = sem("s5_setup_dve"), sem("s5_setup_act"), sem("s5_setup_pe")
        s5_x, s5_y = sem("s5_inputs"), sem("s5_outputs")
        s5_dve = steps("s5_dve", "half0", "half1", "u1", "scan", "carry", "end")
        s5_yd = sem("s5_y_moved")
        s5_pool = steps("s5_pool", "u0", "m0", "m1", "m2", "m3")
        glu_act = steps("glu_act", "gelu_p", "sig0p", "sig1p", "gelu_s", "sig0s", "sig1s")
        glu_pe = steps("glu_pe", "gb0p", "gb1p", "ga0p", "ga1p", "gb0s", "gb1s", "ga0s", "ga1s")
        glu_dve = sem("glu_dve")
        wo_pe = sem("h_products")
        tr_pe, lg_pe = sem("hn_transposed"), sem("logits")
        wo_dve = steps("h_dve", "add", "hn")
        wo_act, wo_inv = steps("h_act", "sq", "rms"), sem("h_inverse_rms")
        hte = sem("hnT_moved")
        lge = sem("logits_moved")
        rt_dve, rt_act, rt_pe, one_hots = sem("route_dve"), sem("route_act"), sem("route_pe"), sem("slot_one_hots")
        indirect_go = sem("indirect_go")
        slots_ready, idxc, outc = sem("slots_ready"), sem("index_copied"), sem("out_index_copied")
        m_xt, m_xte, m_gu, m_sil, m_hm, m_ht, m_hte, m_dn, m_dnA, m_dnD, m_free = (
            [sem(f"moe_{n}{k}") for k in range(2)]
            for n in ("xT", "xT_moved", "gate_up", "silu", "product", "productT", "productT_moved", "down",
                      "down_moved_act", "down_moved_dve",
                      "rows_free"))
        f_pe, f_diag = sem("final_sums"), sem("gates_on_diagonal")
        f_dve_sum, f_dve_y = sem("final_summed"), sem("final_y")
        f_act, f_inv = steps("final_act", "sq", "rms"), sem("final_inverse_rms")

        block = ctx.enter_context(nc.Block())

        TILES = [("g", 0), ("g", 1), ("a", 0), ("a", 1), ("xbc", 0), ("xbc", 1), ("xbc", 2), ("xbc", 3),
                 ("k", 0), ("k", 1), ("q", 0), ("q", 1), ("z", 0), ("z", 1), ("ud", 0), ("ud", 1)]
        EV_AT = {}
        for _j, _t in enumerate(TILES):
            if _t[0] not in "ga":
                EV_AT[_j] = len(EV_AT) + 1
        A0 = TILES.index(("a", 0))
        S5_AT = 6
        CV_AT = 12

        def tile_moved(eng, j):
            if TILES[j][0] == "g":
                eng.wait_ge(g_moved, j + 1)
            elif TILES[j][0] == "a":
                eng.wait_ge(gated, j - A0 + 1)
            else:
                eng.wait_ge(ev, EV_AT[j])

        def tok(i):
            return slice(i * P, i * P + NTOK[i])

        def band(i):
            if i == NT - 1:
                return 1024, [(8 + n, P) for n in range(4)] + [(12, TS)], 0
            lo = max(0, i - 4)
            return lo * P, [(n, P) for n in range(lo, i + 1)], (4 - (i - lo)) * P

        ROUNDS = [(i, h) for i in range(NT) for h in range(HEADS)]
        TAIL = 2 * NT
        S5_FIRST = TAIL + 3
        S5_ROUND = {S5_FIRST + min(max(c, 2 * c - 1), len(ROUNDS) - 1 - S5_FIRST): c for c in range(NT)}

        @block.sync
        def _(sp):
            sp.dma_start(cst[:, :], a["params"]).then_inc(s_params, 16)
            sp.dma_start(mats[:, :], a["mats"]).then_inc(s_params, 16)
            for k in range(KT):
                sp.dma_start(xn[:, k, :], a["xT"][k * P:(k + 1) * P, :]).then_inc(s_x[k], 16)
                if k == 0:
                    sp.dma_start(wring[:, 0, :], a["w_cm"][0]).then_inc(s_w[0], 16)
            for j in range(1, 4):
                sp.dma_start(wring[:, j, :], a["w_cm"][j]).then_inc(s_w[j], 16)
            sp.dma_start(wvd, a["w_vd"]).then_inc(s_wvd, 16)
            sp.dma_start(xb[:, :, CW - 1 + TP:CW - 1 + TP + CW - 1], a["ssd_hist"]).then_inc(s_hist, 16)
            sp.dma_start(vb[:, :, DW - 1 + TP:DW - 1 + TP + DW - 1], a["ccm_hist"]).then_inc(s_hist, 16)
            sp.dma_start(state[1], a["ssd_h0"]).then_inc(s_hist, 16)
            sp.dma_start(kt[:, :, 1024:1536], a["k_cache"]).then_inc(s_cache, 16)
            sp.dma_start(vt[:, 8:12, :], a["v_cache"]).then_inc(s_cache, 16)
            for j in range(4, len(TILES)):
                sp.wait_ge(proj, j - 3)
                sp.dma_start(wring[:, j % 4, :], a["w_cm"][j]).then_inc(s_w[j % 4], 16)
            sp.wait_ge(g_moved, 2)
            sp.dma_start(bias, a["bias"]).then_inc(s_bias, 16)
            sp.dma_start(pww, a["pw_w"]).then_inc(s_pww, 16)
            sp.dma_start(s5raw, a["s5_w"]).then_inc(s_s5w, 16)
            sp.wait_ge(proj, len(TILES))
            sp.dma_start(glu_w, a["glu_w"]).then_inc(s_gluw, 16)
            sp.wait_ge(tailed, 1)
            sp.dma_start(o["ssd_tail"], tail).then_inc(s_out, 16)
            sp.wait_ge(gated, 2)
            sp.dma_start(o["ccm_p"], vb[:, :, TP:TP + DW - 1]).then_inc(s_out, 16)
            sp.dma_start(o["ccm_s"], vb[:, :, VBW - (DW - 1):VBW]).then_inc(s_out, 16)
            sp.wait_ge(ev, len(EV_AT))
            sp.dma_start(o["k_p"], kt[:, :, TP - WIN:TP]).then_inc(s_out, 16)
            sp.dma_start(o["k_s"], kt[:, :, 1536:1600]).then_inc(s_out, 16)
            sp.wait_ge(vd_ev, NT)
            sp.dma_start(o["v_p"], vt[:, 4:8, :]).then_inc(s_out, 16)
            sp.dma_start(o["v_s"], vt[0:TS, 12, :]).then_inc(s_out, 16)
            sp.wait_ge(*ssd_dve.at(NT - 1, "state"))
            sp.dma_start(o["ssd_p"], state[0]).then_inc(s_out, 16)
            sp.dma_start(o["ssd_s"], state[1]).then_inc(s_out, 16)
            sp.wait_ge(*yg_dve.at(0, "norm1"))
            sp.dma_start(w_out, a["w_out"]).then_inc(s_wout, 16)
            sp.wait_ge(*s5_dve.at(NT - 1, "end"))
            sp.dma_start(o["s5_end"], s5end).then_inc(s_out, 16)
            sp.wait_ge(at_ovc, len(ROUNDS))
            sp.dma_start(gffn, a["g_ffn"]).then_inc(s_gffn, 16)
            sp.wait_ge(*s5_pool.at(NT - 1, "m3"))
            sp.dma_start(rw, a["w_route"]).then_inc(s_gffn, 16)
            for i in range(NT):
                if i >= 2:
                    sp.wait_ge(*wo_dve.at(i - 2, "add"))
                sp.dma_start(xtok[i % 2][0:NTOK[i], :], a["x_rows"][tok(i), :]).then_inc(s_xtok[i % 2], 16)
                if i >= 1:
                    sp.wait_ge(*wo_dve.at(i - 1, "hn"))
                    sp.dma_start(hn_dram[tok(i - 1), :], hn[(i - 1) % 2][0:NTOK[i - 1], :]
                                 ).then_inc(s_hst[(i - 1) % 2], 16)
            sp.wait_ge(*wo_dve.at(NT - 1, "hn"))
            sp.dma_start(hn_dram[tok(NT - 1), :], hn[(NT - 1) % 2][0:TS, :]).then_inc(s_hst[(NT - 1) % 2], 16)
            sp.wait_ge(rt_dve, RT["routed"])
            pairs = sp.value_load(npairs[0:1, :], min_val=1, max_val=BLOCKS // 2)
            def gate_up_in(r, i):
                e = sp.value_load(eid[0:1, ds(2 * i + r, 1)], min_val=0, max_val=E - 1)
                sp.wait_ge(m_gu[r], i + 1)
                sp.dma_start(wg[r], a["w_gate"][ds(e, 1), :, :].rearrange("o (p k) n -> (o p) k n", k=KT)
                             ).then_inc(s_wgu[r], 16)
                sp.dma_start(wu[r], a["w_up"][ds(e, 1), :, :].rearrange("o (p k) n -> (o p) k n", k=KT)
                             ).then_inc(s_wgu[r], 16)

            def down_in(r, i):
                e = sp.value_load(eid[0:1, ds(2 * i + r, 1)], min_val=0, max_val=E - 1)
                sp.wait_ge(m_dn[r], i + 1)
                sp.dma_start(wd[r], a["w_down"][ds(e, 1), :, :].rearrange("o (p k) n -> (o p) k n", k=4)
                             ).then_inc(s_wd[r], 16)

            gate_up_in(0, 0)
            sp.wait_ge(s_xg[0], 16)
            gate_up_in(1, 0)
            down_in(0, 0)
            with sp.Fori(1, BLOCKS // 2) as i:
                with sp.If(pairs > i):
                    gate_up_in(0, i)
                    down_in(1, i - 1)
                    gate_up_in(1, i)
                    down_in(0, i)
            down_in(1, pairs - 1)
            sp.dma_start(gfin, a["g_final"]).then_inc(s_gfin, 16)
            sp.wait_ge(s_os[0], 16 * pairs)
            sp.wait_ge(s_os[1], 16 * pairs)
            for i in range(NT):
                for k in range(2):
                    sp.dma_start(og[i][k][0:NTOK[i], :], out_dram[k * T + i * P:k * T + i * P + NTOK[i], :]
                                 ).then_inc(s_og[i], 16)
            for i in range(NT):
                sp.wait_ge(f_dve_y, i + 1)
                dst = o["y_p"][tok(i), :] if i < NT - 1 else o["y_s"]
                sp.dma_start(dst, yrow[i % 3][0:NTOK[i], :]).then_inc(s_yo[i % 3], 16)
            sp.wait_ge(s_out, 16 * 10)
            for k in range(3):
                sp.wait_ge(s_yo[k], 16 * 3)

        @block.tensor
        def _(te):
            te.wait_ge(s_params, 32)

            def squares(n):
                te.wait_ge(sq_pairs, n + 1)
                for ps, lo, hi in ((psC, 0, 512), (psC, 512, TP), (psB, TP, T)):
                    mm = te.matmul(ps[:, lo:hi], ones, sq[2 * n % 4][:, lo:hi], start=(n == 0),
                                   stop=(n == KT // 2 - 1))
                mm.then_inc(nrm_pe, 1)

            def tile_part(j, k):
                for lo, hi in CH:
                    if (j, k, lo) == (1, 0, TP):
                        te.wait_ge(nrm_act.sem, KT + 1)
                    mm = te.matmul(AB[j % 2][:, lo:hi], wring[:, j % 4, k * P:(k + 1) * P], xn[:, k, lo:hi],
                                   start=(k == 0), stop=(k == KT - 1))
                return mm

            for k in range(KT):
                if k == 0:
                    te.wait_ge(s_w[0], 16)
                te.wait_ge(xg_dve, k + 1)
                mm = tile_part(0, k)
                if k == KT - 1:
                    mm.then_inc(proj, 1)
                if k % 2:
                    squares(k // 2)
            for j in range(1, len(TILES)):
                te.wait_ge(s_w[j % 4], 16 * (j // 4 + 1))
                if j >= 2:
                    tile_moved(te, j - 2)
                for k in range(KT):
                    if j == 2:
                        te.wait_ge(xn_dve, k + 1)
                    mm = tile_part(j, k)
                    if j == 1:
                        if k < KT - 1:
                            mm.then_inc(x_used, 1)
                mm.then_inc(proj, 1)
            te.wait_ge(s_wvd, 16)
            te.wait_ge(dw_dve, 2 * 2 * DW)
            te.wait_ge(cv_act, 4)
            tile_moved(te, len(TILES) - 2)
            for j in range(2):
                for lo, hi in CH:
                    mm = te.matmul(psA[:, lo:hi], ones, vc[:, j, lo:hi], start=(j == 0), stop=(j == 1))
            mm.then_inc(*cm_pe.of("mu"))
            for i in range(NT):
                if i == 4:
                    te.wait_ge(*cm_act.at(0, "sq1"))
                    tile_moved(te, len(TILES) - 1)
                    for j in range(2):
                        for lo, hi in CH:
                            mm = te.matmul(psB[:, lo:hi], ones, sg[:, j, lo:hi], start=(j == 0), stop=(j == 1))
                    mm.then_inc(*cm_pe.of("var"))
                if i >= 2:
                    te.wait_ge(vd_ev, i - 1)
                for k in range(KT):
                    mm = te.matmul(psC[0:NTOK[i], 512 * (i % 2):512 * (i % 2) + VD], xn[:, k, tok(i)], wvd[:, k, :],
                                   start=(k == 0), stop=(k == KT - 1))
                mm.then_inc(vd_pe, 1)
            te.wait_ge(s_pww, 16)
            te.wait_ge(*cm_act.at(0, "silu1"))
            for m in range(2):
                for k in range(2):
                    for lo, hi in CH:
                        mm = te.matmul(AB[m][:, lo:hi], pww[:, k, m * P:(m + 1) * P], vc[:, k, lo:hi],
                                       start=(k == 0), stop=(k == 1))
                mm.then_inc(*cm_pe.of(f"pw{m}"))
            te.wait_ge(p5_dve, P5["bb"])
            te.wait_ge(*cm_act.at(0, "out1"))
            for m in range(2):
                for j in range(2):
                    mm = te.transpose(psB[:, (2 * m + j) * P:(2 * m + j + 1) * P],
                                      bb[m].rearrange("p s c -> p (s c)")[:, j * P:(j + 1) * P], ident)
            mm.then_inc(p5_pe, 1)
            te.wait_ge(*dtp_dve.at(0, "a"))
            te.wait_ge(vd_ev, NT)
            L8 = slice(0, TS)
            te.matmul(psC[:, 0:32], upper, aa[:, 0:8, :], start=True, stop=True)
            te.matmul(psC[:, 32:36], upper[L8, :], aa[L8, 8, :], start=True, stop=True)
            te.matmul(psC[:, 512:544], ones, aa[:, 0:8, :], start=True, stop=True)
            te.matmul(psC[:, 544:548], ones[L8, :], aa[L8, 8, :], start=True, stop=True).then_inc(dtp_pe, 1)
            def ssd_sums(c):
                te.wait_ge(*ssd_pool.at(c, "ua"))
                if c:
                    te.wait_ge(*ssd_dve.at(c - 1, "state"))
                te.matmul(psB[:, 0:512], ones[0:NTOK[c], :], ua[0:NTOK[c]], start=True, stop=True
                          ).then_inc(*ssd_pe.of("bc"))

            def ssd_inner(c):
                L = NTOK[c]
                if c:
                    te.wait_ge(*ssd_dve.at(c - 1, "yd"))
                for g in range(2):
                    te.matmul(psB[0:L, 512 * (1 + g):512 * (1 + g) + L], xb[g * 64:g * 64 + 64, 2, tok(c)],
                              xb[g * 64:g * 64 + 64, 3, tok(c)], start=True, stop=True)
                for j in range(3):
                    at = 640 + j * P if j < 2 else 1152
                    mm = te.transpose(psB[0:L, at:at + P], xb[:, j, tok(c)], ident)
                mm.then_inc(*ssd_pe.of("tr"))

            def ssd_outer(c):
                L = NTOK[c]
                te.wait_ge(*ssd_dve.at(c, "ce"))
                st = state[1 if c == NT - 1 else 0]
                for part in range(1 if c == 0 else 2):
                    for h in range(HEADS):
                        g, hh = divmod(h, 2)
                        y = psB[hh * 64:hh * 64 + 64, 896 + 512 * g:896 + 512 * g + L]
                        if part == 0:
                            mm = te.matmul(y, xdt[:, h * 64:h * 64 + 64], dm[:, h, 0:L], start=True, stop=(c == 0))
                        else:
                            mm = te.matmul(y, st[g * 64:g * 64 + 64, hh * 64:hh * 64 + 64],
                                           ce[g * 64:g * 64 + 64, h, 0:L], start=False, stop=True)
                mm.then_inc(*ssd_pe.of("y"))
                te.wait_ge(*ssd_pool.at(c, "xdd"))
                for g in range(2):
                    mm = te.matmul(psB[g * 64:g * 64 + 64, 0:P], btok[0:L, g * 64:g * 64 + 64],
                                   xdd[0:L, g * P:(g + 1) * P], start=True, stop=True)
                mm.then_inc(*ssd_pe.of("st"))

            def group_sums(g):
                te.wait_ge(*yg_act.at(0, f"sq{g}"))
                if g:
                    te.wait_ge(*yg_act.at(0, "ln0"))
                for lo, hi in CH:
                    mm = te.matmul(psB[:, lo:hi], ones, sg[:, g, lo:hi], start=True, stop=True)
                mm.then_inc(yg_pe, 1)

            def s5_in(c, half):
                L = NTOK[c]
                if c + half == 0:
                    te.wait_ge(*yg_act.at(0, "ln1"))
                elif half:
                    te.wait_ge(*s5_dve.at(c, "half0"))
                else:
                    te.wait_ge(*s5_dve.at(c - 1, "half1"))
                for jt in range(2):
                    for m in range(2):
                        for q in (2 * half, 2 * half + 1):
                            at = 512 * (q % 2) + (2 * jt + m) * P
                            mm = te.matmul(psB[:, at:at + L], bbT[m][32 * q:32 * q + 32, jt, :],
                                           mix[32 * q:32 * q + 32, UD + jt, tok(c)], start=True, stop=True)
                mm.then_inc(s5_x, 1)

            def s5_out(c):
                L = NTOK[c]
                if c:
                    te.wait_ge(s5_yd, c)
                for jt in range(2):
                    for x, m in enumerate((0, 2, 1, 1)):
                        if jt == 0:
                            te.wait_ge(*s5_pool.at(c, f"m{x}"))
                        for q in range(4):
                            at, s = 1024 + jt * P, 4 * jt + q
                            mm = te.matmul(psB[32 * q:32 * q + 32, at:at + L], cc[m][:, s, :],
                                           s5back[x][:, s, 0:L], start=(x == 0), stop=(x == 3))
                mm.then_inc(s5_y, 1)

            def scores(r):
                i, h = ROUNDS[r]
                pair, hh = divmod(h, 2)
                k0, tiles, _ = band(i)
                nk = sum(w for _, w in tiles)
                rows = slice(hh * 64, hh * 64 + 64)
                if r:
                    te.wait_ge(at_add, r)
                for lo in range(0, nk, 512):
                    hi = min(lo + 512, nk)
                    mm = te.matmul(psA[0:NTOK[i], lo:hi], mix[rows, Q + pair, tok(i)],
                                   kt[rows, pair, k0 + lo:k0 + hi], start=True, stop=True)
                mm.then_inc(at_s, 1)

            def turn_probs(r):
                i, h = ROUNDS[r]
                _, tiles, _ = band(i)
                nq = NTOK[i]
                te.wait_ge(at_diag, r + 1)
                te.wait_ge(at_exp, r + 1)
                if r >= 1:
                    te.wait_ge(at_ptc, r)
                for n, (_, w) in enumerate(tiles):
                    mm = te.matmul(psC[0:w, n * nq:(n + 1) * nq], pr[r % 2][0:nq, n * P:n * P + w],
                                   diag[r % 2][0:nq, 0:nq], start=True, stop=True)
                mm.then_inc(at_pt, 1)

            def outputs(r):
                i, h = ROUNDS[r]
                hh, nq = h % 2, NTOK[i]
                _, tiles, _ = band(i)
                te.wait_ge(at_ptc, r + 1)
                if r:
                    te.wait_ge(at_ovc, r)
                for n, (v, w) in enumerate(tiles):
                    mm = te.matmul(psA[hh * 64:hh * 64 + 64, 1024:1024 + nq], vt[0:w, v, h * 64:h * 64 + 64],
                                   pts[r % 2][0:w, n * nq:(n + 1) * nq], start=(n == 0), stop=(n == len(tiles) - 1))
                mm.then_inc(at_pv, 1)

            te.wait_ge(p5_act, P5A["bbT"])
            te.wait_ge(*dtp_act.at(0, "etot"))
            te.wait_ge(s_hist, 48)
            te.wait_ge(s_cache, 32)
            scores(0)
            scores(1)
            for r in range(len(ROUNDS)):
                c, second = divmod(r, 2)
                if not second and 1 <= c <= NT:
                    ssd_outer(c - 1)
                if r <= TAIL:
                    turn_probs(r)
                if not second and c < NT:
                    ssd_sums(c)
                if r + 2 < len(ROUNDS):
                    scores(r + 2)
                if r in S5_ROUND:
                    s5_in(S5_ROUND[r], 1)
                if r > TAIL:
                    turn_probs(r)
                if r == TAIL + 1:
                    group_sums(0)
                outputs(r)
                if r == TAIL + 1:
                    group_sums(1)
                if r == TAIL + 2:
                    s5_in(0, 0)
                if not second and c < NT:
                    ssd_inner(c)
                if r in S5_ROUND and S5_ROUND[r]:
                    s5_out(S5_ROUND[r] - 1)
                if r in S5_ROUND and S5_ROUND[r] + 1 < NT:
                    s5_in(S5_ROUND[r] + 1, 0)
            def h_tile(i, n, ks=range(KT)):
                if n == 0 and i >= 2:
                    te.wait_ge(*wo_dve.at(i - 2, "add"))
                for k in ks:
                    mm = te.matmul(hps[i][0:NTOK[i], n * 512:(n + 1) * 512], mix[:, k, tok(i)],
                                   w_out[:, k, n * 512:(n + 1) * 512], start=(k == 0), stop=(k == KT - 1))
                if n == 1 and ks[-1] == KT - 1:
                    mm.then_inc(wo_pe, 1)

            def glu(m, part, cols):
                for k in range(2):
                    for lo, hi in cols:
                        mm = te.matmul(AB[m % 2][:, lo:hi], glu_w[:, k, m * P:(m + 1) * P], gel[:, k, lo:hi],
                                       start=(k == 0), stop=(k == 1))
                mm.then_inc(*glu_pe.of(f"g{'b' if m >= 2 else 'a'}{m % 2}{part}"))

            te.wait_ge(at_ptc, len(ROUNDS))
            te.wait_ge(at_ovc, len(ROUNDS))
            te.wait_ge(s_wout, 16)
            for n in range(2):
                h_tile(0, n, range(UD))
            te.wait_ge(s_gluw, 16)
            te.wait_ge(*glu_act.at(0, "gelu_p"))
            te.wait_ge(*s5_dve.at(NT - 1, "half1"))
            glu(2, "p", CH[:2])
            glu(3, "p", CH[:2])
            s5_out(NT - 1)
            te.wait_ge(*glu_act.at(0, "sig0p"))
            glu(0, "p", CH[:2])
            te.wait_ge(*glu_act.at(0, "sig1p"))
            glu(1, "p", CH[:2])
            te.wait_ge(*glu_act.at(0, "gelu_s"))
            glu(2, "s", CH[2:])
            glu(3, "s", CH[2:])
            te.wait_ge(*glu_act.at(0, "sig0s"))
            glu(0, "s", CH[2:])
            te.wait_ge(*glu_act.at(0, "sig1s"))
            glu(1, "s", CH[2:])
            te.wait_ge(glu_dve, 4)
            for n in range(2):
                h_tile(0, n, range(UD, KT))
            te.wait_ge(s_gffn, 32)
            for i in range(NT):
                if i + 1 < NT:
                    h_tile(i + 1, 0)
                te.wait_ge(*wo_dve.at(i, "hn"))
                if i:
                    te.wait_ge(hte, i)
                for k in range(KT):
                    mm = te.transpose(psC[:, k * P:k * P + NTOK[i]], hn[i % 2][0:NTOK[i], k * P:(k + 1) * P],
                                      ident[0:NTOK[i], 0:NTOK[i]])
                mm.then_inc(tr_pe, 1)
                if i + 1 < NT:
                    h_tile(i + 1, 1)
                te.wait_ge(hte, i + 1)
                if i >= 2:
                    te.wait_ge(lge, i - 1)
                for k in range(KT):
                    mm = te.matmul(AB[i % 2][0:NTOK[i], 1024:1060], hnT[:, k, 0:NTOK[i]], rw[:, k, :],
                                   start=(k == 0), stop=(k == KT - 1))
                mm.then_inc(lg_pe, 1)
            te.wait_ge(rt_dve, RT["pre"])
            te.matmul(psA[:, 0:NT * E], upper, asg, start=True, stop=False)
            te.matmul(psA[:, 0:NT * E], ones, pre[:, 0:NT, :], start=False, stop=True)
            te.matmul(psB[:, 0:E], ones, pre[:, NT, :], start=True, stop=True).then_inc(rt_pe, 1)
            for n in range(2 * NT):
                M = NTOK[n % NT]
                te.wait_ge(one_hots, n + 1)
                mm = te.matmul(psC[:, 0:NB], in_low[n][0:M], in_blk[n][0:M], start=(n == 0), stop=(n == 2 * NT - 1))
            mm.then_inc(rt_pe, 1)

            def turn_rows(b, n):
                te.wait_ge(s_xg[b], 16 * n)
                for k in range(KT):
                    mm = te.transpose(psC[:, k * P:(k + 1) * P], xg[b].rearrange("p (m k) -> p k m", k=KT)[:, k, :],
                                      ident)
                mm.then_inc(m_xt[b], 1)

            def gate_up(r, i):
                te.wait_ge(m_xte[r], i + 2)
                te.wait_ge(s_wgu[r], 32 * i + 32)
                te.wait_ge(m_hm[1 - r], i + r + 1)
                for w, at in ((wg[r], 0), (wu[r], 512)):
                    for k in range(KT):
                        mm = te.matmul(psA[:, at:at + FF], xgT[r][:, k, :], w[:, k, :],
                                       start=(k == 0), stop=(k == KT - 1))
                mm.then_inc(m_gu[r], 1)

            def turn_product(r, i):
                te.wait_ge(m_hm[r], i + 2)
                te.wait_ge(m_hte[1 - r], i + r + 1)
                for k in range(4):
                    mm = te.transpose(psA[:, 1024 + k * P:1024 + (k + 1) * P],
                                      hmid[r].rearrange("p (m k) -> p k m", k=4)[:, k, :], ident)
                mm.then_inc(m_ht[r], 1)

            def down(r, i):
                te.wait_ge(m_hte[r], i + 2)
                te.wait_ge(s_wd[r], 16 * i + 16)
                te.wait_ge(m_dnA[1 - r], i + r + 1)
                te.wait_ge(m_dnD[1 - r], i + r + 1)
                for n in range(2):
                    for k in range(4):
                        mm = te.matmul(psB[:, n * 512:(n + 1) * 512], actg[r][:, k * P:(k + 1) * P],
                                       wd[r][:, k, n * 512:(n + 1) * 512], start=(k == 0), stop=(k == 3))
                mm.then_inc(m_dn[r], 1)

            def block_products(r, i, first=False):
                gate_up(r, i)
                turn_rows(1 - r, i + 1 + r)
                if not first:
                    down(1 - r, i - 1 + r)
                turn_product(r, i)

            te.wait_ge(slots_ready, 1)
            turn_rows(0, 1)
            pairs = te.value_load(npairs[0:1, :], min_val=1, max_val=BLOCKS // 2)
            block_products(0, 0, first=True)
            block_products(1, 0)
            with te.Fori(1, BLOCKS // 2) as i:
                with te.If(pairs > i):
                    for r in range(2):
                        block_products(r, i)
            down(1, pairs - 1)
            te.wait_ge(f_diag, 1)
            te.wait_ge(m_dnA[1], pairs + 1)
            te.wait_ge(m_dnD[1], pairs + 1)
            for i in range(NT):
                M = NTOK[i]
                te.wait_ge(s_og[i], 32)
                if i >= 3:
                    te.wait_ge(f_dve_y, i - 2)
                for n in range(2):
                    for k in range(2):
                        mm = te.matmul(fin[i % 3][0:M, n * 512:(n + 1) * 512], gdiag[i][k][0:M, 0:M],
                                       og[i][k][0:M, n * 512:(n + 1) * 512], start=(k == 0), stop=(k == 1))
                mm.then_inc(f_pe, 1)

        @block.scalar
        def _(ac):
            ac.wait_ge(s_params, 32)
            for k in range(KT):
                ac.wait_ge(s_x[k], 16)
                if k >= 4:
                    ac.wait_ge(nrm_pe, k // 2 - 1)
                ac.activation(sq[k % 4], xn[:, k, :], ACT.Square).then_inc(*nrm_act.of("sq"))
            ac.wait_ge(nrm_pe, KT // 2)
            ac.activation(rms[:, TP:T], psB[:, TP:T], ACT.Ln, scale=1.0 / D, bias=col("eps")
                          ).then_inc(*nrm_act.of("ln_s"))
            ac.activation(psC[:, :], psC[:, :], ACT.Ln, scale=1.0 / D, bias=col("eps")).then_inc(*nrm_act.of("ln"))
            ac.wait_ge(nrm_act.sem, KT + 2)
            ac.activation(rms[:, 0:TP], psC[:, :], ACT.Exp, scale=-0.5)
            ac.activation(rms[:, TP:T], rms[:, TP:T], ACT.Exp, scale=-0.5)
            ac.activation(psC[:, :], psC[:, :], ACT.Exp, scale=-0.5).then_inc(*nrm_act.of("rs"))
            for n in range(2):
                ac.wait_ge(g_moved, n + 1)
                ac.activation(sg[:, n, :], sg[:, n, :], ACT.Sigmoid).then_inc(g_sig, 1)
            ac.activation(s5p[:, DT, :], col("log_dt", 0, 8), ACT.Exp).then_inc(p5_act, 1)
            ac.wait_ge(zeroed, 3)
            for j, (kind, n) in enumerate(TILES):
                if kind in "ga":
                    continue
                ac.wait_ge(proj, j + 1)
                ps = AB[j % 2]
                if kind == "xbc":
                    ac.copy(xb[:, n, CW - 1:CW - 1 + TP], ps[:, 0:TP])
                    last = ac.copy(xb[:, n, XBW - TS:XBW], ps[:, TP:T])
                elif kind == "k":
                    ac.copy(kt[:, n, 0:TP], ps[:, 0:TP])
                    last = ac.copy(kt[:, n, 1536:1600], ps[:, TP:T])
                elif kind == "q":
                    last = ac.copy(mix[:, Q + n, :], ps[:, 0:T])
                elif kind == "z":
                    last = ac.activation(mix[:, Z + n, :], ps[:, 0:T], ACT.Silu)
                else:
                    last = ac.copy(mix[:, UD + n, :], ps[:, 0:T])
                last.then_inc(ev, 1)
                if j == S5_AT:
                    ac.wait_ge(p5_dve, P5["lrdt"])
                    ac.activation(s5p[:, MAG, :], s5p[:, T0, :], ACT.Exp).then_inc(p5_act, 1)
                    ac.wait_ge(p5_dve, P5["angles"])
                    ac.activation(s5p[:, SIN, :], s5p[:, TH, :], ACT.Sin).then_inc(p5_act, 1)
                    ac.activation(s5p[:, COS, :], s5p[:, T1, :], ACT.Sin).then_inc(p5_act, 1)
                if j >= CV_AT:
                    n = j - CV_AT
                    ac.wait_ge(tailed, 1)
                    ac.wait_ge(cv_dve, 2 * CW * (n + 1))
                    ac.activation(xb[:, n, 0:TP], psC[:, 0:TP], ACT.Silu)
                    ac.activation(xb[:, n, TP:T], cvs[:, n, :], ACT.Silu).then_inc(cv_act, 1)

            def vd_moved(i):
                ac.wait_ge(vd_pe, i + 1)
                M, at = NTOK[i], 512 * (i % 2)
                ac.copy(vt[0:M, i if i < NT - 1 else 12, :], psC[0:M, at:at + 256])
                ac.copy(dtr[0:M, i, :], psC[0:M, at + 256:at + VD]).then_inc(vd_ev, 1)

            vd_moved(0)
            vd_moved(1)
            for j in range(2):
                ac.wait_ge(*cm_dve.at(0, f"cen{j}"))
                ac.activation(sg[:, j, :], vc[:, j, :], ACT.Square).then_inc(*cm_act.of(f"sq{j}"))
            vd_moved(2)
            vd_moved(3)
            ac.wait_ge(*cm_pe.at(0, "var"))
            ac.activation(psB[:, 0:T], psB[:, 0:T], ACT.Ln, scale=1.0 / 256, bias=col("eps")).then_inc(*cm_act.of("ln"))
            ac.wait_ge(*cm_act.at(0, "ln"))
            ac.activation(psB[:, 0:T], psB[:, 0:T], ACT.Exp, scale=-0.5).then_inc(*cm_act.of("rs"))
            vd_moved(4)
            vd_moved(5)
            for j in range(2):
                ac.wait_ge(*cm_dve.at(0, f"n{j}"))
                ac.activation(vc[:, j, :], vc[:, j, :], ACT.Silu, scale=col("ln_g", j), bias=col("ln_b", j)
                              ).then_inc(*cm_act.of(f"silu{j}"))
            for i in range(6, NT):
                vd_moved(i)
            ac.wait_ge(*dtp_dve.at(0, "abs"))
            ac.activation(dta, dta, ACT.Exp, scale=-1.0).then_inc(*dtp_act.of("e"))
            ac.wait_ge(*dtp_act.at(0, "e"))
            ac.activation(dta, dta, ACT.Ln, bias=col("one")).then_inc(*dtp_act.of("ln"))
            ac.activation(aexp, col("a_log", 0, 4), ACT.Exp).then_inc(*dtp_act.of("aexp"))
            for m in range(2):
                ac.wait_ge(*cm_pe.at(0, f"pw{m}"))
                ac.activation(mix[:, CA + m, :], AB[m][:, 0:T], ACT.Identity, bias=col("pw_b", m)
                              ).then_inc(*cm_act.of(f"out{m}"))
            ac.wait_ge(p5_pe, 1)
            for m in range(2):
                last = ac.copy(bbT[m].rearrange("p j n -> p (j n)"), psB[:, 2 * m * P:(2 * m + 2) * P])
            last.then_inc(p5_act, 1)
            ac.wait_ge(*dtp_dve.at(0, "decin"))
            ac.activation(dec, dec, ACT.Exp).then_inc(*dtp_act.of("dec"))
            ac.activation(etot.rearrange("p i h -> p (i h)"), psC[:, 512:548], ACT.Exp).then_inc(*dtp_act.of("etot"))

            def ssd_ebc(c):
                ac.wait_ge(*ssd_pe.at(c, "bc"))
                if c:
                    ac.wait_ge(*ssd_dve.at(c - 1, "ce"))
                ac.activation(ebc.rearrange("p h t -> p (h t)"), psB[:, 0:512], ACT.Exp).then_inc(*ssd_act.of("ebc"))

            def ssd_decay(c):
                L = NTOK[c]
                ac.wait_ge(*ssd_dve.at(c, "dm"))
                for h in range(HEADS):
                    last = ac.activation(dm[0:L, h, 0:L], dm[0:L, h, 0:L], ACT.Exp, bias=nacs[0:L, c, h:h + 1])
                last.then_inc(*ssd_act.of("decay"))

            def group_squares(g):
                ac.wait_ge(ssd_gated, NT)
                ac.activation(sg[:, g, :], xb[:, g, 0:T], ACT.Square).then_inc(*yg_act.of(f"sq{g}"))

            def group_rms():
                for g in range(2):
                    ac.wait_ge(yg_pe, g + 1)
                    ac.activation(sg[:, g, :], psB[:, 0:T], ACT.Ln, scale=1.0 / P, bias=col("eps")
                                  ).then_inc(*yg_act.of(f"ln{g}"))
                for g in range(2):
                    ac.wait_ge(*yg_act.at(0, f"ln{g}"))
                    ac.activation(sg[:, g, :], sg[:, g, :], ACT.Exp, scale=-0.5).then_inc(*yg_act.of(f"rs{g}"))

            def probs(r):
                i, h = ROUNDS[r]
                nq, nk = NTOK[i], sum(w for _, w in band(i)[1])
                ac.wait_ge(at_max, r + 1)
                if r >= 2:
                    ac.wait_ge(at_pt, r - 1)
                ac.activation(pr[r % 2][0:nq, 0:nk], sc[r % 2][0:nq, 0:nk], ACT.Exp, bias=nmx[0:nq, r:r + 1],
                              accum_out=rsum[0:nq, r:r + 1]).then_inc(at_exp, 1)

            def move_probs(r):
                i, h = ROUNDS[r]
                nq, tiles = NTOK[i], band(i)[1]
                full = [w for _, w in tiles].count(P)
                ac.wait_ge(at_pt, r + 1)
                if r >= 2:
                    ac.wait_ge(at_pv, r - 1)
                last = ac.copy(pts[r % 2][:, 0:full * nq], psC[:, 0:full * nq])
                if full < len(tiles):
                    last = ac.copy(pts[r % 2][0:TS, full * nq:(full + 1) * nq], psC[0:TS, full * nq:(full + 1) * nq])
                last.then_inc(at_ptc, 1)

            def move_output(r):
                i, h = ROUNDS[r]
                pair, hh = divmod(h, 2)
                rows = slice(hh * 64, hh * 64 + 64)
                ac.wait_ge(at_pv, r + 1)
                ac.copy(mix[rows, Q + pair, tok(i)], psA[rows, 1024:1024 + NTOK[i]]).then_inc(at_ovc, 1)

            probs(0)
            for r in range(len(ROUNDS)):
                c, second = divmod(r, 2)
                if second and c < NT:
                    ssd_decay(c)
                if r + 1 < len(ROUNDS):
                    probs(r + 1)
                move_probs(r)
                if not second and c < NT:
                    ssd_ebc(c)
                move_output(r)
                if r == TAIL:
                    group_squares(0)
                    group_squares(1)
                if r == TAIL + 1:
                    group_rms()
            for part, lo, hi, n in (("p", 0, TP, NT - 1), ("s", TP, T, NT)):
                ac.wait_ge(s5_yd, n)
                ac.activation(gel[:, :, lo:hi], gel[:, :, lo:hi], ACT.Gelu_apprx_tanh
                              ).then_inc(*glu_act.of(f"gelu_{part}"))
                for j in range(2):
                    ac.wait_ge(*glu_pe.at(0, f"gb{j}{part}"))
                    ac.activation(sigm[j][:, lo:hi], AB[j][:, lo:hi], ACT.Sigmoid, bias=col("glu_b", 2 + j)
                                  ).then_inc(*glu_act.of(f"sig{j}{part}"))
            for i in range(NT):
                M = NTOK[i]
                ac.wait_ge(*wo_dve.at(i, "add"))
                if i >= 2:
                    ac.wait_ge(tr_pe, i - 1)
                    ac.wait_ge(s_hst[i % 2], 16 * (i // 2))
                ac.activation(hn[i % 2][0:M, :], hres[0:M, i, :], ACT.Square, accum_out=ssum[0:M, i:i + 1]
                              ).then_inc(*wo_act.of("sq"))
                ac.wait_ge(*wo_act.at(i, "sq"))
                ac.activation(hrs[0:M, i:i + 1], ssum[0:M, i:i + 1], ACT.Sqrt, scale=1.0 / D, bias=col("eps")[0:M]
                              ).then_inc(*wo_act.of("rms"))
                ac.wait_ge(tr_pe, i + 1)
                if i:
                    ac.wait_ge(lg_pe, i)
                ac.copy(hnT[:, :, 0:M], psC[:, :].rearrange("p (k n) -> p k n", k=KT)[:, :, 0:M]).then_inc(hte, 1)
                ac.wait_ge(lg_pe, i + 1)
                if i == 0:
                    ac.wait_ge(zeroed, 4)
                ac.copy(lgt[0:M, i, :], AB[i % 2][0:M, 1024:1060]).then_inc(lge, 1)
            ac.wait_ge(rt_dve, RT["d4"])
            ac.activation(prod[:, :, :, 0], d4, ACT.Exp).then_inc(rt_act, 1)
            ac.wait_ge(rt_dve, RT["dm"])
            ac.activation(gs, gs, ACT.Exp).then_inc(rt_act, 1)
            def activated(r, i):
                ac.wait_ge(m_gu[r], i + 2)
                ac.wait_ge(m_dn[r], i + 1)
                ac.activation(actg[r], psA[:, 0:FF], ACT.Silu).then_inc(m_sil[r], 1)

            def product_moved(r, i):
                ac.wait_ge(m_ht[r], i + 2)
                ac.copy(actg[r], psA[:, 1024:1536]).then_inc(m_hte[r], 1)

            def result_moved(r, i):
                ac.wait_ge(m_dn[r], i + 2)
                ac.wait_ge(m_free[r], i + 1)
                ac.copy(orow[r][:, 0:512], psB[:, 0:512]).then_inc(m_dnA[r], 1)

            def block_moves(r, i, first=False):
                activated(r, i)
                if not first:
                    result_moved(1 - r, i - 1 + r)
                product_moved(r, i)

            ac.wait_ge(rt_dve, RT["routed"])
            pairs = ac.value_load(npairs[0:1, :], min_val=1, max_val=BLOCKS // 2)
            block_moves(0, 0, first=True)
            block_moves(1, 0)
            with ac.Fori(1, BLOCKS // 2) as i:
                with ac.If(pairs > i):
                    for r in range(2):
                        block_moves(r, i)
            result_moved(1, pairs - 1)
            for i in range(NT):
                M = NTOK[i]
                ac.wait_ge(f_dve_sum, i + 1)
                ac.activation(sqrow[i % 2][0:M, :], fin[i % 3][0:M, 0:D], ACT.Square, accum_out=ssum[0:M, i:i + 1]
                              ).then_inc(*f_act.of("sq"))
                ac.wait_ge(*f_act.at(i, "sq"))
                ac.activation(hrs[0:M, i:i + 1], ssum[0:M, i:i + 1], ACT.Sqrt, scale=1.0 / D, bias=col("eps")[0:M]
                              ).then_inc(*f_act.of("rms"))

        @block.vector
        def _(ve):
            ve.wait_ge(s_params, 32)
            for k in range(KT):
                ve.wait_ge(nrm_act.sem, k + 1)
                ve.tensor_scalar(xn[:, k, :], xn[:, k, :], col("g_mix", k), None, ALU.mult).then_inc(xg_dve, 1)
                if k % 2:
                    a, b = sq[k % 4 - 1], sq[k % 4]
                    ve.tensor_tensor(a, a, b, ALU.add).then_inc(sq_pairs, 1)

            def gate_moved(n):
                ve.wait_ge(proj, n + 1)
                ve.tensor_tensor(sg[:, n, :], AB[n][:, 0:T], rms, ALU.mult).then_inc(g_moved, 1)

            ve.wait_ge(nrm_act.sem, KT + 3)
            for k in range(KT):
                if k < KT - 1:
                    ve.wait_ge(x_used, k + 1)
                else:
                    ve.wait_ge(proj, 2)
                ve.tensor_tensor(xn[:, k, 0:TP], xn[:, k, 0:TP], psC[:, :], ALU.mult)
                ve.tensor_tensor(xn[:, k, TP:T], xn[:, k, TP:T], rms[:, TP:T], ALU.mult).then_inc(xn_dve, 1)
                if k == 1:
                    gate_moved(0)
            gate_moved(1)
            n5 = [0]

            def link5(ins, name=None):
                ins.then_inc(p5_dve, 1)
                n5[0] += 1
                assert name is None or P5[name] == n5[0], (name, n5[0])
                ve.wait_ge(p5_dve, n5[0])

            def c5(n):
                return s5p[:, n, :]
            lre, lim = col("lam_re", 0, 8), col("lam_im", 0, 8)
            ve.wait_ge(p5_act, 1)
            link5(ve.tensor_tensor(c5(T0), lre, c5(DT), ALU.mult), "lrdt")
            link5(ve.tensor_tensor(c5(TH), lim, c5(DT), ALU.mult))
            link5(ve.tensor_scalar(c5(T1), c5(TH), 1.0 / (2 * math.pi), 12582912.0, ALU.mult, ALU.add))
            link5(ve.tensor_scalar(c5(T1), c5(T1), -12582912.0, None, ALU.add))
            link5(ve.scalar_tensor_tensor(out=c5(TH), in0=c5(T1), scalar=-6.28125, in1=c5(TH), op0=ALU.mult,
                                          op1=ALU.add))
            link5(ve.scalar_tensor_tensor(out=c5(TH), in0=c5(T1), scalar=-(2 * math.pi - 6.28125), in1=c5(TH),
                                          op0=ALU.mult, op1=ALU.add))
            link5(ve.tensor_scalar(c5(TH), c5(TH), 3.141592, -3.141592, ALU.min, ALU.max))
            link5(ve.scalar_tensor_tensor(out=c5(T1), in0=c5(TH), scalar=-1.0, in1=c5(TH), op0=ALU.mult, op1=ALU.max))
            link5(ve.tensor_scalar(c5(T1), c5(T1), -1.0, math.pi / 2, ALU.mult, ALU.add), "angles")
            ve.wait_ge(zeroed, 3)
            for n in range(2):
                j = A0 + n
                ve.wait_ge(proj, j + 1)
                ve.wait_ge(g_sig, n + 1)
                ve.tensor_tensor(vb[:, n, DW - 1:DW - 1 + TP], AB[j % 2][:, 0:TP], sg[:, n, 0:TP], ALU.mult)
                ve.tensor_tensor(vb[:, n, VBW - TS:VBW], AB[j % 2][:, TP:T], sg[:, n, TP:T], ALU.mult
                                 ).then_inc(gated, 1)
            def tap(x, w, b, t, width, out, count, sample_out):
                for acc, dst, at, n, k in ((psC[:, 0:TP], out, 0, TP, 0),
                                           (sample_out, sample_out, TP + width - 1, TS, 1)):
                    if t == 0:
                        ins = ve.tensor_scalar(acc, x[:, at:at + n], w(0), b, ALU.mult, ALU.add)
                    else:
                        ve.wait_ge(count[0], count[1] + 2 * t - 1 + k)
                        ins = ve.scalar_tensor_tensor(out=dst if t == width - 1 else acc, in0=x[:, at + t:at + t + n],
                                                      scalar=w(t), in1=acc, op0=ALU.mult, op1=ALU.add)
                    ins.then_inc(count[0], 1)

            ve.wait_ge(gated, 2)
            ve.wait_ge(s_hist, 48)
            for j in range(2):
                if j:
                    ve.wait_ge(dw_dve, 2 * DW * j)
                for t in range(DW):
                    tap(vb[:, j, :], lambda t: col("dw_w", DW * j + t), col("dw_b", j), t, DW, vc[:, j, 0:TP],
                        (dw_dve, 2 * DW * j), vc[:, j, TP:T])

            def conv4(j):
                ve.wait_ge(ev, EV_AT[TILES.index(("xbc", j))])
                if j:
                    ve.wait_ge(cv_act, j)
                else:
                    ve.wait_ge(dw_dve, 2 * 2 * DW)
                for t in range(CW):
                    tap(xb[:, j, :], lambda t: col("conv_w", 4 * j + t), col("conv_b", j), t, CW, psC[:, 0:TP],
                        (cv_dve, 2 * CW * j), cvs[:, j, :])

            conv4(0)
            ve.wait_ge(p5_act, 4)
            link5(ve.tensor_tensor(c5(AR), c5(MAG), c5(COS), ALU.mult))
            link5(ve.tensor_tensor(c5(AI), c5(MAG), c5(SIN), ALU.mult))
            link5(ve.tensor_tensor(c5(T0), lre, lre, ALU.mult))
            link5(ve.tensor_tensor(c5(T1), lim, lim, ALU.mult))
            link5(ve.tensor_tensor(c5(T0), c5(T0), c5(T1), ALU.add))
            link5(ve.reciprocal(c5(T2), c5(T0)))
            link5(ve.scalar_tensor_tensor(out=c5(T0), in0=c5(AR), scalar=-1.0, in1=lre, op0=ALU.add, op1=ALU.mult))
            link5(ve.tensor_tensor(c5(T1), c5(AI), lim, ALU.mult))
            link5(ve.tensor_tensor(c5(T0), c5(T0), c5(T1), ALU.add))
            link5(ve.tensor_tensor(c5(CR), c5(T0), c5(T2), ALU.mult))
            link5(ve.scalar_tensor_tensor(out=c5(T0), in0=c5(AR), scalar=-1.0, in1=lim, op0=ALU.add, op1=ALU.mult))
            link5(ve.tensor_tensor(c5(T1), c5(AI), lre, ALU.mult))
            link5(ve.tensor_tensor(c5(T1), c5(T1), c5(T0), ALU.subtract))
            link5(ve.tensor_tensor(c5(CI), c5(T1), c5(T2), ALU.mult))
            link5(ve.tensor_copy(cosT[:, :, 0:1], c5(COS).unsqueeze(2)))
            link5(ve.tensor_copy(sinT[:, :, 0:1], c5(SIN).unsqueeze(2)))
            k = 1
            while k < P:
                cl = cosT[:, :, k - 1:k].broadcast_to([P, ST, k])
                sl = sinT[:, :, k - 1:k].broadcast_to([P, ST, k])
                lo, hi = slice(0, k), slice(k, 2 * k)
                link5(ve.tensor_tensor(tt[0][:, :, lo], cosT[:, :, lo], cl, ALU.mult))
                link5(ve.tensor_tensor(tt[1][:, :, lo], sinT[:, :, lo], sl, ALU.mult))
                link5(ve.tensor_tensor(cosT[:, :, hi], tt[0][:, :, lo], tt[1][:, :, lo], ALU.subtract))
                link5(ve.tensor_tensor(tt[0][:, :, lo], cosT[:, :, lo], sl, ALU.mult))
                link5(ve.tensor_tensor(tt[1][:, :, lo], sinT[:, :, lo], cl, ALU.mult))
                link5(ve.tensor_tensor(sinT[:, :, hi], tt[0][:, :, lo], tt[1][:, :, lo], ALU.add),
                      "tables" if k == 64 else None)
                k *= 2

            for j in range(1, 4):
                conv4(j)
            ve.wait_ge(*cm_pe.at(0, "mu"))
            for j in range(2):
                ve.scalar_tensor_tensor(out=vc[:, j, :], in0=psA[:, 0:T], scalar=-1.0 / 256, in1=vc[:, j, :],
                                        op0=ALU.mult, op1=ALU.add).then_inc(*cm_dve.of(f"cen{j}"))
            ve.wait_ge(*cm_act.at(0, "rs"))
            for j in range(2):
                ve.tensor_tensor(vc[:, j, :], vc[:, j, :], psB[:, 0:T], ALU.mult).then_inc(*cm_dve.of(f"n{j}"))
            ve.wait_ge(proj, len(TILES))
            ve.wait_ge(s_s5w, 16)
            for m in range(2):
                link5(ve.memset(bb[m], 0.0))
            for m in range(3):
                link5(ve.memset(cc[m], 0.0))
            for m, op in ((0, ALU.subtract), (1, ALU.add)):
                link5(ve.tensor_tensor(t5[0], s5w[:, m, :, :], bc(c5(CR), 2, 16), ALU.mult))
                link5(ve.tensor_tensor(t5[1], s5w[:, 1 - m, :, :], bc(c5(CI), 2, 16), ALU.mult))
                for g in range(2):
                    rows = slice(g * 64, g * 64 + 64)
                    link5(ve.tensor_tensor(bb[m][rows, :, g * 16:g * 16 + 16], t5[0][rows], t5[1][rows], op))
            for m, src, sgn in ((0, 2, 1.0), (1, 3, -1.0), (2, 2, -1.0)):
                for g in range(2):
                    rows = slice(g * 64, g * 64 + 64)
                    link5(ve.tensor_scalar(cc[m][rows, :, g * 16:g * 16 + 16], s5w[rows, src, :, :], sgn, None,
                                           ALU.mult), "bb" if m + g == 3 else None)
            ve.wait_ge(vd_ev, NT)
            ve.tensor_tensor(dtr, dtr, bc(col("dt_bias", 0, 4), 1, NT), ALU.add).then_inc(*dtp_dve.of("raw"))
            ve.wait_ge(*dtp_dve.at(0, "raw"))
            ve.scalar_tensor_tensor(out=dta, in0=dtr, scalar=-1.0, in1=dtr, op0=ALU.mult, op1=ALU.max
                                    ).then_inc(*dtp_dve.of("abs"))
            ve.wait_ge(*dtp_act.at(0, "aexp"))
            ve.scalar_tensor_tensor(out=dtt, in0=dtr, scalar=0.0, in1=dta, op0=ALU.max, op1=ALU.add
                                    ).then_inc(*dtp_dve.of("dt"))
            ve.wait_ge(*dtp_dve.at(0, "dt"))
            ve.scalar_tensor_tensor(out=aa, in0=dtt, scalar=-1.0, in1=bc(aexp, 1, NT), op0=ALU.mult, op1=ALU.mult
                                    ).then_inc(*dtp_dve.of("a"))
            ve.wait_ge(dtp_pe, 1)
            ve.tensor_scalar(nacs.rearrange("p i h -> p (i h)"), psC[:, 0:36], -1.0, None, ALU.mult
                             ).then_inc(*dtp_dve.of("nacs"))
            ve.wait_ge(*dtp_dve.at(0, "nacs"))
            ve.tensor_tensor(dec.rearrange("p i h -> p (i h)"), psC[:, 512:548], nacs.rearrange("p i h -> p (i h)"),
                             ALU.add).then_inc(*dtp_dve.of("decin"))

            def ssd_masked(c):
                L = NTOK[c]
                ve.wait_ge(*ssd_act.at(c, "ebc"))
                ve.tensor_tensor(dm[0:L, :, :], psB[0:L, 0:512].rearrange("p (h t) -> p h t", h=4),
                                 bc(negmask[0:L, :], 1, 4), ALU.add).then_inc(*ssd_dve.of("dm"))

            def ssd_operands(c):
                L = NTOK[c]
                ve.wait_ge(*ssd_act.at(c, "decay"))
                ve.wait_ge(*ssd_pe.at(c, "tr"))
                for g in range(2):
                    at = 512 * (1 + g)
                    last = ve.tensor_tensor(dm[0:L, 2 * g:2 * g + 2, 0:L], dm[0:L, 2 * g:2 * g + 2, 0:L],
                                            bc(psB[0:L, at:at + L], 1, 2), ALU.mult)
                last.then_inc(*ssd_dve.of("m"))
                if c:
                    ve.wait_ge(*ssd_pool.at(c - 1, "xdd"))
                if L < P:
                    ve.memset(xdt[L:P], 0.0)
                ve.tensor_tensor(xdt[0:L].rearrange("p (h d) -> p h d", h=4),
                                 psB[0:L, 640:896].rearrange("p (h d) -> p h d", h=4), bc(dtt[0:L, c, :], 2, 64),
                                 ALU.mult).then_inc(*ssd_dve.of("xdt"))
                ve.tensor_copy(btok[0:L, :], psB[0:L, 1152:1280]).then_inc(*ssd_dve.of("btok"))
                for g in range(2):
                    rows = slice(g * 64, g * 64 + 64)
                    last = ve.tensor_tensor(ce[rows, 2 * g:2 * g + 2, 0:L], bc(xb[rows, 3, tok(c)], 1, 2),
                                            ebc[rows, 2 * g:2 * g + 2, 0:L], ALU.mult)
                last.then_inc(*ssd_dve.of("ce"))

            def ssd_results(c):
                L = NTOK[c]
                ve.wait_ge(*ssd_pe.at(c, "st"))
                st = state[1 if c == NT - 1 else 0]
                for h in range(HEADS):
                    g, hh = divmod(h, 2)
                    rows, cols = slice(g * 64, g * 64 + 64), slice(hh * 64, hh * 64 + 64)
                    new = psB[rows, hh * 64:hh * 64 + 64]
                    if c == 0:
                        last = ve.tensor_copy(st[rows, cols], new)
                    else:
                        last = ve.scalar_tensor_tensor(out=st[rows, cols], in0=st[rows, cols],
                                                       scalar=etot[rows, c, h:h + 1], in1=new,
                                                       op0=ALU.mult, op1=ALU.add)
                last.then_inc(*ssd_dve.of("state"))
                for g in range(2):
                    at = 896 + 512 * g
                    last = ve.scalar_tensor_tensor(out=xb[:, g, tok(c)], in0=xb[:, g, tok(c)],
                                                   scalar=col("ssd_d", g), in1=psB[:, at:at + L],
                                                   op0=ALU.mult, op1=ALU.add)
                last.then_inc(*ssd_dve.of("yd"))

            def group_norm(g):
                ve.wait_ge(*yg_act.at(0, f"rs{g}"))
                ve.scalar_tensor_tensor(out=mix[:, Z + g, :], in0=xb[:, g, 0:T], scalar=col("norm_w", g),
                                        in1=sg[:, g, :], op0=ALU.mult, op1=ALU.mult).then_inc(*yg_dve.of(f"norm{g}"))

            def biased(r):
                i, h = ROUNDS[r]
                _, tiles, b0 = band(i)
                nq, nk = NTOK[i], sum(w for _, w in tiles)
                ve.wait_ge(at_s, r + 1)
                if r >= 2:
                    ve.wait_ge(at_exp, r - 1)
                ve.scalar_tensor_tensor(out=sc[r % 2][0:nq, 0:nk], in0=psA[0:nq, 0:nk], scalar=ATT_SCALE,
                                        in1=bias[0:nq, h, b0:b0 + nk], op0=ALU.mult, op1=ALU.add).then_inc(at_add, 1)
                ve.wait_ge(at_add, r + 1)
                ve.tensor_reduce(nmx[0:nq, r:r + 1], sc[r % 2][0:nq, 0:nk], AX.X, ALU.max, negate=True
                                 ).then_inc(at_max, 1)

            def diagonal(r):
                nq = NTOK[ROUNDS[r][0]]
                ve.wait_ge(at_exp, r + 1)
                ve.reciprocal(rinv[0:nq, r:r + 1], rsum[0:nq, r:r + 1]).then_inc(at_rinv, 1)
                ve.wait_ge(at_rinv, r + 1)
                if r >= 2:
                    ve.wait_ge(at_pt, r - 1)
                ve.tensor_scalar(diag[r % 2][0:nq, 0:nq], ident[0:nq, 0:nq], rinv[0:nq, r:r + 1], None, ALU.mult
                                 ).then_inc(at_diag, 1)

            def views(x, half, L):
                return x.rearrange("p (j q) t -> p q j t", j=2)[:, 2 * half:2 * half + 2, :, 0:L]

            def s5_result(c):
                L = NTOK[c]
                ve.wait_ge(s5_y, c + 1)
                for jt in range(2):
                    last = ve.scalar_tensor_tensor(out=gel[:, jt, tok(c)], in0=mix[:, UD + jt, tok(c)],
                                                   scalar=col("s5_d", jt),
                                                   in1=psB[:, 1024 + jt * P:1024 + jt * P + L],
                                                   op0=ALU.mult, op1=ALU.add)
                last.then_inc(s5_yd, 1)

            def s5_input(c, m):
                x = psB[:, 0:1024].rearrange("p (q j m t) -> p q j m t", q=2, j=2, m=2)
                return x[:, :, :, m, 0:NTOK[c]]

            def s5_turned(c, half):
                L = NTOK[c]
                ve.wait_ge(s5_x, 2 * c + half + 1)
                for dst, m, table in ((s5t[0], 0, cosT), (s5t[1], 1, sinT), (s5u[0], 1, cosT), (s5u[1], 0, sinT)):
                    last = ve.tensor_tensor(views(dst, half, L), s5_input(c, m), views(table, half, L), ALU.mult)
                last.then_inc(*s5_dve.of(f"half{half}"))

            def s5_added(c):
                L = NTOK[c]
                ve.wait_ge(*s5_dve.at(c, "half1"))
                ve.tensor_tensor(s5u[1][:, :, 0:L], s5u[0][:, :, 0:L], s5u[1][:, :, 0:L], ALU.subtract
                                 ).then_inc(*s5_dve.of("u1"))

            def s5_scanned(c):
                L = NTOK[c]
                ve.wait_ge(*s5_dve.at(c, "u1"))
                ve.wait_ge(*s5_pool.at(c, "u0"))
                r = 1 if c == NT - 1 else 0
                for s in range(ST):
                    for m in range(2):
                        if c == 0:
                            init = 0.0
                        elif c == NT - 1:
                            init = col("h0_re" if m == 0 else "h0_im", s)
                        else:
                            init = s5end[:, 0, m, s:s + 1]
                        last = ve.tensor_tensor_scan(s5g[m][:, s, 0:L], s5p[:, MAG, s:s + 1].broadcast_to([P, L]),
                                                     (s5t[0], s5u[1])[m][:, s, 0:L], init, ALU.mult, ALU.add)
                last.then_inc(*s5_dve.of("scan"))
                ve.wait_ge(*s5_dve.at(c, "scan"))
                ce_, se_ = cosT[:, :, L - 1], sinT[:, :, L - 1]
                gr, gi = s5g[0][:, :, L - 1], s5g[1][:, :, L - 1]
                for x, (p0, p1) in enumerate(((gr, ce_), (gi, se_), (gr, se_), (gi, ce_))):
                    last = ve.tensor_tensor(cmul[:, x, :], p0, p1, ALU.mult)
                last.then_inc(*s5_dve.of("carry"))
                ve.wait_ge(*s5_dve.at(c, "carry"))
                ve.tensor_tensor(s5end[:, r, 0, :], cmul[:, 0, :], cmul[:, 1, :], ALU.subtract)
                ve.tensor_tensor(s5end[:, r, 1, :], cmul[:, 2, :], cmul[:, 3, :], ALU.add).then_inc(*s5_dve.of("end"))
                ve.wait_ge(*s5_dve.at(c, "end"))

            ve.wait_ge(s_bias, 16)
            ve.wait_ge(cv_act, 4)
            biased(0)
            for r in range(len(ROUNDS)):
                c, second = divmod(r, 2)
                if r + 1 < len(ROUNDS):
                    biased(r + 1)
                if r - 1 in S5_ROUND:
                    s5_scanned(S5_ROUND[r - 1])
                    if S5_ROUND[r - 1]:
                        s5_result(S5_ROUND[r - 1] - 1)
                if r in S5_ROUND:
                    s5_turned(S5_ROUND[r], 0)
                diagonal(r)
                if not second and 1 <= c <= NT:
                    ssd_results(c - 1)
                if second and c < NT:
                    ssd_operands(c)
                if not second and c < NT:
                    ssd_masked(c)
                if r == TAIL + 2:
                    group_norm(0)
                    group_norm(1)
                if r in S5_ROUND:
                    s5_turned(S5_ROUND[r], 1)
                    s5_added(S5_ROUND[r])
            s5_scanned(NT - 1)
            s5_result(NT - 2)
            s5_result(NT - 1)
            for part, lo, hi in (("p", 0, TP), ("s", TP, T)):
                for m in range(2):
                    ve.wait_ge(*glu_pe.at(0, f"ga{m}{part}"))
                    ve.scalar_tensor_tensor(out=mix[:, UD + m, lo:hi], in0=AB[m][:, lo:hi], scalar=col("glu_b", m),
                                            in1=sigm[m][:, lo:hi], op0=ALU.add, op1=ALU.mult).then_inc(glu_dve, 1)
            for i in range(NT):
                M = NTOK[i]
                if i == 0:
                    ve.wait_ge(s_out, 16 * 10)
                    ve.wait_ge(s_gffn, 32)
                ve.wait_ge(wo_pe, i + 1)
                ve.wait_ge(s_xtok[i % 2], 16 * (i // 2 + 1))
                ve.tensor_tensor(hres[0:M, i, :], hps[i][0:M, 0:D], xtok[i % 2][0:M, :], ALU.add
                                 ).then_inc(*wo_dve.of("add"))
                ve.wait_ge(*wo_act.at(i, "rms"))
                ve.reciprocal(hrs[0:M, i:i + 1], hrs[0:M, i:i + 1]).then_inc(wo_inv, 1)
                ve.wait_ge(wo_inv, i + 1)
                ve.scalar_tensor_tensor(out=hn[i % 2][0:M, :], in0=hres[0:M, i, :], scalar=hrs[0:M, i:i + 1],
                                        in1=gffn[0:M, :], op0=ALU.mult, op1=ALU.mult).then_inc(*wo_dve.of("hn"))
            nr = [0]

            def linkr(ins, name=None):
                ins.then_inc(rt_dve, 1)
                nr[0] += 1
                assert name is None or RT[name] == nr[0], (name, nr[0])
                ve.wait_ge(rt_dve, nr[0])

            def first(onehot, marks, order, best, n):
                linkr(ve.tensor_tensor(marks, marks, bc(order, 1, NT), ALU.mult))
                linkr(ve.tensor_reduce(best, marks, AX.X, ALU.max))
                linkr(ve.tensor_tensor(onehot, marks, bc(best, 2, n), ALU.is_equal))

            ve.wait_ge(lge, NT)
            l4 = lgt[:, :, 0:G]
            l32 = lgt[:, :, G:G + E].rearrange("p i (g e) -> p i g e", g=G)
            linkr(ve.tensor_reduce(m4, l4, AX.X, ALU.max))
            linkr(ve.tensor_tensor(d4, l4, bc(m4, 2, G), ALU.subtract), "d4")
            linkr(ve.tensor_scalar(ohg, d4, 0.0, None, ALU.is_ge))
            first(ohg, ohg, col("order4", 0, G), mm, G)
            ve.wait_ge(rt_act, 1)
            linkr(ve.tensor_reduce(pgr, prod[:, :, :, 0], AX.X, ALU.add))
            linkr(ve.reciprocal(pgr, pgr))
            linkr(ve.tensor_tensor(prod, l32, bc(ohg, 3, EPG), ALU.mult))
            linkr(ve.tensor_reduce(les, prod.rearrange("p i g e -> p i e g"), AX.X, ALU.add))
            linkr(ve.tensor_reduce(m1, les, AX.X, ALU.max))
            linkr(ve.tensor_tensor(t8, les, bc(m1, 2, EPG), ALU.is_ge))
            first(oh[0], t8, col("order8", 0, EPG), mm, EPG)
            linkr(ve.scalar_tensor_tensor(out=les, in0=oh[0], scalar=NEG, in1=les, op0=ALU.mult, op1=ALU.add))
            linkr(ve.tensor_reduce(m2, les, AX.X, ALU.max))
            linkr(ve.tensor_tensor(t8, les, bc(m2, 2, EPG), ALU.is_ge))
            first(oh[1], t8, col("order8", 0, EPG), mm, EPG)
            linkr(ve.tensor_tensor(gs, m2, m1, ALU.subtract), "dm")
            for k in range(2):
                linkr(ve.tensor_tensor(oe[k], bc(ohg, 3, EPG), bc(oh[k], 2, G), ALU.mult))
            linkr(ve.memset(oe[0][TS:P, NT - 1], 0.0))
            linkr(ve.memset(oe[1][TS:P, NT - 1], 0.0))
            flat = [x.rearrange("p i g e -> p i (g e)") for x in oe]
            linkr(ve.tensor_tensor(asg, flat[0], flat[1], ALU.add))
            linkr(ve.memset(pre[:, 0, :], 0.0))
            for i in range(NT):
                linkr(ve.tensor_tensor(pre[:, i + 1, :], pre[:, i, :], asg[:, i, :], ALU.add),
                      "pre" if i == NT - 1 else None)
            ve.wait_ge(rt_pe, 1)
            c3 = cmp[:, 0:E * THR].rearrange("p (e n) -> p e n", n=THR)
            linkr(ve.tensor_tensor(c3, bc(psB[:, 0:E], 2, THR), bc(col("thr", 0, THR), 1, E), ALU.is_gt))
            linkr(ve.tensor_reduce(nblk, c3, AX.X, ALU.add))
            linkr(ve.tensor_tensor_scan(bend, ones[:, 0:E], nblk, 0.0, ALU.mult, ALU.add))
            c2 = cmp[0:1, :].rearrange("p (b e) -> p b e", e=E)
            linkr(ve.tensor_tensor(c2, bc(bend[0:1, :], 1, BLOCKS), bc(col("iota", 0, BLOCKS)[0:1, :], 2, E), ALU.is_le))
            linkr(ve.tensor_reduce(eidf[0:1, :], c2, AX.X, ALU.add))
            linkr(ve.tensor_scalar(eidf[0:1, :], eidf[0:1, :], float(E - 1), None, ALU.min))
            linkr(ve.tensor_copy(eid[0:1, :], eidf[0:1, :]))
            even = col("iota", 0, BLOCKS)[0:1, :].rearrange("p (i two) -> p i two", two=2)[:, :, 0]
            linkr(ve.tensor_tensor(slotf[0:1, 0:BLOCKS // 2], even,
                                   bend[0:1, E - 1:E].broadcast_to([1, BLOCKS // 2]), ALU.is_lt))
            linkr(ve.tensor_reduce(slotf[0:1, BLOCKS:BLOCKS + 1], slotf[0:1, 0:BLOCKS // 2], AX.X, ALU.add))
            linkr(ve.tensor_copy(npairs[0:1, :], slotf[0:1, BLOCKS:BLOCKS + 1]), "routed")
            linkr(ve.tensor_tensor(base, bend, nblk, ALU.subtract))
            linkr(ve.tensor_scalar(base, base, float(P), -1.0, ALU.mult, ALU.add))
            linkr(ve.tensor_tensor(dmap, psA[:, 0:NT * E].rearrange("p (i e) -> p i e", e=E), bc(base, 1, NT),
                                   ALU.add))
            for k in range(2):
                linkr(ve.tensor_tensor(prod.rearrange("p i g e -> p i (g e)"), flat[k], dmap, ALU.mult))
                linkr(ve.tensor_reduce(destf[:, k, :], prod.rearrange("p i g e -> p i (g e)"), AX.X, ALU.add))
            linkr(ve.tensor_scalar(blkf, destf, 1.0 / P, -(P - 1) / (2.0 * P), ALU.mult, ALU.add))
            linkr(ve.tensor_scalar(blkf, blkf, 12582912.0, None, ALU.add))
            linkr(ve.tensor_scalar(blkf, blkf, -12582912.0, None, ALU.add))
            linkr(ve.scalar_tensor_tensor(out=lowf, in0=blkf, scalar=-float(P), in1=destf, op0=ALU.mult, op1=ALU.add))
            for n in range(2 * NT):
                k, i = divmod(n, NT)
                M = NTOK[i]
                ve.tensor_scalar(in_low[n][0:M], col("iota", 0, P)[0:M], lowf[0:M, k, i:i + 1], None, ALU.is_equal)
                ve.tensor_scalar(in_blk[n][0:M], col("iota", 0, NB)[0:M], blkf[0:M, k, i:i + 1],
                                 col("asg_row", n)[0:M], ALU.is_equal, ALU.mult).then_inc(one_hots, 1)
            ve.wait_ge(rt_act, 2)
            linkr(ve.tensor_scalar(m1, gs, 1.0, None, ALU.add))
            linkr(ve.reciprocal(m1, m1))
            linkr(ve.tensor_tensor(gate[0], m1, pgr, ALU.mult))
            linkr(ve.tensor_tensor(gate[1], gate[0], gs, ALU.mult))
            ve.wait_ge(rt_pe, 2)
            linkr(ve.tensor_scalar(slotc, psC[:, 0:NB], 2.0 * T, None, ALU.add))
            linkr(ve.tensor_scalar(slotm, slotc, float(T), float(-T), ALU.is_ge, ALU.mult))
            linkr(ve.tensor_tensor(slotm, slotm, slotc, ALU.add))
            ve.tensor_copy(slot_out, slotc)
            ve.tensor_copy(slot_in, slotm).then_inc(slots_ready, 1)
            ve.wait_ge(slots_ready, 1)

            def rows_moved(b, n):
                ve.wait_ge(m_xt[b], n + 1)
                ve.tensor_copy(xgT[b].rearrange("p k n -> p (k n)"), psC[:, :]).then_inc(m_xte[b], 1)

            def multiplied(r, i):
                ve.wait_ge(m_sil[r], i + 2)
                ve.wait_ge(m_ht[r], i + 1)
                ve.tensor_tensor(hmid[r], psA[:, 512:1024], actg[r], ALU.mult).then_inc(m_hm[r], 1)

            def result_half(r, i):
                ve.wait_ge(m_dn[r], i + 2)
                ve.wait_ge(m_free[r], i + 1)
                ve.tensor_copy(orow[r][:, 512:1024], psB[:, 512:1024]).then_inc(m_dnD[r], 1)

            def block_parts(r, i, first=False):
                multiplied(r, i)
                rows_moved(1 - r, i + 1 + r)
                if not first:
                    result_half(1 - r, i - 1 + r)

            rows_moved(0, 1)
            pairs = ve.value_load(npairs[0:1, :], min_val=1, max_val=BLOCKS // 2)
            block_parts(0, 0, first=True)
            block_parts(1, 0)
            ve.wait_ge(s_hst[0], 16 * 5)
            ve.wait_ge(s_hst[1], 16 * 4)
            for i in range(NT):
                for k in range(2):
                    last = ve.tensor_scalar(gdiag[i][k][0:NTOK[i], 0:NTOK[i]], ident[0:NTOK[i], 0:NTOK[i]],
                                            gate[k][0:NTOK[i], i:i + 1], None, ALU.mult)
            last.then_inc(f_diag, 1)
            with ve.Fori(1, BLOCKS // 2) as i:
                with ve.If(pairs > i):
                    for r in range(2):
                        block_parts(r, i)
            result_half(1, pairs - 1)
            ve.wait_ge(s_gfin, 16)
            ve.wait_ge(s_xg[0], 16 * pairs + 32)
            ve.wait_ge(s_xg[1], 16 * pairs + 16)

            def summed(i):
                M = NTOK[i]
                ve.wait_ge(f_pe, i + 1)
                ve.tensor_tensor(fin[i % 3][0:M, 0:D], fin[i % 3][0:M, 0:D], hres[0:M, i, :], ALU.add
                                 ).then_inc(f_dve_sum, 1)

            def final_norm(i):
                M = NTOK[i]
                ve.wait_ge(*f_act.at(i, "rms"))
                ve.reciprocal(hrs[0:M, i:i + 1], hrs[0:M, i:i + 1]).then_inc(f_inv, 1)
                ve.wait_ge(f_inv, i + 1)
                if i >= 3:
                    ve.wait_ge(s_yo[i % 3], 16 * (i // 3))
                ve.scalar_tensor_tensor(out=yrow[i % 3][0:M, :], in0=fin[i % 3][0:M, 0:D], scalar=hrs[0:M, i:i + 1],
                                        in1=gfin[0:M, :], op0=ALU.mult, op1=ALU.mult).then_inc(f_dve_y, 1)

            summed(0)
            for i in range(NT):
                if i + 1 < NT:
                    summed(i + 1)
                final_norm(i)

        @block.gpsimd
        def _(po):
            for x in (m_xt, m_xte, m_gu, m_sil, m_hm, m_ht, m_hte, m_dn, m_dnA, m_dnD, m_free):
                for k in range(2):
                    po.sem_inc(x[k], 1)
            po.memset(xb[:, :, 0:CW - 1], 0.0).then_inc(zeroed, 1)
            po.memset(vb[:, :, 0:DW - 1], 0.0).then_inc(zeroed, 1)
            po.memset(dtr, 0.0).then_inc(zeroed, 1)
            po.wait_ge(ev, EV_AT[TILES.index(("xbc", 3))])
            po.wait_ge(s_hist, 48)
            po.tensor_copy(tail[:, :, 0, :], xb[:, :, TP:TP + CW - 1])
            po.tensor_copy(tail[:, :, 1, :], xb[:, :, XBW - (CW - 1):XBW]).then_inc(tailed, 1)
            po.wait_ge(s_params, 32)
            po.wait_ge(*dtp_act.at(0, "etot"))
            po.wait_ge(*dtp_dve.at(0, "a"))

            def gated_output(c):
                po.wait_ge(*ssd_dve.at(c, "yd"))
                for g in range(2):
                    last = po.tensor_tensor(xb[:, g, tok(c)], xb[:, g, tok(c)], mix[:, Z + g, tok(c)], ALU.mult)
                last.then_inc(ssd_gated, 1)

            for c in range(NT):
                L = NTOK[c]
                if c:
                    po.wait_ge(*ssd_pe.at(c - 1, "bc"))
                po.tensor_tensor(ua[0:L], bc(upper[0:L, :], 1, 4), bc(aa[0:L, c, :], 2, P), ALU.mult
                                 ).then_inc(*ssd_pool.of("ua"))
                po.wait_ge(*ssd_dve.at(c, "xdt"))
                if c:
                    po.wait_ge(*ssd_pe.at(c - 1, "st"))
                po.tensor_tensor(xdd[0:L].rearrange("p (h d) -> p h d", h=4),
                                 xdt[0:L].rearrange("p (h d) -> p h d", h=4), bc(dec[0:L, c, :], 2, 64), ALU.mult
                                 ).then_inc(*ssd_pool.of("xdd"))
                if c:
                    gated_output(c - 1)
            gated_output(NT - 1)
            po.wait_ge(p5_dve, P5["tables"])
            for c in range(NT):
                L = NTOK[c]
                po.wait_ge(*s5_dve.at(c, "half1"))
                po.tensor_tensor(s5t[0][:, :, 0:L], s5t[0][:, :, 0:L], s5t[1][:, :, 0:L], ALU.add
                                 ).then_inc(*s5_pool.of("u0"))
                po.wait_ge(*s5_dve.at(c, "scan"))
                if c:
                    po.wait_ge(s5_y, c)
                for x, (part, table) in enumerate(((0, cosT), (1, sinT), (0, sinT), (1, cosT))):
                    po.tensor_tensor(s5back[x][:, :, 0:L], s5g[part][:, :, 0:L], table[:, :, 0:L], ALU.mult
                                     ).then_inc(*s5_pool.of(f"m{x}"))
            po.wait_ge(*s5_pool.at(NT - 1, "m3"))
            po.wait_ge(*s5_dve.at(NT - 1, "end"))
            po.memset(lgt[:, NT - 1, :], 0.0).then_inc(zeroed, 1)
            po.wait_ge(slots_ready, 1)
            po.wait_ge(s_hst[0], 16 * 5)
            po.wait_ge(s_hst[1], 16 * 4)

            last_in, last_out = po.to_reg(T - 1), po.to_reg(2 * T - 1)

            def gather(b, n, blk):
                po.wait_ge(m_xt[b], n + 1)
                po.tensor_copy(curidx[b], slot_in[:, blk:blk + 1] if isinstance(blk, int) else slot_in[:, ds(blk, 1)]
                               ).then_inc(idxc, 1)
                po.wait_ge(idxc, blk + 1)
                po.sem_inc(indirect_go, 1)
                po.indirect_dma_start(xg[b], None, hn_dram, bass.IndirectOffsetOnAxis(ap=curidx[b], axis=0),
                                      bounds_check=last_in, oob_is_err=False).then_inc(s_xg[b], 16)

            def scatter(r, i, blk, freed=True):
                po.wait_ge(m_dnA[r], i + 2)
                po.wait_ge(m_dnD[r], i + 2)
                po.tensor_copy(curout[r], slot_out[:, ds(blk, 1)]).then_inc(outc, 1)
                po.wait_ge(outc, blk + 1)
                po.sem_inc(indirect_go, 1)
                po.indirect_dma_start(out_dram, bass.IndirectOffsetOnAxis(ap=curout[r], axis=0), orow[r], None,
                                      bounds_check=last_out, oob_is_err=False).then_inc(s_os[r], 16)
                if freed:
                    po.wait_ge(s_os[1 - r], 16 * (i + r))
                    po.sem_inc(m_free[1 - r], 1)

            gather(0, 0, 0)
            pairs = po.value_load(npairs[0:1, :], min_val=1, max_val=BLOCKS // 2)
            gather(1, 0, 1)
            gather(0, 1, 2)
            gather(1, 1, 3)
            gather(0, 2, 4)
            scatter(0, 0, 0, freed=False)
            with po.Fori(1, BLOCKS // 2) as i:
                with po.If(pairs > i):
                    gather(1, i + 1, 2 * i + 3)
                    scatter(1, i - 1, 2 * i - 1)
                    gather(0, i + 2, 2 * i + 4)
                    scatter(0, i, 2 * i)
            scatter(1, pairs - 1, 2 * pairs - 1, freed=False)


_OUTS = {"y_p": (TP, D), "y_s": (TS, D), "ssd_p": (P, P), "ssd_s": (P, P), "ssd_tail": (P, 24),
         "ccm_p": (P, 2, DW - 1), "ccm_s": (P, 2, DW - 1), "k_p": (P, 2, WIN), "k_s": (P, 2, TS),
         "v_p": (P, 4, 256), "v_s": (TS, 256), "s5_end": (P, 4 * ST)}


def _pack(x):
    import numpy as np

    x = {n: np.asarray(v) for n, v in x.items()}

    def chan(v, n):
        return np.moveaxis(v.reshape((n, P) + v.shape[1:]), 0, 1)

    def states(v):
        return np.moveaxis(v.reshape((ST, P) + v.shape[2:]), 0, 1)

    def every(v):
        return np.broadcast_to(v.reshape(1, -1), (P, v.size))
    w_in = x["w_in"][0]
    at = {"z": 0, "xbc": 256, "a": 772, "g": 1028, "q": 1284, "k": 1540, "ud": 2052}
    order = [("g", 0), ("g", 1), ("a", 0), ("a", 1)] + [("xbc", j) for j in range(4)] + \
            [(n, j) for n in ("k", "q", "z", "ud") for j in range(2)]
    f = np.float32
    parts = {
        "g_mix": chan(x["g_mix"][0], 8), "conv_w": chan(x["ssd_conv_w"][0].T, 4), "conv_b": chan(x["ssd_conv_b"][0], 4),
        "dw_w": chan(x["ccm_dw_w"][0].T, 2), "dw_b": chan(x["ccm_dw_b"][0], 2), "ln_g": chan(x["ccm_ln_g"][0], 2),
        "ln_b": chan(x["ccm_ln_b"][0], 2), "pw_b": chan(x["ccm_pw_b"][0], 2),
        "ssd_d": chan(np.repeat(x["ssd_d"][0], HD), 2), "norm_w": chan(x["ssd_norm_w"][0], 2),
        "glu_b": chan(x["s5_glu_b"][0], 4), "lam_re": states(x["s5_lam_re"][0]), "lam_im": states(x["s5_lam_im"][0]),
        "log_dt": states(np.repeat(x["s5_log_dt"][0][:, None], 64, 1)), "h0_re": states(x["state_s5_re"][0, 0]),
        "h0_im": states(x["state_s5_im"][0, 0]), "s5_d": chan(x["s5_d"][0].reshape(256), 2),
        "dt_bias": every(x["ssd_dt_bias"][0]), "a_log": every(x["ssd_a_log"][0]),
        "eps": np.full((P, 1), EPS, f), "one": np.ones((P, 1), f),
        "asg_row": (np.arange(2)[None, :, None] * T + np.arange(NT)[None, None, :] * P
                    + np.arange(P)[:, None, None] - 2 * T).astype(f),
        "thr": every(np.arange(THR, dtype=f) * P), "iota": every(np.arange(P, dtype=f)),
        "order4": every(np.arange(G, 0, -1).astype(f)), "order8": every(np.arange(EPG, 0, -1).astype(f)),
    }
    j, t = np.arange(P)[:, None], np.arange(P)[None, :]
    mats = np.concatenate([np.eye(P, dtype=f), np.ones((P, P), f), (j <= t).astype(f),
                           np.where(j > t, f(NEG), f(0))], axis=1)
    q, c = np.arange(P)[:, None], np.arange(BANDW)[None, :]
    seen = (c // 64 <= q // 64 + 8) & (c // 64 >= q // 64)
    idx = np.where(seen, np.clip(WIN + q - c, -128, 128) + 128, 257)
    table = np.concatenate([x["att_rel_bias"][0], np.full((HEADS, 1), NEG, f)], axis=1)
    s5w = [states(x[n][0]) for n in ("s5_b_re", "s5_b_im")] + \
          [states(np.moveaxis(x[n][0], 1, 2)) for n in ("s5_c_re", "s5_c_im")]
    rows = np.concatenate([x["x_prompt"][0], x["x_sample"][0]], axis=0)
    return {
        "params": np.concatenate([parts[n].reshape(P, w) for n, w in FIELDS], axis=1),
        "mats": mats, 
        "xT": rows.T, "x_rows": rows,
        "w_cm": np.stack([np.moveaxis(w_in[:, at[n] + i * P:at[n] + (i + 1) * P].reshape(KT, P, P), 0, 1).reshape(P, D)
                          for n, i in order]),
        "w_vd": chan(np.concatenate([w_in[:, 1796:2052], w_in[:, 768:772]], axis=1), KT),
        "ssd_hist": chan(x["state_ssd_conv"][0, 0].T, 4), "ccm_hist": chan(x["state_ccm_conv"][0, 0].T, 2),
        "ssd_h0": x["state_ssd"][0, 0].reshape(2, 2, HD, 64).transpose(0, 3, 1, 2).reshape(P, P),
        "k_cache": chan(x["cache_att_k"][0, 0].reshape(WIN, 256).T, 2),
        "v_cache": chan(x["cache_att_v"][0, 0].reshape(WIN, 256), 4),
        "bias": np.moveaxis(table[:, idx], 0, 1), "pw_w": chan(x["ccm_pw_w"][0], 2),
        "s5_w": np.stack(s5w, axis=1).reshape(P, -1), "glu_w": chan(x["s5_glu_w"][0], 2),
        "w_out": chan(x["w_out"][0], KT), "g_ffn": every(x["g_ffn"][0]), "g_final": every(x["g_final"]),
        "w_route": chan(np.concatenate([x["moe_w_group"][0], np.moveaxis(x["moe_w_expert"][0], 0, 1).reshape(D, E)],
                                       axis=1), KT),
        "w_gate": x["moe_w_gate"][0], "w_up": x["moe_w_up"][0], "w_down": x["moe_w_down"][0],
    }


def kernel(**inputs):
    import numpy as np
    import concourse.bacc as bacc
    from concourse.bass_utils import run_bass_kernel_spmd

    nc = bacc.Bacc("TRN2", target_bir_lowering=False, num_devices=1)
    arrays, a, o = {}, {}, {}
    for name, v in _pack(inputs).items():
        arrays["in_" + name] = v = np.ascontiguousarray(v)
        a[name] = nc.dram_tensor("in_" + name, v.shape, mybir.dt.from_np(v.dtype), kind="ExternalInput").ap()
    for name, shape in _OUTS.items():
        o[name] = nc.dram_tensor("out_" + name, shape, F32, kind="ExternalOutput").ap()
    encoder_step(nc, a, o)
    res = run_bass_kernel_spmd(nc, [arrays], core_ids=[0]).results[0]
    r = {name: np.asarray(res["out_" + name]).reshape(shape) for name, shape in _OUTS.items()}

    def state(v):
        return np.ascontiguousarray(v.reshape(2, 64, 2, HD).transpose(0, 2, 3, 1)).reshape(1, 1, 4, HD, 64)

    def rows(v, w):
        return np.ascontiguousarray(np.moveaxis(v, 0, 1).reshape(-1, w).T)
    tail = r["ssd_tail"].reshape(P, 4, 2, 3)
    end = r["s5_end"].reshape(P, 2, 2, ST)

    def s5(s, m):
        return np.ascontiguousarray(end[:, s, m, :].T).reshape(1, 1, 16, 64)
    return (r["y_p"].reshape(1, TP, D), r["y_s"].reshape(1, TS, D), state(r["ssd_p"]), state(r["ssd_s"]),
            rows(tail[:, :, 0], 3).reshape(1, 1, 3, 512), rows(tail[:, :, 1], 3).reshape(1, 1, 3, 512),
            rows(r["ccm_p"], DW - 1).reshape(1, 1, DW - 1, 256), rows(r["ccm_s"], DW - 1).reshape(1, 1, DW - 1, 256),
            rows(r["k_p"], WIN).reshape(1, 1, WIN, 4, HD), rows(r["k_s"], TS).reshape(1, 1, TS, 4, HD),
            np.ascontiguousarray(np.moveaxis(r["v_p"], 0, 1)).reshape(1, 1, WIN, 4, HD),
            r["v_s"].reshape(1, 1, TS, 4, HD), s5(0, 0), s5(1, 0), s5(0, 1), s5(1, 1))
```
